# Optimizing a Trainium2 kernel written in Bass

```python
import jax, jax.numpy as jnp
from jax import lax
import numpy as np

D_MODEL = 1024
BATCH = 1
SEQ = 1024
DEPTH = 1
DEC_BATCH = 1
DEC_SEQ = 32
PAST_LEN = 512

CHUNK = 64
N_META = 16
Q_BLOCK = 128
META_PAD = Q_BLOCK - N_META
RET_HEADS = 4
RET_QK_DIM = D_MODEL // 8
RET_V_DIM = D_MODEL // 4
RET_QK_W = RET_HEADS * RET_QK_DIM
RET_V_W = RET_HEADS * RET_V_DIM
FOX_HEADS = 8
FOX_DIM = D_MODEL // 8
FOX_W = FOX_HEADS * FOX_DIM
D_FF = 4 * D_MODEL
ROPE_BASE = 10000.0
EPS = 1e-6
NEG_INF = -1e30
IN_SIZES = (RET_QK_W, RET_QK_W, RET_V_W, RET_V_W, FOX_W, FOX_W, FOX_W, FOX_HEADS, D_MODEL, D_MODEL)
IN_W = 2 * RET_QK_W + 2 * RET_V_W + 3 * FOX_W + FOX_HEADS + 2 * D_MODEL

kernel_name = "hybrid_retention_fox_stream_step"

def rmsnorm(x, g):
    xf = x.astype(jnp.float32)
    y = xf * lax.rsqrt(jnp.mean(xf * xf, axis=-1, keepdims=True) + EPS)
    return (y * g.astype(jnp.float32)).astype(x.dtype)

def rotary(x, pos):
    half = x.shape[-1] // 2
    inv = ROPE_BASE ** (-jnp.arange(half, dtype=jnp.float32) / half)
    ang = pos.astype(jnp.float32)[:, None] * inv[None, :]
    cos = jnp.cos(ang)[:, None, :]
    sin = jnp.sin(ang)[:, None, :]
    xf = x.astype(jnp.float32)
    x1, x2 = xf[..., :half], xf[..., half:]
    return jnp.concatenate([x1 * cos - x2 * sin, x2 * cos + x1 * sin], axis=-1).astype(x.dtype)

def retention_log_decay():
    return jnp.log(1.0 - 2.0 ** (-5.0 - jnp.arange(RET_HEADS, dtype=jnp.float32)))

def retention_block(q, k, v, state, log_gamma):
    c_len = q.shape[2]
    n = jnp.arange(c_len, dtype=jnp.float32)
    lg = log_gamma[:, None]
    diff = n[:, None] - n[None, :]
    decay = jnp.where(diff >= 0, jnp.exp(lg[..., None] * jnp.maximum(diff, 0.0)), 0.0)
    qf, kf, vf = q.astype(jnp.float32), k.astype(jnp.float32), v.astype(jnp.float32)
    scores = jnp.einsum('bhnd,bhmd->bhnm', qf, kf) * decay
    inner = jnp.einsum('bhnm,bhmv->bhnv', scores, vf)
    cross = jnp.einsum('bhnd,bhdv->bhnv', qf * jnp.exp(lg * (n + 1.0))[..., None], state)
    new_state = jnp.exp(lg * c_len)[..., None] * state + jnp.einsum(
        'bhmd,bhmv->bhdv', kf * jnp.exp(lg * (c_len - 1.0 - n))[..., None], vf)
    return inner + cross, new_state

def retention_out(y, rg, gn_g):
    y = jnp.swapaxes(y, 1, 2)
    b, t = y.shape[0], y.shape[1]
    yc = y - jnp.mean(y, axis=-1, keepdims=True)
    yn = yc * lax.rsqrt(jnp.mean(yc * yc, axis=-1, keepdims=True) + EPS)
    yn = yn.reshape(b, t, RET_V_W) * gn_g.astype(jnp.float32)
    return (jax.nn.silu(rg.astype(jnp.float32)) * yn).astype(rg.dtype)

def fox_attend(q, k, v, cq, ck, allowed):
    s = jnp.einsum('bhqd,bhkd->bhqk', q.astype(jnp.float32), k.astype(jnp.float32)) * (FOX_DIM ** -0.5)
    s = s + cq[..., :, None] - ck[..., None, :]
    s = jnp.where(allowed, s, NEG_INF)
    p = jax.nn.softmax(s, axis=-1)
    return jnp.einsum('bhqk,bhkd->bhqd', p, v.astype(jnp.float32))

def project_in(h, pos, norm1_g, w_in, b_forget, q_norm_g, k_norm_g):
    b, t, _ = h.shape
    xn = rmsnorm(h, norm1_g)
    z = jnp.einsum('btd,de->bte', xn, w_in)
    cuts = [int(c) for c in np.cumsum(IN_SIZES)[:-1]]
    rq, rk, rv, rg, fq, fk, fv, ff, ga, gb = jnp.split(z, cuts, axis=-1)
    rq = rotary(rq.reshape(b, t, RET_HEADS, RET_QK_DIM), pos)
    rk = rotary(rk.reshape(b, t, RET_HEADS, RET_QK_DIM), pos) * (RET_QK_DIM ** -0.5)
    rv = rv.reshape(b, t, RET_HEADS, RET_V_DIM)
    fq = rmsnorm(fq.reshape(b, t, FOX_HEADS, FOX_DIM), q_norm_g)
    fk = rmsnorm(fk.reshape(b, t, FOX_HEADS, FOX_DIM), k_norm_g)
    fv = fv.reshape(b, t, FOX_HEADS, FOX_DIM)
    logf = jax.nn.log_sigmoid(ff.astype(jnp.float32) + b_forget.astype(jnp.float32))
    return rq, rk, rv, rg, fq, fk, fv, logf, ga, gb

def merge_and_mlp(h, ret_o, fox_o, ga, gb, w_ret_out, w_fox_out, w_o, norm2_g, w_ff1, w_ff2):
    m = jax.nn.sigmoid(ga) * (ret_o @ w_ret_out) + jax.nn.sigmoid(gb) * (fox_o @ w_fox_out)
    h = h + m @ w_o
    u = jax.nn.relu(rmsnorm(h, norm2_g) @ w_ff1)
    return h + (u * u) @ w_ff2

def prompt_layer(h, pos, valid, lw):
    (norm1_g, w_in, b_forget, q_norm_g, k_norm_g, ret_gn_g,
     w_ret_out, w_fox_out, w_o, norm2_g, w_ff1, w_ff2) = lw
    b, l_len, _ = h.shape
    rq, rk, rv, rg, fq, fk, fv, logf, ga, gb = project_in(h, pos, norm1_g, w_in, b_forget, q_norm_g, k_norm_g)
    rk = rk * valid[None, :, None, None].astype(rk.dtype)
    n_chunks = l_len // CHUNK
    log_gamma = retention_log_decay()

    def to_chunks(a):
        return a.reshape(b, n_chunks, CHUNK, a.shape[2], a.shape[3]).transpose(1, 0, 3, 2, 4)

    def step(state, qkv):
        q_c, k_c, v_c = qkv
        o_c, state = retention_block(q_c, k_c, v_c, state, log_gamma)
        return state, o_c

    s0 = jnp.zeros((b, RET_HEADS, RET_QK_DIM, RET_V_DIM), jnp.float32)
    s_fin, o = lax.scan(step, s0, (to_chunks(rq), to_chunks(rk), to_chunks(rv)))
    o = o.transpose(1, 2, 0, 3, 4).reshape(b, RET_HEADS, l_len, RET_V_DIM)
    ret_o = retention_out(o, rg, ret_gn_g)
    logf = jnp.where(valid[None, :, None], logf, 0.0)
    c = jnp.cumsum(logf, axis=1).transpose(0, 2, 1)
    qh, kh, vh = fq.transpose(0, 2, 1, 3), fk.transpose(0, 2, 1, 3), fv.transpose(0, 2, 1, 3)
    n_blocks = l_len // Q_BLOCK
    qb = qh.reshape(b, FOX_HEADS, n_blocks, Q_BLOCK, FOX_DIM).transpose(2, 0, 1, 3, 4)
    cb = c.reshape(b, FOX_HEADS, n_blocks, Q_BLOCK).transpose(2, 0, 1, 3)
    kpos = jnp.arange(l_len)

    def attend_block(args):
        q_i, c_i, blk = args
        qpos = blk * Q_BLOCK + jnp.arange(Q_BLOCK)
        allowed = (kpos[None, :] <= qpos[:, None]) & valid[None, :]
        return fox_attend(q_i, kh, vh, c_i, c, allowed)

    ob = lax.map(attend_block, (qb, cb, jnp.arange(n_blocks)))
    fox_o = ob.transpose(1, 0, 3, 2, 4).reshape(b, l_len, FOX_W).astype(h.dtype)
    h = merge_and_mlp(h, ret_o, fox_o, ga, gb, w_ret_out, w_fox_out, w_o, norm2_g, w_ff1, w_ff2)
    return h, s_fin, fk[:, META_PAD:], fv[:, META_PAD:], logf[:, META_PAD:]

def sample_layer(h, state, cache_k, cache_v, cache_logf, lw):
    (norm1_g, w_in, b_forget, q_norm_g, k_norm_g, ret_gn_g,
     w_ret_out, w_fox_out, w_o, norm2_g, w_ff1, w_ff2) = lw
    b, t, _ = h.shape
    past = cache_k.shape[1]
    pos = past + jnp.arange(t)
    rq, rk, rv, rg, fq, fk, fv, logf, ga, gb = project_in(h, pos, norm1_g, w_in, b_forget, q_norm_g, k_norm_g)
    o, s_new = retention_block(rq.transpose(0, 2, 1, 3), rk.transpose(0, 2, 1, 3), rv.transpose(0, 2, 1, 3),
                               state.astype(jnp.float32), retention_log_decay())
    ret_o = retention_out(o, rg, ret_gn_g)
    k_all = jnp.concatenate([cache_k.astype(fk.dtype), fk], axis=1).transpose(0, 2, 1, 3)
    v_all = jnp.concatenate([cache_v.astype(fv.dtype), fv], axis=1).transpose(0, 2, 1, 3)
    c = jnp.cumsum(jnp.concatenate([cache_logf.astype(jnp.float32), logf], axis=1), axis=1).transpose(0, 2, 1)
    allowed = jnp.arange(past + t)[None, :] <= (past + jnp.arange(t))[:, None]
    fo = fox_attend(fq.transpose(0, 2, 1, 3), k_all, v_all, c[..., past:], c, allowed)
    fox_o = fo.transpose(0, 2, 1, 3).reshape(b, t, FOX_W).astype(h.dtype)
    h = merge_and_mlp(h, ret_o, fox_o, ga, gb, w_ret_out, w_fox_out, w_o, norm2_g, w_ff1, w_ff2)
    return h, s_new.astype(state.dtype), fk, fv, logf

def setup_inputs(seed: int = 0) -> dict:
    key = jax.random.key(seed)
    ks = jax.random.split(key, 20)
    nrm = jax.random.normal
    x_prompt = nrm(ks[0], (BATCH, SEQ, D_MODEL), jnp.float32)
    x_sample = nrm(ks[1], (DEC_BATCH, DEC_SEQ, D_MODEL), jnp.float32)
    state_ret = 0.3 * nrm(ks[2], (DEPTH, DEC_BATCH, RET_HEADS, RET_QK_DIM, RET_V_DIM), jnp.float32)
    cache_fox_k = nrm(ks[3], (DEPTH, DEC_BATCH, PAST_LEN, FOX_HEADS, FOX_DIM), jnp.float32)
    cache_fox_v = nrm(ks[4], (DEPTH, DEC_BATCH, PAST_LEN, FOX_HEADS, FOX_DIM), jnp.float32)
    b_forget = jnp.linspace(1.0, 5.0, FOX_HEADS, dtype=jnp.float32)[None, :] + 0.1 * nrm(ks[5], (DEPTH, FOX_HEADS), jnp.float32)
    cache_fox_logf = jax.nn.log_sigmoid(
        b_forget[:, None, None, :] + 0.5 * nrm(ks[6], (DEPTH, DEC_BATCH, PAST_LEN, FOX_HEADS), jnp.float32))
    meta_tokens = nrm(ks[7], (N_META, D_MODEL), jnp.float32)
    norm1_g = 1.0 + 0.02 * nrm(ks[8], (DEPTH, D_MODEL), jnp.float32)
    w_in = nrm(ks[9], (DEPTH, D_MODEL, IN_W), jnp.float32) * D_MODEL ** -0.5
    q_norm_g = 1.0 + 0.02 * nrm(ks[10], (DEPTH, FOX_DIM), jnp.float32)
    k_norm_g = 1.0 + 0.02 * nrm(ks[11], (DEPTH, FOX_DIM), jnp.float32)
    ret_gn_g = 1.0 + 0.02 * nrm(ks[12], (DEPTH, RET_V_W), jnp.float32)
    w_ret_out = nrm(ks[13], (DEPTH, RET_V_W, D_MODEL), jnp.float32) * RET_V_W ** -0.5
    w_fox_out = nrm(ks[14], (DEPTH, FOX_W, D_MODEL), jnp.float32) * FOX_W ** -0.5
    w_o = nrm(ks[15], (DEPTH, D_MODEL, D_MODEL), jnp.float32) * D_MODEL ** -0.5
    norm2_g = 1.0 + 0.02 * nrm(ks[16], (DEPTH, D_MODEL), jnp.float32)
    w_ff1 = nrm(ks[17], (DEPTH, D_MODEL, D_FF), jnp.float32) * D_MODEL ** -0.5
    w_ff2 = nrm(ks[18], (DEPTH, D_FF, D_MODEL), jnp.float32) * D_FF ** -0.5
    return {"x_prompt": x_prompt, "x_sample": x_sample, "state_ret": state_ret,
            "cache_fox_k": cache_fox_k, "cache_fox_v": cache_fox_v, "cache_fox_logf": cache_fox_logf,
            "meta_tokens": meta_tokens, "norm1_g": norm1_g, "w_in": w_in, "b_forget": b_forget,
            "q_norm_g": q_norm_g, "k_norm_g": k_norm_g, "ret_gn_g": ret_gn_g,
            "w_ret_out": w_ret_out, "w_fox_out": w_fox_out, "w_o": w_o, "norm2_g": norm2_g,
            "w_ff1": w_ff1, "w_ff2": w_ff2}

def reference(x_prompt, x_sample, state_ret, cache_fox_k, cache_fox_v, cache_fox_logf,
              meta_tokens, norm1_g, w_in, b_forget, q_norm_g, k_norm_g, ret_gn_g,
              w_ret_out, w_fox_out, w_o, norm2_g, w_ff1, w_ff2):
    bp = x_prompt.shape[0]
    dt = x_prompt.dtype
    hp = jnp.concatenate([jnp.zeros((bp, META_PAD, D_MODEL), dt),
                          jnp.broadcast_to(meta_tokens.astype(dt)[None], (bp, N_META, D_MODEL)),
                          x_prompt], axis=1)
    pos_p = jnp.arange(hp.shape[1]) - (META_PAD + N_META)
    valid_p = pos_p >= -N_META
    hs = x_sample
    p_st, p_k, p_v, p_lf, s_st, s_k, s_v, s_lf = [], [], [], [], [], [], [], []
    for l in range(DEPTH):
        lw = (norm1_g[l], w_in[l], b_forget[l], q_norm_g[l], k_norm_g[l], ret_gn_g[l],
              w_ret_out[l], w_fox_out[l], w_o[l], norm2_g[l], w_ff1[l], w_ff2[l])
        hp, st, kr, vr, lf = prompt_layer(hp, pos_p, valid_p, lw)
        p_st.append(st)
        p_k.append(kr)
        p_v.append(vr)
        p_lf.append(lf)
        hs, st, kr, vr, lf = sample_layer(hs, state_ret[l], cache_fox_k[l], cache_fox_v[l], cache_fox_logf[l], lw)
        s_st.append(st)
        s_k.append(kr)
        s_v.append(vr)
        s_lf.append(lf)
    y_prompt = hp[:, META_PAD + N_META:]
    return (y_prompt, hs, jnp.stack(p_st), jnp.stack(p_k), jnp.stack(p_v), jnp.stack(p_lf),
            jnp.stack(s_st), jnp.stack(s_k), jnp.stack(s_v), jnp.stack(s_lf))


_drawn_inputs = setup_inputs


def setup_inputs(seed=0):
    import zlib

    import numpy as np

    out = dict(_drawn_inputs(seed))
    spreads = {}
    factors = {'q_norm_g': 186.898, 'ret_gn_g': 22.17, 'norm2_g': 9.279}
    for name, (base, spread) in spreads.items():
        noise = np.random.default_rng([zlib.crc32(name.encode()), seed]).standard_normal(out[name].shape)
        drawn = base * np.exp(spread * noise) if base else spread * noise
        out[name] = __import__('jax').numpy.asarray(drawn.astype(out[name].dtype))
    for name, factor in factors.items():
        out[name] = (out[name] * factor).astype(out[name].dtype)
    return out
```

```python
from contextlib import ExitStack

import concourse.bass as bass
from concourse import mybir

F32 = mybir.dt.float32
F32R = mybir.dt.float32r
ALU = mybir.AluOpType
ACT = mybir.ActivationFunctionType
AX = mybir.AxisListType

P = 128
D = 1024
KC = D // P
SEQ = 1024
NT = SEQ // P
NS = 32
NM = 16
NPAST = 512
NC = NPAST // P
TOUT = SEQ + NS
TALL = TOUT + NM
TPAD = (NT + 1) * P
NQ = NT + 1
FH = 8
RH = 4
RV = 256
EPS = 1e-6
SCALE = float(P) ** -0.5
NEG = -1e30
W_RQ, W_RV, W_RG, W_FQ, W_FK, W_FV, W_FF, W_GA, W_GB = 0, 1024, 2048, 3072, 4096, 5120, 6144, 6152, 7176
UNIT = 1024
NB = 2


def hybrid_step(nc, x_prompt, x_sample, state_ret, cache_k, cache_v, cache_logf, meta, norm1_g, w_in,
                b_forget, q_norm_g, k_norm_g, ret_gn_g, w_ret_out, w_fox_out, w_o, norm2_g, w_ff1, w_ff2,
                c_ident, c_mask, c_cos, c_sin, c_decay,
                y_prompt, y_sample, p_state, p_k, p_v, p_logf, s_state, s_k, s_v, s_logf):
    ctx = ExitStack()

    def sb(name, shape, dt=F32, stack=ctx):
        return stack.enter_context(nc.sbuf_tensor(name, shape, dt))

    def sem(name):
        return ctx.enter_context(nc.semaphore(name))

    def wait(eng, s, value):
        if not isinstance(value, int) or value > 0:
            eng.wait_ge(s, value)

    xp = x_prompt.rearrange("a t d -> (a t) d")
    xs = x_sample.rearrange("a t d -> (a t) d")
    st_in = state_ret.rearrange("l b h d v -> (l b h) d v")
    ck = cache_k.rearrange("l b t h d -> (l b t) (h d)")
    cv = cache_v.rearrange("l b t h d -> (l b t) (h d)")
    clf = cache_logf.rearrange("l b t h -> (l b t) h")
    win = w_in.rearrange("l (k p) n -> p (l k) n", p=P)
    wro = w_ret_out.rearrange("l (k p) n -> p (l k) n", p=P)
    wfo = w_fox_out.rearrange("l (k p) n -> p (l k) n", p=P)
    wout = w_o.rearrange("l (k p) n -> p (l k) n", p=P)
    wf1 = w_ff1.rearrange("l (k p) n -> p (l k) n", p=P)
    wf2 = w_ff2.rearrange("l (k p) n -> p (l k) n", p=P)
    yp = y_prompt.rearrange("a t d -> (a t) d")
    ys = y_sample.rearrange("a t d -> (a t) d")
    pst = p_state.rearrange("l b h d v -> (l b h) d v")
    sst = s_state.rearrange("l b h d v -> (l b h) d v")
    pk = p_k.rearrange("l b t h d -> (l b t) (h d)")
    pv = p_v.rearrange("l b t h d -> (l b t) (h d)")
    plf = p_logf.rearrange("l b t h -> (l b t) h")
    sk = s_k.rearrange("l b t h d -> (l b t) (h d)")
    sv = s_v.rearrange("l b t h d -> (l b t) (h d)")
    slf = s_logf.rearrange("l b t h -> (l b t) h")

    def dram(name, shape, dt=F32):
        return nc.dram_tensor(name, shape, dt, kind="Internal").ap()

    pq = dram("q_rows", (NM + SEQ, D))
    sq = dram("q_rows_sample", (NS, D))
    prv = dram("rv_rows", (NM + SEQ, D))
    srv = dram("rv_rows_sample", (NS, D))
    rot = dram("rotated", (8, P, TALL))
    gates = dram("gates", (24, P, TOUT))
    negc = dram("neg_cumsum", (2, FH, SEQ + NM + NPAST + NS), F32R)
    foxT = dram("fox_out_T", (KC, P, TOUT))
    retT = dram("ret_out_T", (KC, P, TOUT))
    hrow = dram("h_rows", (TOUT, D))

    xh = sb("act_hi", [P, KC, TPAD], F32R)
    xl = sb("act_lo", [P, KC, TPAD], F32R)
    raw = sb("w_raw", [P, 4, UNIT])
    wh = sb("w_hi", [P, 4, UNIT], F32R)
    wl = sb("w_lo", [P, 4, UNIT], F32R)
    ident = sb("ident", [P, P])
    identr = sb("ident_r", [P, P], F32R)
    maskf = sb("mask", [P, P])
    maskr = sb("mask_r", [P, P], F32R)
    onesr = sb("ones_r", [P, P], F32R)
    stat = sb("stat", [P, 8, 18])
    gnT = sb("gn_gain", [P, KC])
    mx = sb("neg_max", [P, 2])
    lsum = sb("row_sum", [P, 2])
    linv = sb("row_sum_inv", [P, 2])
    bfT = sb("b_forget_col", [FH, 1])

    def arena(sizes):
        with ExitStack() as s:
            return [sb(n, shape, dt, s) for n, shape, dt in sizes]

    xt, xn, g1, xsq = arena([("x_rows", [P, NQ, D], F32), ("xn_rows", [P, 2, D], F32), ("norm1_bc", [P, D], F32), ("x_squares", [P, 2, D], F32)])
    rows, cosT, sinT, gq, gk, stage, rtmp, lf, lfc, cst, crow, lfr, nchl, junk = arena([
        ("strip_rows", [P, 2, NQ, 256], F32), ("cos", [P, TALL], F32), ("sin", [P, TALL], F32),
        ("gq_bc", [P, P], F32), ("gk_bc", [P, P], F32), ("stage", [P, 2, TALL], F32),
        ("rot_tmp", [P, 2, 2, 360], F32), ("logf_T", [FH, TALL], F32), ("lf_tmp", [FH, 2, TALL], F32),
        ("cumsum", [FH, TALL + NPAST], F32), ("cache_lf_rows", [P, NC, FH], F32),
        ("logf_rows", [P, NQ, FH], F32), ("negc_hl", [FH, 2, SEQ + NM + NPAST + NS], F32R), ("row_squares", [P, 18, P], F32)])
    (qrow, qsrow, krow, kmrow, ksrow, kcrow, vrow, vmrow, vsrow, vcrow, qT, kT, kcT, prob, pT, ncr, fst) = arena([
        ("fq_rows", [P, NT, P], F32), ("fq_rows_s", [NS, P], F32), ("fk_rows", [P, NT, P], F32),
        ("fk_rows_m", [NM, P], F32), ("fk_rows_s", [NS, P], F32), ("fk_rows_c", [P, NC, P], F32),
        ("fv_rows", [P, NT, P], F32), ("fv_rows_m", [NM, P], F32), ("fv_rows_s", [NS, P], F32),
        ("fv_rows_c", [P, NC, P], F32),
        ("fqT", [P, TOUT], F32), ("fkT", [P, SEQ + NM + NS], F32), ("fkcT", [P, NPAST], F32),
        ("probs", [P, 2, SEQ + NM], F32), ("probsT", [P, NT + 1, P], F32),
        ("negc_rows", [P, SEQ + NM + NPAST + NS], F32R), ("fox_stage", [P, TOUT], F32)])
    (rqT, rkT, rvrow, rvm, rvs, dec, rgT, rst, sTd, kd, qg, yraw, state, bns, s0s) = arena([
        ("rqT", [P, TALL], F32), ("rkT", [P, TALL], F32), ("rv_rows_sb", [P, NT, RV], F32),
        ("rv_rows_m", [NM, RV], F32), ("rv_rows_s", [NS, RV], F32), ("decay", [P, 264], F32),
        ("rgT", [P, 2, TOUT], F32), ("ret_stage", [P, 2, TOUT], F32), ("scores_T", [P, 2, P], F32),
        ("k_decayed", [P, 2, P], F32), ("q_decayed", [P, 2, P], F32), ("y_raw", [P, NQ, RV], F32),
        ("ret_state", [P, RV], F32), ("bn_stats", [P, NQ, 8], F32),
        ("sample_state", [P, RV], F32)])
    araw, mT, gate, mtmp = arena([("act_raw", [P, 3, TOUT], F32), ("merged_T", [P, KC, TOUT], F32),
                                  ("gate_T", [P, 2, TOUT], F32), ("gated", [P, 2, 352], F32)])
    hsb, xrow, hn, g2, hsq = arena([("h_sb", [P, NQ, D], F32), ("x_again", [P, 2, NQ, 256], F32),
                               ("hn_rows", [P, 2, D], F32), ("norm2_bc", [P, D], F32), ("h_squares", [P, 2, D], F32)])
    yT, uh, ul, relu, usq = arena([("y_T", [P, KC, TOUT], F32), ("u_hi", [P, 4, TOUT], F32R), ("u_lo", [P, 4, TOUT], F32R),
                                   ("relu", [P, 2, 352], F32), ("u", [P, 2, 352], F32)])
    _, hback, yout = arena([("y_T_kept", [P, KC, TOUT], F32), ("h_back", [P, 2, D], F32), ("y_rows", [P, 2, D], F32)])

    pd = ctx.enter_context(nc.psum_tensor("ps_dense", [P, NB, 512], F32))
    pt = ctx.enter_context(nc.psum_tensor("ps_turn", [P, 2, 512], F32))
    ps = ctx.enter_context(nc.psum_tensor("ps_scores", [P, 3 * 512], F32))
    po = ctx.enter_context(nc.psum_tensor("ps_out", [P, 512], F32))

    w_in_s = [sem(f"w_landed{i}") for i in range(4)]
    w_hi_s = sem("w_hi_ready")
    w_lo_s = sem("w_lo_ready")
    mm_done = sem("dense_done")
    bank_free = sem("dense_read")
    const_in = sem("const_landed")
    const_ok = sem("const_ready")
    pad_ok = sem("pad_zeroed")
    x_in = [sem(f"x_landed{i}") for i in range(NQ)]
    dch = sem("dve_chain")
    a_ssq = sem("ssq_ready")
    a_root = sem("root_ready")
    v_norm = sem("rows_normed")
    t_done = [sem("turned0"), sem("turned1")]
    t_read = [sem("turn_read0"), sem("turn_read1")]
    a_hi = sem("act_hi_ready")
    a_lo = sem("act_lo_ready")

    T3 = [(0, 358), (358, 358), (716, 356)]
    O3 = [(0, 352), (352, 352), (704, 352)]

    class At:

        def __init__(self, first, step=0, i=None):
            self.first, self.step, self.i = first, step, i

        def __add__(self, k):
            return At(self.first + k, self.step, self.i)

        def __sub__(self, k):
            return self + (-k)

        def mod(self, m):
            assert self.i is None or self.step % m == 0
            return self.first % m

        def times(self, m, plus=0):
            return At(self.first * m + plus, self.step * m, self.i).v

        def over(self, m):
            assert self.i is None or self.step % m == 0
            return At(self.first // m, self.step // m, self.i)

        @property
        def v(self):
            return self.first if self.i is None else self.i * self.step + self.first

    STRIPS = 16
    U_STRIP, N_STRIP = 1, 3
    U_TURN, N_TURN = U_STRIP + 2 * STRIPS, N_STRIP + NQ * STRIPS
    U_FOX, N_FOX = U_TURN + 32, N_TURN + 96
    U_RET, N_RET = U_FOX + 8, N_FOX + 24
    U_WO, N_WO = U_RET + 8, N_RET + 24
    U_MLP, N_MLP = U_WO + 8, N_WO + 4 * NQ
    G_N = 36
    U_END = U_MLP + 64
    A_NORM1 = 2 * NQ
    A_FOX, A_RET, A_M, A_NORM2 = A_NORM1 + 8, A_NORM1 + 16, A_NORM1 + 24, A_NORM1 + 24 + 2 * NQ
    ST_STRIP = 48
    ST_TURN = ST_STRIP * STRIPS
    ST_ATT = ST_TURN + 16 * 32
    ST_RET = ST_ATT + 16 * FH

    def load_unit(sp, u, src):
        wait(sp, w_lo_s, (u - 3).v)
        k = src.shape[1]
        sp.dma_start(raw[:, u.mod(4), :].rearrange("p (k m) -> p k m", k=k), src).then_inc(w_in_s[u.mod(4)], 16)

    def split_hi(act, u, n):
        act.wait_ge(w_in_s[u.mod(4)], At(u.first // 4, u.step // 4, u.i).times(16, 16))
        wait(act, mm_done, n.v)
        nc.scalar.copy(wh[:, u.mod(4), :], raw[:, u.mod(4), :]).then_inc(w_hi_s, 1)

    def split_lo(dve, u):
        dve.wait_ge(w_hi_s, (u + 1).v)
        nc.vector.tensor_tensor(wl[:, u.mod(4), :], raw[:, u.mod(4), :], wh[:, u.mod(4), :],
                                ALU.subtract).then_inc(w_lo_s, 1)

    def turned_step(pe, n, us, c, w, hi=xh, lo=xl, kc=KC, m0=0):
        wait(pe, bank_free, (n - 1).v)
        width = UNIT // kc
        a, b = (x[:, us, :].rearrange("p (k m) -> p k m", m=width) for x in (wh, wl))
        for k in range(kc):
            for q, (lhs, rhs) in enumerate(((b, hi), (a, lo), (a, hi))):
                mm = nc.tensor.matmul(pd[:, n.mod(NB), 0:w], lhs[:, k, m0:m0 + P], rhs[:, k, c:c + w],
                                      start=(k == 0 and q == 0), stop=(k == kc - 1 and q == 2))
        mm.then_inc(mm_done, 1)

    def strip_step(pe, n, u, i):
        wait(pe, bank_free, (n - 1).v)
        for k in range(KC):
            us = (u + k // 4).mod(4)
            a, b = (x[:, us, 256 * (k % 4):256 * (k % 4) + 256] for x in (wh, wl))
            t = slice(i * P, i * P + P)
            for q, (lhs, rhs) in enumerate(((xh, b), (xl, a), (xh, a))):
                mm = nc.tensor.matmul(pd[:, n.mod(NB), 0:256], lhs[:, k, t], rhs,
                                      start=(k == 0 and q == 0), stop=(k == KC - 1 and q == 2))
        mm.then_inc(mm_done, 1)

    def strip_src(w, c):
        return [w[:, 4 * j:4 * j + 4, c] for j in range(2)]

    def link(dve, ins, chain):
        ins.then_inc(dch, 1)
        chain[0] = chain[0] + 1
        dve.wait_ge(dch, chain[0].v)

    def root_start(dve, src, w, inv, chain):
        link(dve, nc.vector.tensor_scalar(stat[:, 1, 0:w], src, inv, EPS, ALU.mult, ALU.add), chain)

    def root_end(dve, w, scale, chain):
        v, r, rr, e, t, o = stat[:, 1, 0:w], stat[:, 2, 0:w], stat[:, 3, 0:w], stat[:, 4, 0:w], stat[:, 6, 0:w], stat[:, 5, 0:w]
        link(dve, nc.vector.reciprocal(rr, r), chain)
        link(dve, nc.vector.tensor_tensor(e, rr, rr, ALU.mult), chain)
        link(dve, nc.vector.tensor_tensor(t, e, v, ALU.mult), chain)
        link(dve, nc.vector.tensor_scalar(e, t, -0.5, 1.5, ALU.mult, ALU.add), chain)
        link(dve, nc.vector.scalar_tensor_tensor(o, rr, scale, e, ALU.mult, ALU.mult), chain)

    def turn_rows_pe(pe, rows_ap, i, a_base, norm_base):
        pe.wait_ge(v_norm, norm_base + i + 1)
        for g in range(2):
            wait(pe, a_lo, a_base + max(2 * i + g - 1, 0))
            for c in range(4):
                mm = nc.tensor.transpose(pt[:, g, c * P:c * P + P],
                                         rows_ap[:, i % 2, (4 * g + c) * P:(4 * g + c + 1) * P], ident[:])
            mm.then_inc(t_done[g], 1)

    def act_cols(x, i, g):
        return x[:, 4 * g:4 * g + 4, i * P:i * P + P]

    def turn_rows_act(act, i, t_base):
        for g in range(2):
            act.wait_ge(t_done[g], t_base[g] + i + 1)
            nc.scalar.copy(act_cols(xh, i, g), pt[:, g, :].rearrange("p (c t) -> p c t", c=4)).then_inc(a_hi, 1)

    def turn_rows_dve(dve, i, h_base, l_base=None):
        for g in range(2):
            dve.wait_ge(a_hi, h_base + 2 * i + g + 1)
            nc.vector.tensor_tensor(act_cols(xl, i, g), pt[:, g, :].rearrange("p (c t) -> p c t", c=4),
                                    act_cols(xh, i, g), ALU.subtract).then_inc(a_lo, 1)

    def att_groups():
        out = []
        for q in range(6):
            out.append((-1, q, len(out) % 2))
        for j in range(NT):
            blocks = list(range(j + 1)) + [NT]
            for b in range(0, len(blocks), 4):
                out.append((j, blocks[b:b + 4], len(out) % 2))
        out.append((NT, list(range(NC + 1)), len(out) % 2))
        return out

    GROUPS = att_groups()
    PER_BANK = [sum(g[2] == b for g in GROUPS) for b in range(2)]
    T_ATT = [NQ + 1, NQ + 1]
    T_NORM2 = [T_ATT[b] + FH * PER_BANK[b] for b in range(2)]
    T_FIN = [T_NORM2[b] + NQ for b in range(2)]

    def nth(g):
        return sum(x[2] == GROUPS[g][2] for x in GROUPS[:g])

    def step_groups(j):
        return [g for g in range(len(GROUPS)) if GROUPS[g][0] == j]

    NKEY = SEQ + NM

    def turn_prologue(q):
        if q < 2:
            return [(qrow[:, 4 * q + x, :], x * P, P) for x in range(4)], [(qT[:, 512 * q:512 * q + 512], 0, 512)]
        if q < 4:
            z = q - 2
            return ([(krow[:, 4 * z + x, :], x * P, P) for x in range(4)],
                    [(kT[:, NM + 512 * z:NM + 512 * z + 512], 0, 512)])
        if q == 4:
            return ([(kcrow[:, 0, :], 0, P), (qsrow[:], P, NS), (kmrow[:], P + 32, NM), (ksrow[:], P + 64, NS)],
                    [(kcT[:, 0:P], 0, P), (qT[:, SEQ:TOUT], P, NS), (kT[:, 0:NM], P + 32, NM),
                     (kT[:, NKEY:NKEY + NS], P + 64, NS)])
        return [(kcrow[:, x + 1, :], x * P, P) for x in range(3)], [(kcT[:, P:], 0, 3 * P)]

    def prob_block(j, b):
        if j == NT:
            return b * P, (P if b < NC else NS)
        return (0, NM) if b == NT else (NM + b * P, P)

    def read_group(eng_copy, g):
        j, blocks, bank = GROUPS[g]
        if j < 0:
            for dst, c, w in turn_prologue(blocks)[1]:
                last = eng_copy(dst, pt[:, bank, c:c + w])
            return last
        if j == NT:
            eng_copy(pT[:, 0, 0:NS], pt[:, bank, 0:NS])
            eng_copy(pT[:, 1:NC, 0:NS], pt[:, bank, P:P + 3 * NS].rearrange("p (b w) -> p b w", b=3))
            return eng_copy(pT[0:NS, NC, 0:NS], pt[0:NS, bank, P + 3 * NS:P + 4 * NS])
        width = P
        full = [b for b in blocks if prob_block(j, b)[1] == P]
        if full:
            n = len(full)
            last = eng_copy(pT[:, full[0]:full[0] + n, 0:width],
                            pt[:, bank, 0:n * width].rearrange("p (b w) -> p b w", b=n))
        for x, b in enumerate(blocks):
            k = prob_block(j, b)[1]
            if k != P:
                last = eng_copy(pT[0:k, b, 0:width], pt[0:k, bank, x * width:x * width + width])
        return last

    ATT = FH * 9
    E0, O0 = 1, 1

    CH = [(TOUT, NM)] + [(i * P, P) for i in range(NT)] + [(SEQ, NS)]
    NCH = len(CH)
    D_GQ, D_COL = P, 2 * P
    C_KP, C_KM, C_KS, C_GP, C_GS = range(5)

    RT_GROUPS = [(e, [(e, 4 * z + x, P) for x in range(4)]) for e in range(2) for z in range(2)]
    RT_GROUPS.append((None, [(0, NT, P), (1, NT, P)]))
    CH_ROOT1 = 2

    small_in = sem("small_landed"); ssq_v = sem("strip_mean_square"); ncr_zero = sem("negc_rows_zero")
    yz_ok = sem("ret_pad_set"); hz_ok = sem("h_pad_zero"); ld_g = sem("gain_landed"); y_rd = sem("y_turn_read")
    strip_ok = sem("strip_ready")
    ssq2 = sem("strip_ssq")
    unit_v = sem("rotated_ready")
    unit_c = sem("gate_raw")
    unit_a = sem("gate_ready")
    stored = sem("stored")
    lf_raw = sem("logf_raw"); lf_e = sem("logf_exp"); lf_ok = sem("logf_ready"); lf_c = sem("cache_logf_landed")
    lf_T = sem("logf_turned"); lf_r = sem("logf_rows_ready"); nc_ok = sem("negc_ready"); lf_st = sem("logf_stored")
    ld_qk = sem("qk_landed"); ld_v = sem("v_landed"); ld_n = sem("negc_landed")
    s_done = sem("scores_done"); m_done = sem("max_done"); e_done = sem("exp_done"); p_done = sem("probs_ready")
    o_done = sem("out_done"); o_read = sem("out_read"); f_done = sem("fox_head_ready")
    ld_r = sem("ret_landed"); ld_s = sem("sample_state_landed")
    r_a = sem("ret_scores_done"); r_ad = sem("ret_scores_read"); r_b = sem("ret_out_done"); r_bd = sem("ret_out_read")
    r_t = sem("ret_turned"); r_tr = sem("ret_turn_read"); r_n = sem("ret_normed"); r_ok = sem("ret_head_ready")
    r_v = sem("ret_var_ready"); r_st = sem("ret_state_ready"); r_sto = sem("ret_stored")
    ar_in = [sem(f"act_landed{i}") for i in range(3)]
    g_in = [sem("gate_landed0"), sem("gate_landed1")]
    m_ok = sem("merged_ready"); x2_in = [sem("x_again0"), sem("x_again1")]; g2_in = sem("norm2_landed")
    h_ok = sem("h_ready"); h_st = sem("h_stored"); hb_in = [sem("h_back0"), sem("h_back1")]
    u_relu = sem("relu_ready"); u_sq = sem("u_ready"); u_hi = sem("u_hi_ready"); u_lo = sem("u_lo_ready")
    y_acc = sem("y_accumulated"); y_ok = sem("y_rows_ready"); y_st = [sem("y_stored0"), sem("y_stored1")]

    block = ctx.enter_context(nc.Block())

    @block.sync
    def _(sp):
        sp.dma_start(ident[:], c_ident).then_inc(const_in, 16)
        sp.dma_start(maskf[:], c_mask).then_inc(const_in, 16)
        sp.dma_start(g1[:], norm1_g[0].partition_broadcast(P)).then_inc(const_in, 16)
        for i in range(NT):
            sp.dma_start(xt[:, i, :], xp[i * P:(i + 1) * P, :]).then_inc(x_in[i], 16)
        sp.wait_ge(pad_ok, 1)
        sp.dma_start(xt[0:NS, NT, :], xs).then_inc(x_in[NT], 16)
        sp.dma_start(xt[NS:NS + NM, NT, :], meta).then_inc(x_in[NT], 16)
        load_unit(sp, At(0), win[:, :, W_FF:W_FF + P])
        sp.dma_start(bfT[:], b_forget.rearrange("a h -> h a")).then_inc(small_in, 16)
        cols = [W_FQ, W_FK, W_FV, W_RV]

        def strip_units(u, c):
            for j in range(2):
                load_unit(sp, u + j, win[:, 4 * j:4 * j + 4, c])

        for s in range(2):
            strip_units(At(U_STRIP + 2 * s), slice(W_FQ + 256 * s, W_FQ + 256 * s + 256))
            if s == 0:
                sp.wait_ge(a_lo, A_NORM1)
                for dst, src in ((cosT[:], c_cos), (sinT[:], c_sin), (gq[:], q_norm_g[0].partition_broadcast(P)),
                                 (gk[:], k_norm_g[0].partition_broadcast(P)),
                                 (crow[:], clf.rearrange("(c p) h -> p c h", p=P))):
                    sp.dma_start(dst, src).then_inc(small_in, 16)
        for s in range(2, 4):
            strip_units(At(U_STRIP + 2 * s), slice(W_FQ + 256 * s, W_FQ + 256 * s + 256))
        for kind in range(1, 4):
            with sp.Fori(0, 2) as i:
                for s in range(2):
                    strip_units(At(U_STRIP + 8 * kind + 2 * s, 4, i), bass.ds(i * 512 + (cols[kind] + 256 * s), 256))
        with sp.Fori(0, 8) as i:
            for q, c in enumerate((W_RQ, W_RG, W_GA, W_GB)):
                load_unit(sp, At(U_TURN + q, 4, i), win[:, :, bass.ds(i * P + c, P)])

        def load_qk(h):
            hc = h if isinstance(h, slice) else bass.ds(h * P, P)
            for dst, src in ((qrow[:], pq[NM:, hc].rearrange("(i p) d -> p i d", p=P)), (qsrow[:], sq[:, hc]),
                             (krow[:], pk[NM:, hc].rearrange("(i p) d -> p i d", p=P)), (kmrow[:], pk[0:NM, hc]),
                             (ksrow[:], sk[:, hc]), (kcrow[:], ck[:, hc].rearrange("(i p) d -> p i d", p=P))):
                sp.dma_start(dst, src).then_inc(ld_qk, 16)

        def load_v(h):
            hc = h if isinstance(h, slice) else bass.ds(h * P, P)
            for dst, src in ((vrow[:], pv[NM:, hc].rearrange("(i p) d -> p i d", p=P)), (vmrow[:], pv[0:NM, hc]),
                             (vsrow[:], sv[:, hc]), (vcrow[:], cv[:, hc].rearrange("(i p) d -> p i d", p=P))):
                sp.dma_start(dst, src).then_inc(ld_v, 16)
            row = negc[:, 0, :] if isinstance(h, slice) else negc[:, bass.ds(h, 1), :].rearrange("a b n -> a (b n)")
            sp.dma_start(ncr[0:2, :].bitcast(F32), row.bitcast(F32)).then_inc(ld_n, 16)

        for q in range(2):
            load_unit(sp, At(U_FOX + q), wfo[:, :, q * P:q * P + P])
        sp.wait_ge(stored, ST_ATT)
        sp.wait_ge(lf_st, 64)
        sp.wait_ge(ncr_zero, 1)
        load_qk(slice(0, P))
        load_v(slice(0, P))
        with sp.Fori(1, FH) as h:
            sp.wait_ge(s_done, h * 9 - 8)
            load_qk(h)
            sp.wait_ge(o_done, h * 9)
            load_v(h)

        def load_ret(r):
            pick = (lambda x, k, b: x[b]) if r is None else (lambda x, k, b: x[bass.ds(r * k + b, 1)].rearrange("a p n -> (a p) n"))
            vc = slice(0, RV) if r is None else bass.ds(r * RV, RV)
            for dst, src in ((rqT[:], pick(rot, 1, 0)), (rkT[:], pick(rot, 1, 4)),
                             (rvrow[:], prv[NM:, vc].rearrange("(i p) d -> p i d", p=P)), (rvm[:], prv[0:NM, vc]),
                             (rvs[:], srv[:, vc]), (dec[:], pick(c_decay, 1, 0)), (rgT[:, 0, :], pick(gates, 2, 0)),
                             (rgT[:, 1, :], pick(gates, 2, 1)), (s0s[:], pick(st_in, 1, 0))):
                sp.dma_start(dst, src).then_inc(ld_r, 16)

        sp.wait_ge(stored, ST_RET)
        sp.dma_start(gnT[:], ret_gn_g.rearrange("a (k p) -> p (a k)", p=P), allow_slow_non_contiguous=True).then_inc(ld_g, 16)
        sp.wait_ge(yz_ok, 1)
        load_ret(None)
        with sp.Fori(1, RH) as r:
            sp.wait_ge(r_sto, r * 64)
            load_ret(r)

        sp.wait_ge(r_sto, RH * 64)
        for b, src in enumerate((foxT, retT)):
            for k in range(KC):
                x = 8 * b + k
                wait(sp, a_lo, A_NORM1 + x - 2 if x > 2 else 0)
                sp.dma_start(araw[:, x % 3, :], src[k]).then_inc(ar_in[x % 3], 16)
            for q in range(KC):
                sp.wait_ge(bank_free, N_FOX + 24 * b + 3 * q - 3)
                sp.dma_start(gate[:, q % 2, :], gates[16 - 8 * b + q]).then_inc(g_in[q % 2], 16)
                if q + 2 < KC:
                    load_unit(sp, At(U_FOX + 8 * b + q + 2), (wfo, wro)[b][:, :, (q + 2) * P:(q + 3) * P])
                elif b == 0:
                    load_unit(sp, At(U_RET + q - 6), wro[:, :, (q - 6) * P:(q - 5) * P])
                else:
                    load_unit(sp, At(U_WO + q - 6), wout[:, 4 * (q - 6):4 * (q - 6) + 4, 0:256])

        sp.wait_ge(a_lo, A_M)
        sp.wait_ge(hz_ok, 1)
        sp.dma_start(g2[:], norm2_g[0].partition_broadcast(P)).then_inc(g2_in, 16)
        for s in range(4):
            c = slice(256 * s, 256 * s + 256)
            if s >= 2:
                sp.wait_ge(bank_free, N_WO + NQ * (s - 1))
            sp.dma_start(xrow[:, s % 2, 0:NT, :], xp[:, c].rearrange("(i p) d -> p i d", p=P)).then_inc(x2_in[s % 2], 16)
            sp.dma_start(xrow[0:NS, s % 2, NT, :], xs[:, c]).then_inc(x2_in[s % 2], 16)
            for j in range(2 if s else 0):
                load_unit(sp, At(U_WO + 2 * s + j), wout[:, 4 * j:4 * j + 4, c])

        with sp.Fori(0, 8) as g:
            for q in range(4):
                load_unit(sp, At(U_MLP + q, 8, g), wf1[:, :, bass.ds(g * 512 + q * P, P)])
            for q in range(4):
                load_unit(sp, At(U_MLP + 4 + q, 8, g), wf2[:, bass.ds(g * 4, 4), 256 * q:256 * q + 256])

        sp.wait_ge(h_st, 32)
        sp.wait_ge(bank_free, N_MLP + 8 * G_N)

        def hload(i):
            n = P if i < NT else NS
            sp.dma_start(hback[0:n, i % 2, :], hrow[i * P:i * P + n, :]).then_inc(hb_in[i % 2], 16)

        hload(0)
        hload(1)
        for i in range(NQ):
            sp.wait_ge(y_rd, 2 * i + 2)
            n = P if i < NT else NS
            sp.dma_start(yp[i * P:i * P + P, :] if i < NT else ys, yout[0:n, i % 2, :]).then_inc(y_st[i % 2], 16)
            if i + 2 < NQ:
                hload(i + 2)
        sp.wait_ge(y_st[0], 16 * 5)
        sp.wait_ge(y_st[1], 16 * 4)
        sp.wait_ge(lf_st, 64)
        sp.wait_ge(stored, ST_RET)
        sp.wait_ge(r_sto, RH * 64)

    @block.gpsimd
    def _(pool):
        nc.gpsimd.memset(xt[:, NT, :], 0.0).then_inc(pad_ok, 1)

        def store_strip(s, prompt, sample, c, normed, n=None):
            if normed:
                pool.wait_ge(strip_ok, (s + 1).v)
            else:
                pool.wait_ge(bank_free, (n + NQ).v)
            src = rows[:, s.mod(2)]
            pool.dma_start(prompt[NM:, c].rearrange("(i p) d -> p i d", p=P), src[:, 0:NT, :]).then_inc(stored, 16)
            pool.dma_start(sample[:, c], src[0:NS, NT, :]).then_inc(stored, 16)
            pool.dma_start(prompt[0:NM, c], src[NS:NS + NM, NT, :]).then_inc(stored, 16)
            pool.wait_ge(stored, s.times(ST_STRIP, ST_STRIP))

        def store_logf():
            pool.wait_ge(nc_ok, 1)
            pool.dma_start(negc.rearrange("a h n -> h a n").bitcast(F32), nchl[:].bitcast(F32)).then_inc(lf_st, 16)
            pool.wait_ge(lf_r, 1)
            pool.dma_start(plf[NM:, :].rearrange("(i p) h -> p i h", p=P), lfr[:, 0:NT, :]).then_inc(lf_st, 16)
            pool.dma_start(slf, lfr[0:NS, NT, :]).then_inc(lf_st, 16)
            pool.dma_start(plf[0:NM, :], lfr[NS:NS + NM, NT, :]).then_inc(lf_st, 16)
            pool.wait_ge(lf_st, 64)

        store_logf()
        for s in range(4):
            store_strip(At(s), pq, sq, slice(256 * s, 256 * s + 256), True)
        for kind, (p_rows, s_rows) in ((1, (pk, sk)), (2, (pv, sv)), (3, (prv, srv))):
            with pool.Fori(0, 2) as i:
                for s in range(2):
                    store_strip(At(4 * kind + s, 2, i), p_rows, s_rows, bass.ds(i * 512 + 256 * s, 256), kind == 1,
                                At(N_STRIP + NQ * (4 * kind + s), 2 * NQ, i))
        with pool.Fori(0, 8) as i:
            pool.wait_ge(unit_v, (At(1, 1, i)).v)
            pool.dma_start(rot[bass.ds(i, 1)].rearrange("a p n -> (a p) n"), stage[:, 0, :]).then_inc(stored, 16)
            pool.wait_ge(stored, At(ST_TURN + 16, 64, i).v)
            for q in range(3):
                pool.wait_ge(unit_a, At(q + 1, 3, i).v)
                dst = gates[bass.ds(i + 8 * q, 1)].rearrange("a p n -> (a p) n")
                pool.dma_start(dst, stage[:, (q + 1) % 2, 0:TOUT]).then_inc(stored, 16)
                pool.wait_ge(stored, At(ST_TURN + 32 + 16 * q, 64, i).v)
        nc.gpsimd.memset(ncr[:].bitcast(F32), 0.0).then_inc(ncr_zero, 1)
        with pool.Fori(0, FH) as h:
            pool.wait_ge(o_read, At(O0 + 9, 9, h).v)
            pool.dma_start(foxT[bass.ds(h, 1)].rearrange("a p n -> (a p) n"), fst[:]).then_inc(stored, 16)
            pool.wait_ge(stored, At(ST_ATT + 16, 16, h).v)
        nc.gpsimd.memset(yraw[:, NT, :], 0.0)
        nc.gpsimd.memset(bns[:, NT, :], 1.0).then_inc(yz_ok, 1)
        with pool.Fori(0, RH) as r:
            pool.wait_ge(r_bd, At(NCH, NCH, r).v)
            pool.dma_start(pst[bass.ds(r, 1)].rearrange("a p n -> (a p) n"), state[:]).then_inc(r_sto, 16)
            pool.dma_start(sst[bass.ds(r, 1)].rearrange("a p n -> (a p) n"), s0s[:]).then_inc(r_sto, 16)
            pool.wait_ge(r_tr, At(5, 5, r).v)
            for e in range(2):
                pool.dma_start(retT[bass.ds(r * 2 + e, 1)].rearrange("a p n -> (a p) n"), rst[:, e, :]).then_inc(r_sto, 16)
            pool.wait_ge(r_sto, At(64, 64, r).v)
        pool.wait_ge(a_lo, A_M)
        nc.gpsimd.memset(hsb[:, NT, :], 0.0).then_inc(hz_ok, 1)
        pool.wait_ge(bank_free, N_MLP)
        pool.dma_start(hrow[0:SEQ, :].rearrange("(i p) d -> p i d", p=P), hsb[:, 0:NT, :]).then_inc(h_st, 16)
        pool.dma_start(hrow[SEQ:, :], hsb[0:NS, NT, :]).then_inc(h_st, 16)
        pool.wait_ge(h_st, 32)

    @block.tensor
    def _(pe):
        pe.wait_ge(const_in, 48)
        for i in range(NQ):
            turn_rows_pe(pe, xn, i, 0, 0)
        pe.wait_ge(a_lo, A_NORM1)
        pe.wait_ge(w_lo_s, 1)
        for j, (c, w) in enumerate(T3):
            turned_step(pe, At(j), 0, c, w)

        def strip(u, n):
            pe.wait_ge(w_lo_s, (u + 2).v)
            for i in range(NQ):
                strip_step(pe, n + i, u, i)

        def logf_turns():
            pe.wait_ge(small_in, 96)
            for c in range(NC):
                mm = nc.tensor.transpose(pt[0:FH, 0, c * P:c * P + P], crow[:, c, :], ident[:])
            mm.then_inc(t_done[0], 1)
            pe.wait_ge(lf_ok, 1)
            for i in range(NQ):
                w = P if i < NT else NS + NM
                mm = nc.tensor.transpose(pt[0:w, 1, FH * i:FH * i + FH], lf[:, i * P:i * P + w], ident[0:FH, 0:FH])
            mm.then_inc(t_done[1], 1)

        for s in range(4):
            strip(At(U_STRIP + 2 * s), At(N_STRIP + NQ * s))
            if s == 0:
                logf_turns()
        for kind in range(1, 4):
            with pe.Fori(0, 2) as i:
                for s in range(2):
                    strip(At(U_STRIP + 8 * kind + 2 * s, 4, i), At(N_STRIP + NQ * (4 * kind + s), 2 * NQ, i))
        with pe.Fori(0, 8) as i:
            for q in range(4):
                pe.wait_ge(w_lo_s, At(U_TURN + q + 1, 4, i).v)
                for j, (c, w) in enumerate(T3 if q == 0 else O3):
                    turned_step(pe, At(N_TURN + 3 * q + j, 12, i), (U_TURN + q) % 4, c, w)

        T_READ0 = (1, 1)

        def tgroup(h, g):
            j, blocks, bank = GROUPS[g]
            pe.wait_ge(t_read[bank], At(T_READ0[bank] + nth(g), PER_BANK[bank], h).v)
            if j < 0:
                for src, c, n in turn_prologue(blocks)[0]:
                    mm = nc.tensor.transpose(pt[:, bank, c:c + n], src, ident[0:n, 0:n])
            else:
                for x, b in enumerate(blocks):
                    c, k = prob_block(j, b)
                    m, o = (NS, P + (x - 1) * NS) if j == NT and x else (P, x * P)
                    mm = nc.tensor.transpose(pt[0:k, bank, o:o + m], prob[0:m, j % 2, c:c + k], ident[0:m, 0:m])
            mm.then_inc(t_done[bank], 1)

        def turned_before(h, g):
            for b in range(2):
                pe.wait_ge(t_read[b], At(T_READ0[b] + sum(x[2] == b for x in GROUPS[:g]), PER_BANK[b], h).v)

        def scores(h, j):
            pe.wait_ge(e_done, At(E0 + j, 9, h).v)
            if j == 0:
                turned_before(h, 6)
                pe.wait_ge(ld_n, At(16, 16, h).v)
            if j < NT:
                n = NM + P * (j + 1)
                for a in range(0, n, 512):
                    b = min(n, a + 512)
                    d0 = max(a, n - P)
                    nc.tensor.matmul(ps[:, a:b], qT[:, j * P:j * P + P], kT[:, a:b], start=True, stop=False)
                    mm = nc.tensor.matmul(ps[:, a:b], onesr[:], ncr[:, a:b], start=False, stop=(d0 >= b))
                    if d0 < b:
                        mm = nc.tensor.matmul(ps[:, d0:b], identr[:], maskr[:, d0 - n + P:b - n + P], start=False, stop=True)
            else:
                q, o1 = qT[:, SEQ:TOUT], onesr[:, 0:NS].bitcast(F32)
                nr = ncr[:].bitcast(F32)
                nc.tensor.matmul(ps[0:NS, 0:512], q, kcT[:], start=True, stop=False)
                nc.tensor.matmul(ps[0:NS, 0:512], o1, nr[:, NKEY:NKEY + NPAST], start=False, stop=True)
                nc.tensor.matmul(ps[0:NS, 512:512 + NS], q, kT[:, NKEY:NKEY + NS], start=True, stop=False)
                nc.tensor.matmul(ps[0:NS, 512:512 + NS], o1, nr[:, NKEY + NPAST:], start=False, stop=False)
                mm = nc.tensor.matmul(ps[0:NS, 512:512 + NS], ident[:, 0:NS], maskr[:, 0:NS].bitcast(F32), start=False, stop=True)
            mm.then_inc(s_done, 1)

        def weigh(h, j):
            pe.wait_ge(p_done, At(j + 1, 9, h).v)
            gs = step_groups(j)
            for g in gs:
                tgroup(h, g)
            turned_before(h, gs[-1] + 1)
            if j == 0:
                pe.wait_ge(ld_v, At(64, 64, h).v)
            pe.wait_ge(o_read, At(O0 + j, 9, h).v)
            w = NS if j == NT else P
            if j == NT:
                parts = [(vcrow[:, b, :], pT[:, b, 0:w]) for b in range(NC)] + [(vsrow[:], pT[0:NS, NC, 0:w])]
            else:
                parts = [(vrow[:, b, :], pT[:, b, 0:w]) for b in range(j + 1)] + [(vmrow[:], pT[0:NM, NT, 0:w])]
            for x, (a, b) in enumerate(parts):
                mm = nc.tensor.matmul(po[:, 0:w], a, b, start=(x == 0), stop=(x == len(parts) - 1))
            mm.then_inc(o_done, 1)

        with pe.Fori(0, FH) as h:
            pe.wait_ge(ld_qk, At(96, 96, h).v)
            for g in range(6):
                tgroup(h, g)
            scores(h, 0)
            for j in range(1, 9):
                scores(h, j)
                weigh(h, j - 1)
            weigh(h, 8)

        def ret_a(r, c):
            c0, m = CH[c]
            if c:
                pe.wait_ge(r_ad, At(c, NCH, r).v)
                nc.tensor.matmul(ps[0:m, 0:m], rkT[:, c0:c0 + m], rqT[:, c0:c0 + m], start=True, stop=True)
            nc.tensor.transpose(pt[0:m, 0, 0:P], rkT[:, c0:c0 + m], ident[:]).then_inc(r_a, 1)

        def ret_b(r, c):
            c0, m = CH[c]
            pe.wait_ge(r_ad, At(c + 1, NCH, r).v)
            if c:
                pe.wait_ge(r_bd, At(c, NCH, r).v)
            v = rvm[:] if c == 0 else (rvs[:] if c == NCH - 1 else rvrow[:, c - 1, :])
            mm = nc.tensor.matmul(ps[:, 1024:1024 + RV], kd[0:m, c % 2, :], v, start=True, stop=True)
            if c == 0:
                mm.then_inc(r_b, 1)
            else:
                st = s0s if c == NCH - 1 else state
                nc.tensor.matmul(ps[0:m, 512:512 + RV], sTd[0:m, c % 2, 0:m], v, start=True, stop=False)
                nc.tensor.matmul(ps[0:m, 512:512 + RV], qg[:, c % 2, 0:m], st[:], start=False, stop=True).then_inc(r_b, 1)

        with pe.Fori(0, RH) as r:
            pe.wait_ge(ld_r, At(9 * 16, 9 * 16, r).v)
            ret_a(r, 0)
            for c in range(1, NCH):
                ret_a(r, c)
                ret_b(r, c - 1)
            ret_b(r, NCH - 1)
            pe.wait_ge(r_n, r + 1)
            for q, (e, tiles) in enumerate(RT_GROUPS):
                if q >= 2:
                    pe.wait_ge(r_tr, At(q - 1, 5, r).v)
                for x, (ee, i, w) in enumerate(tiles):
                    mm = nc.tensor.transpose(pt[:, q % 2, P * x:P * x + w], yraw[0:w, i, ee * P:ee * P + P], ident[0:w, 0:w])
                mm.then_inc(r_t, 1)

        for b in range(2):
            pe.wait_ge(a_lo, (A_FOX, A_RET)[b])
            with pe.Fori(0, 2) as i:
                for q in range(4):
                    pe.wait_ge(w_lo_s, At(U_FOX + 8 * b + q + 1, 4, i).v)
                    for j, (c, w) in enumerate(O3):
                        turned_step(pe, At(N_FOX + 24 * b + 3 * q + j, 12, i), (U_FOX + q) % 4, c, w)
        pe.wait_ge(a_lo, A_M)
        for s in range(4):
            strip(At(U_WO + 2 * s), At(N_WO + NQ * s))
        for i in range(NQ):
            turn_rows_pe(pe, hn, i, A_M, NQ)
        pe.wait_ge(a_lo, A_NORM2)

        with pe.Fori(0, 8) as g:
            for q in range(4):
                pe.wait_ge(w_lo_s, At(U_MLP + q + 1, 8, g).v)
                for j, (c, w) in enumerate(O3):
                    turned_step(pe, At(N_MLP + 3 * q + j, G_N, g), (U_MLP + q) % 4, c, w)
            for q in range(4):
                pe.wait_ge(w_lo_s, At(U_MLP + 5 + q, 8, g).v)
                if q == 0:
                    pe.wait_ge(u_lo, At(12, 12, g).v)
                for m in range(2):
                    for j, (c, w) in enumerate(O3):
                        turned_step(pe, At(N_MLP + 12 + 6 * q + 3 * m + j, G_N, g), (U_MLP + q) % 4, c, w,
                                    hi=uh, lo=ul, kc=4, m0=m * P)
        pe.wait_ge(bank_free, N_MLP + 8 * G_N)
        for i in range(NQ):
            w = P if i < NT else NS
            for g in range(2):
                if i:
                    pe.wait_ge(y_rd, 2 * i + g - 1)
                for c in range(4):
                    mm = nc.tensor.transpose(pt[0:w, g, c * P:c * P + P], yT[:, 4 * g + c, i * P:i * P + w], ident[:])
                mm.then_inc(t_done[g], 1)

    @block.scalar
    def _(act):
        for i in range(NQ):
            act.wait_ge(x_in[i], 16 if i < NT else 32)
            wait(act, a_ssq, i - 1)
            nc.scalar.activation(xsq[:, i % 2, :], xt[:, i, :], ACT.Square, accum_out=stat[:, 0, i:i + 1]).then_inc(a_ssq, 1)
        act.wait_ge(dch, CH_ROOT1)
        nc.scalar.activation(stat[:, 2, 0:NQ], stat[:, 1, 0:NQ], ACT.Sqrt).then_inc(a_root, 1)
        for i in range(NQ):
            turn_rows_act(act, i, (0, 0))
        split_hi(act, At(0), At(0))
        split_hi(act, At(1), At(0))
        split_hi(act, At(2), At(0))
        act.wait_ge(lf_raw, 1)
        nc.scalar.activation(lfc[:, 0, :], lfc[:, 1, :], ACT.Exp, scale=-1.0).then_inc(e_done, 1)
        act.wait_ge(e_done, 1)
        nc.scalar.activation(lfc[:, 1, :], lfc[:, 0, :], ACT.Ln, bias=1.0).then_inc(lf_e, 1)

        def logf_rows():
            act.wait_ge(t_done[1], NQ + 1)
            nc.scalar.copy(lfr[:, 0:NT, :], pt[:, 1, 0:NT * FH].rearrange("p (i h) -> p i h", h=FH)).then_inc(t_read[1], 1)
            nc.scalar.copy(lfr[0:NS + NM, NT, :], pt[0:NS + NM, 1, NT * FH:NQ * FH]).then_inc(lf_r, 1)

        def strip(s, u, n, squares):
            for j in range(2):
                split_hi(act, u + 2 + j, n)
            if squares:
                for i in range(NQ):
                    act.wait_ge(bank_free, (n + i + 1).v)
                    for e in range(2):
                        ins = nc.scalar.activation(junk[:, 2 * i + e, :], rows[:, s.mod(2), i, e * P:e * P + P], ACT.Square,
                                                   accum_out=stat[:, 0, 2 * i + e:2 * i + e + 1])
                ins.then_inc(ssq2, 1)
                act.wait_ge(ssq_v, (s + 1).v)
                nc.scalar.activation(stat[:, 2, :], stat[:, 1, :], ACT.Sqrt).then_inc(a_root, 1)

        for s in range(4):
            strip(At(s), At(U_STRIP + 2 * s), At(N_STRIP + NQ * s), True)
            if s == 0:
                logf_rows()
        for kind in range(1, 4):
            with act.Fori(0, 2) as i:
                for s in range(2):
                    strip(At(4 * kind + s, 2, i), At(U_STRIP + 8 * kind + 2 * s, 4, i),
                          At(N_STRIP + NQ * (4 * kind + s), 2 * NQ, i), kind == 1)
        with act.Fori(0, 8) as i:
            for q in range(4):
                split_hi(act, At(U_TURN + q + 2, 4, i), At(N_TURN + 3 * q, 12, i))
                if q:
                    act.wait_ge(bank_free, At(N_TURN + 3 * q + 3, 12, i).v)
                    s_ = stage[:, q % 2, 0:TOUT]
                    nc.scalar.activation(s_, s_, ACT.Silu if q == 1 else ACT.Sigmoid).then_inc(unit_a, 1)

        def exps(h, j):
            act.wait_ge(m_done, At(j + 1, 9, h).v)
            m, n = (P, NM + P * (j + 1)) if j < NT else (NS, NPAST + NS)
            nc.scalar.activation(prob[0:m, j % 2, 0:n], ps[0:m, 0:n], ACT.Exp, bias=mx[0:m, j % 2:j % 2 + 1],
                                 accum_out=lsum[0:m, j % 2:j % 2 + 1]).then_inc(e_done, 1)

        def reads(h, gs):
            for g in gs:
                if GROUPS[g][2] == 1:
                    act.wait_ge(t_done[1], At(T_ATT[1] + nth(g) + 1, PER_BANK[1], h).v)
                    read_group(lambda o, i_: nc.scalar.copy(o, i_), g).then_inc(t_read[1], 1)

        with act.Fori(0, FH) as h:
            reads(h, range(6))
            exps(h, 0)
            for j in range(1, 9):
                exps(h, j)
                reads(h, step_groups(j - 1))
            reads(h, step_groups(8))

        with act.Fori(0, RH) as r:
            act.wait_ge(r_v, r + 1)
            nc.scalar.activation(stat[:, 2, 0:NQ], stat[:, 1, 0:NQ], ACT.Sqrt).then_inc(a_root, 1)

        for b in range(2):
            for k in range(KC):
                x = 8 * b + k
                act.wait_ge(ar_in[x % 3], 16 * (x // 3 + 1))
                act.wait_ge(mm_done, (N_FOX, N_RET)[b])
                nc.scalar.copy(xh[:, k, 0:TOUT], araw[:, x % 3, :]).then_inc(a_hi, 1)
            with act.Fori(0, 2) as i:
                for q in range(4):
                    split_hi(act, At(U_FOX + 8 * b + q + 2, 4, i), At(N_FOX + 24 * b + 3 * q, 12, i))
        for k in range(KC):
            act.wait_ge(mm_done, N_WO)
            act.wait_ge(m_ok, 24)
            nc.scalar.copy(xh[:, k, 0:TOUT], mT[:, k, :]).then_inc(a_hi, 1)
        for s in range(4):
            for j in range(2):
                split_hi(act, At(U_WO + 2 * s + 2 + j), At(N_WO + NQ * s))
        act.wait_ge(bank_free, N_MLP)
        for i in range(NQ):
            wait(act, a_ssq, NQ + i - 1)
            nc.scalar.activation(hsq[:, i % 2, :], hsb[:, i, :], ACT.Square, accum_out=stat[:, 0, i:i + 1]).then_inc(a_ssq, 1)
        act.wait_ge(r_v, RH + 1)
        nc.scalar.activation(stat[:, 2, 0:NQ], stat[:, 1, 0:NQ], ACT.Sqrt).then_inc(a_root, 1)
        for i in range(NQ):
            turn_rows_act(act, i, T_NORM2)

        def mlp_group(g, tail):
            for q in range(4):
                split_hi(act, At(U_MLP + q + 2, 8, g), At(N_MLP + 3 * q, G_N, g))
                for j, (c, w) in enumerate(O3):
                    n = At(N_MLP + 3 * q + j, G_N, g)
                    act.wait_ge(mm_done, (n + 1).v)
                    par = (3 * q + j) % 2
                    nc.scalar.activation(relu[:, par, 0:w], pd[:, n.mod(NB), 0:w], ACT.Relu).then_inc(u_relu, 1)
                    act.wait_ge(bank_free, (n + 1).v)
                    nc.scalar.copy(uh[:, q, c:c + w], usq[:, par, 0:w]).then_inc(u_hi, 1)
            for q in range(4):
                if q < 2 or not tail:
                    split_hi(act, At(U_MLP + 6 + q, 8, g), At(N_MLP + 12 + 6 * q, G_N, g))

        with act.Fori(0, 7) as g:
            mlp_group(g, False)
        mlp_group(7, True)

    @block.vector
    def _(dve):
        ch = [At(0)]
        dve.wait_ge(const_in, 48)
        nc.vector.tensor_copy(identr[:], ident[:])
        nc.vector.tensor_copy(maskr[:], maskf[:])
        link(dve, nc.vector.memset(onesr[:].bitcast(F32), 0.0), ch)
        nc.vector.memset(onesr[0:2, :].bitcast(F32), 1.0).then_inc(const_ok, 1)
        dve.wait_ge(a_ssq, NQ)
        root_start(dve, stat[:, 0, 0:NQ], NQ, 1.0 / D, ch)
        assert ch[0].v == CH_ROOT1
        dve.wait_ge(a_root, 1)
        root_end(dve, NQ, 1.0, ch)

        def norm_row(i, src, dst, gain, t_base):
            if i >= 2:
                for g in range(2):
                    dve.wait_ge(t_done[g], t_base[g] + i - 1)
            nc.vector.scalar_tensor_tensor(dst[:, i % 2, :], src[:, i, :], stat[:, 5, i:i + 1], gain[:],
                                           ALU.mult, ALU.mult).then_inc(v_norm, 1)

        for i in range(NQ):
            norm_row(i, xt, xn, g1, (0, 0))
            if i:
                turn_rows_dve(dve, i - 1, 0)
        turn_rows_dve(dve, NQ - 1, 0)
        for u in range(3):
            split_lo(dve, At(u))
        dve.wait_ge(small_in, 96)
        for j, (c, w) in enumerate(T3):
            dve.wait_ge(mm_done, j + 1)
            ins = nc.vector.tensor_scalar(lf[:, c:c + w], pd[0:FH, j % NB, 0:w], bfT[:, 0:1], None, ALU.add)
            ins.then_inc(bank_free, 1)
        dve.wait_ge(bank_free, 3)
        nc.vector.scalar_tensor_tensor(lfc[:, 1, :], lf[:], -1.0, lf[:], ALU.mult, ALU.max).then_inc(lf_raw, 1)

        def logf_rest():
            dve.wait_ge(lf_e, 1)
            link(dve, nc.vector.memset(lfc[:, 0, :], 1.0), ch)
            nc.vector.scalar_tensor_tensor(lf[:], lf[:], 0.0, lfc[:, 1, :], ALU.min, ALU.subtract).then_inc(lf_ok, 1)
            dve.wait_ge(lf_ok, 1)
            one = lfc[:, 0, :]
            dve.wait_ge(t_done[0], NQ + 1)
            nc.vector.tensor_copy(cst[:, NKEY:NKEY + NPAST], pt[0:FH, 0, :]).then_inc(t_read[0], 1)
            dve.wait_ge(t_read[0], 1)
            nc.vector.tensor_tensor_scan(cst[:, 0:NM], one[:, 0:NM], lf[:, TOUT:TALL], 0.0, ALU.mult, ALU.add).then_inc(o_read, 1)
            dve.wait_ge(o_read, 1)
            link(dve, nc.vector.tensor_tensor_scan(cst[:, NM:NKEY], one[:, 0:SEQ], lf[:, 0:SEQ], cst[:, NM - 1:NM], ALU.mult, ALU.add), ch)
            link(dve, nc.vector.tensor_tensor_scan(cst[:, NKEY:NKEY + NPAST], one[:, 0:NPAST], cst[:, NKEY:NKEY + NPAST], 0.0, ALU.mult, ALU.add), ch)
            link(dve, nc.vector.tensor_tensor_scan(cst[:, NKEY + NPAST:], one[:, 0:NS], lf[:, SEQ:TOUT], cst[:, NKEY + NPAST - 1:NKEY + NPAST], ALU.mult, ALU.add), ch)
            link(dve, nc.vector.tensor_scalar(nchl[:, 0, :], cst[:], -1.0, None, ALU.mult), ch)
            nc.vector.scalar_tensor_tensor(nchl[:, 1, :], cst[:], -1.0, nchl[:, 0, :], ALU.mult, ALU.subtract).then_inc(nc_ok, 1)

        def strip(s, u, n, gain, scale):
            for j in range(2):
                split_lo(dve, u + 2 + j)
            for i in range(NQ):
                if i == 0:
                    wait(dve, stored, s.times(ST_STRIP, -ST_STRIP) if s.i is not None or s.first > 1 else 0)
                dve.wait_ge(mm_done, (n + i + 1).v)
                ins = nc.vector.tensor_copy(rows[:, s.mod(2), i, :], pd[:, (n + i).mod(NB), 0:256])
                ins.then_inc(bank_free, 1)
            if gain is None:
                return
            dve.wait_ge(ssq2, (s + 1).v)
            nc.vector.tensor_scalar(stat[:, 1, :], stat[:, 0, :], 1.0 / P, EPS, ALU.mult, ALU.add).then_inc(ssq_v, 1)
            dve.wait_ge(a_root, (s + 2).v)
            root_end(dve, 18, scale, ch)
            for i in range(NQ):
                for e in range(2):
                    x = rows[:, s.mod(2), i, e * P:e * P + P]
                    ins = nc.vector.scalar_tensor_tensor(x, x, stat[:, 5, 2 * i + e:2 * i + e + 1], gain[:], ALU.mult, ALU.mult)
            ins.then_inc(strip_ok, 1)

        for s in range(4):
            strip(At(s), At(U_STRIP + 2 * s), At(N_STRIP + NQ * s), gq, SCALE)
            if s == 0:
                logf_rest()
        for kind in range(1, 4):
            c0 = ch[0]
            per = 10 if kind == 1 else 0
            with dve.Fori(0, 2) as i:
                ch[0] = At(c0.first, per, i)
                for s in range(2):
                    strip(At(4 * kind + s, 2, i), At(U_STRIP + 8 * kind + 2 * s, 4, i),
                          At(N_STRIP + NQ * (4 * kind + s), 2 * NQ, i), gk if kind == 1 else None, 1.0)
                assert ch[0].first == c0.first + per
            ch[0] = At(c0.first + 2 * per)
        c0 = ch[0]
        with dve.Fori(0, 8) as i:
            for q in range(4):
                split_lo(dve, At(U_TURN + q + 2, 4, i))
                dve.wait_ge(stored, At(ST_TURN + 16 * max(q - 1, 0), 64, i).v)
                for j, (c, w) in enumerate(T3 if q == 0 else O3):
                    n = At(N_TURN + 3 * q + j, 12, i)
                    dve.wait_ge(mm_done, (n + 1).v)
                    z = pd[:, n.mod(NB), 0:w]
                    if q:
                        ins = nc.vector.tensor_copy(stage[:, q % 2, c:c + w], z)
                        ins.then_inc(bank_free, 1)
                        continue
                    tmp = rtmp[:, n.mod(2)]
                    nc.vector.tensor_tensor(tmp[:, 0, 0:w], z, cosT[:, c:c + w], ALU.mult)
                    nc.vector.tensor_tensor(tmp[0:64, 1, 0:w], z[64:P], sinT[64:P, c:c + w], ALU.mult)
                    nc.vector.tensor_tensor(tmp[64:P, 1, 0:w], z[0:64], sinT[0:64, c:c + w], ALU.mult).then_inc(bank_free, 1)
                    dve.wait_ge(bank_free, (n + 1).v)
                    ins = nc.vector.tensor_tensor(stage[:, 0, c:c + w], tmp[:, 0, 0:w], tmp[:, 1, 0:w], ALU.add)
                    if j == 2:
                        ins.then_inc(unit_v, 1)

        def maxes(h, j):
            dve.wait_ge(s_done, At(j + 1, 9, h).v)
            m, n = (P, NM + P * (j + 1)) if j < NT else (NS, NPAST + NS)
            nc.vector.tensor_reduce(mx[0:m, j % 2:j % 2 + 1], ps[0:m, 0:n], AX.X, ALU.max, negate=True).then_inc(m_done, 1)

        def scale_probs(h, j):
            dve.wait_ge(e_done, At(E0 + j + 1, 9, h).v)
            m, n = (P, NM + P * (j + 1)) if j < NT else (NS, NPAST + NS)
            link(dve, nc.vector.reciprocal(linv[0:m, j % 2:j % 2 + 1], lsum[0:m, j % 2:j % 2 + 1]), ch)
            nc.vector.tensor_scalar(prob[0:m, j % 2, 0:n], prob[0:m, j % 2, 0:n], linv[0:m, j % 2:j % 2 + 1], None,
                                    ALU.mult).then_inc(p_done, 1)

        def reads(h, gs):
            for g in gs:
                if GROUPS[g][2] == 0:
                    dve.wait_ge(t_done[0], At(T_ATT[0] + nth(g) + 1, PER_BANK[0], h).v)
                    read_group(lambda o, i_: nc.vector.tensor_copy(o, i_), g).then_inc(t_read[0], 1)

        def out_read(h, j):
            dve.wait_ge(o_done, At(j + 1, 9, h).v)
            if j == 0:
                dve.wait_ge(stored, At(ST_ATT, 16, h).v)
            w = NS if j == NT else P
            nc.vector.tensor_copy(fst[:, j * P:j * P + w], po[:, 0:w]).then_inc(o_read, 1)

        c0 = ch[0]
        with dve.Fori(0, FH) as h:
            ch[0] = At(c0.first, 9, h)
            reads(h, range(6))
            maxes(h, 0)
            for j in range(1, 9):
                scale_probs(h, j - 1)
                maxes(h, j)
                reads(h, step_groups(j - 1))
                out_read(h, j - 1)
            scale_probs(h, 8)
            reads(h, step_groups(8))
            out_read(h, 8)
        ch[0] = At(c0.first + 9 * FH)

        def ret_ad(r, c):
            c0_, m = CH[c]
            dve.wait_ge(r_a, At(c + 1, NCH, r).v)
            if c >= 2:
                dve.wait_ge(r_b, At(c - 1, NCH, r).v)
            kcol = D_COL + (C_KM if c == 0 else (C_KS if c == NCH - 1 else C_KP))
            if c:
                nc.vector.tensor_tensor(sTd[0:m, c % 2, 0:m], ps[0:m, 0:m], dec[0:m, 0:m], ALU.mult)
                nc.vector.tensor_tensor(qg[:, c % 2, 0:m], rqT[:, c0_:c0_ + m], dec[:, D_GQ:D_GQ + m], ALU.mult)
            nc.vector.tensor_scalar(kd[0:m, c % 2, :], pt[0:m, 0, 0:P], dec[0:m, kcol:kcol + 1], None, ALU.mult).then_inc(r_ad, 1)

        def ret_bd(r, c):
            c0_, m = CH[c]
            dve.wait_ge(r_b, At(c + 1, NCH, r).v)
            U = ps[:, 1024:1024 + RV]
            if c == 0:
                nc.vector.tensor_copy(state[:], U).then_inc(r_bd, 1)
                return
            i = c - 1
            nc.vector.tensor_copy(yraw[0:m, i, :], ps[0:m, 512:512 + RV])
            link(dve, nc.vector.bn_stats(bns[0:m, i, 0:6], ps[0:m, 512:512 + RV]), ch)
            st, gcol = (s0s, C_GS) if c == NCH - 1 else (state, C_GP)
            nc.vector.scalar_tensor_tensor(st[:], st[:], dec[:, D_COL + gcol:D_COL + gcol + 1], U, ALU.mult, ALU.add)
            nc.vector.bn_aggr(bns[0:m, i, 6:8], bns[0:m, i, 0:6]).then_inc(r_bd, 1)
            dve.wait_ge(r_bd, At(c + 1, NCH, r).v)

        c0 = ch[0]
        PER_R = 9 + 5
        with dve.Fori(0, RH) as r:
            ch[0] = At(c0.first, PER_R, r)
            dve.wait_ge(ld_r, At(9 * 16, 9 * 16, r).v)
            dve.wait_ge(ld_g, 16)
            ret_ad(r, 0)
            for c in range(1, NCH):
                ret_ad(r, c)
                ret_bd(r, c - 1)
            ret_bd(r, NCH - 1)
            nc.vector.tensor_scalar(stat[:, 1, 0:NQ], bns[:, :, 7], 1.0, EPS, ALU.mult, ALU.add).then_inc(r_v, 1)
            dve.wait_ge(a_root, At(10, 1, r).v)
            root_end(dve, NQ, 1.0, ch)
            for i in range(NQ):
                m = P if i < NT else NS
                ins = nc.vector.tensor_scalar(yraw[0:m, i, :], yraw[0:m, i, :], bns[0:m, i, 6:7], stat[0:m, 5, i:i + 1],
                                              ALU.subtract, ALU.mult)
            ins.then_inc(r_n, 1)
            for q, (e, tiles) in enumerate(RT_GROUPS):
                dve.wait_ge(r_t, At(q + 1, 5, r).v)
                if e is not None:
                    t0 = tiles[0][1] * P
                    ins = nc.vector.scalar_tensor_tensor(rst[:, e, t0:t0 + 512], pt[:, q % 2, :], gnT[:, bass.ds(r * 2 + e, 1)],
                                                         rgT[:, e, t0:t0 + 512], ALU.mult, ALU.mult)
                else:
                    for ee in range(2):
                        ins = nc.vector.scalar_tensor_tensor(rst[:, ee, SEQ:TOUT], pt[:, q % 2, P * ee:P * ee + NS],
                                                             gnT[:, bass.ds(r * 2 + ee, 1)], rgT[:, ee, SEQ:TOUT], ALU.mult, ALU.mult)
                ins.then_inc(r_tr, 1)
            assert ch[0].first == c0.first + PER_R, ch[0].first - c0.first
        ch[0] = At(c0.first + PER_R * RH)

        for b in range(2):
            for k in range(KC):
                x = 8 * b + k
                dve.wait_ge(a_hi, A_NORM1 + x + 1)
                nc.vector.tensor_tensor(xl[:, k, 0:TOUT], araw[:, x % 3, :], xh[:, k, 0:TOUT], ALU.subtract).then_inc(a_lo, 1)
            with dve.Fori(0, 2) as i:
                for q in range(4):
                    split_lo(dve, At(U_FOX + 8 * b + q + 2, 4, i))
                    dve.wait_ge(g_in[q % 2], At(16 * (4 * b + q // 2 + 1), 32, i).v)
                    for j, (c, w) in enumerate(O3):
                        n = At(N_FOX + 24 * b + 3 * q + j, 12, i)
                        dve.wait_ge(mm_done, (n + 1).v)
                        m = mT[:, bass.ds(i * 4 + q, 1), c:c + w].rearrange("p a n -> p (a n)")
                        z, gt = pd[:, n.mod(NB), 0:w], gate[:, q % 2, c:c + w]
                        if b == 0:
                            nc.vector.tensor_tensor(m, z, gt, ALU.mult).then_inc(bank_free, 1)
                        else:
                            nc.vector.tensor_tensor(mtmp[:, n.mod(2), 0:w], z, gt, ALU.mult).then_inc(bank_free, 1)
                            dve.wait_ge(bank_free, (n + 1).v)
                            nc.vector.tensor_tensor(m, m, mtmp[:, n.mod(2), 0:w], ALU.add).then_inc(m_ok, 1)
        for k in range(KC):
            dve.wait_ge(a_hi, A_RET + k + 1)
            nc.vector.tensor_tensor(xl[:, k, 0:TOUT], mT[:, k, :], xh[:, k, 0:TOUT], ALU.subtract).then_inc(a_lo, 1)

        dve.wait_ge(hz_ok, 1)
        for s in range(4):
            for j in range(2):
                split_lo(dve, At(U_WO + 2 * s + 2 + j))
            dve.wait_ge(x2_in[s % 2], 32 * (s // 2 + 1))
            for i in range(NQ):
                n = At(N_WO + NQ * s + i)
                dve.wait_ge(mm_done, (n + 1).v)
                m = P if i < NT else NS
                nc.vector.tensor_tensor(hsb[0:m, i, 256 * s:256 * s + 256], pd[0:m, n.mod(NB), 0:256],
                                        xrow[0:m, s % 2, i, :], ALU.add).then_inc(bank_free, 1)
        dve.wait_ge(a_ssq, 2 * NQ)
        nc.vector.tensor_scalar(stat[:, 1, 0:NQ], stat[:, 0, 0:NQ], 1.0 / D, EPS, ALU.mult, ALU.add).then_inc(r_v, 1)
        dve.wait_ge(a_root, 10 + RH)
        root_end(dve, NQ, 1.0, ch)
        dve.wait_ge(g2_in, 16)
        for i in range(NQ):
            norm_row(i, hsb, hn, g2, T_NORM2)
            if i:
                turn_rows_dve(dve, i - 1, A_M)
        turn_rows_dve(dve, NQ - 1, A_M)

        dve.wait_ge(h_st, 32)
        link(dve, nc.vector.memset(yT[:], 0.0), ch)
        def mlp_group(g, tail):
            for q in range(4):
                split_lo(dve, At(U_MLP + q + 2, 8, g))
                for j, (c, w) in enumerate(O3):
                    n = At(N_MLP + 3 * q + j, G_N, g)
                    par = (3 * q + j) % 2
                    dve.wait_ge(u_relu, At(3 * q + j + 1, 12, g).v)
                    nc.vector.scalar_tensor_tensor(usq[:, par, 0:w], pd[:, n.mod(NB), 0:w], 0.0, relu[:, par, 0:w],
                                                   ALU.max, ALU.mult).then_inc(bank_free, 1)
                    dve.wait_ge(u_hi, At(3 * q + j + 1, 12, g).v)
                    nc.vector.tensor_tensor(ul[:, q, c:c + w], usq[:, par, 0:w], uh[:, q, c:c + w], ALU.subtract).then_inc(u_lo, 1)
            for q in range(4):
                if q < 2 or not tail:
                    split_lo(dve, At(U_MLP + 6 + q, 8, g))
                for m in range(2):
                    for j, (c, w) in enumerate(O3):
                        n = At(N_MLP + 12 + 6 * q + 3 * m + j, G_N, g)
                        dve.wait_ge(mm_done, (n + 1).v)
                        dve.wait_ge(bank_free, n.v)
                        y = yT[:, 2 * q + m, c:c + w]
                        nc.vector.tensor_tensor(y, y, pd[:, n.mod(NB), 0:w], ALU.add).then_inc(bank_free, 1)

        with dve.Fori(0, 7) as g:
            mlp_group(g, False)
        mlp_group(7, True)
        for i in range(NQ):
            w = P if i < NT else NS
            dve.wait_ge(hb_in[i % 2], 16 * (i // 2 + 1))
            if i >= 2:
                dve.wait_ge(y_st[i % 2], 16 * (i // 2))
            for g in range(2):
                dve.wait_ge(t_done[g], T_FIN[g] + i + 1)
                nc.vector.tensor_tensor(yout[0:w, i % 2, 512 * g:512 * g + 512], pt[0:w, g, :],
                                        hback[0:w, i % 2, 512 * g:512 * g + 512], ALU.add).then_inc(y_rd, 1)

    ctx.close()


_INS = ["x_prompt", "x_sample", "state_ret", "cache_fox_k", "cache_fox_v", "cache_fox_logf", "meta_tokens",
        "norm1_g", "w_in", "b_forget", "q_norm_g", "k_norm_g", "ret_gn_g", "w_ret_out", "w_fox_out", "w_o",
        "norm2_g", "w_ff1", "w_ff2"]
_OUTS = [(1, 1024, 1024), (1, 32, 1024), (1, 1, 4, 128, 256), (1, 1, 1040, 8, 128), (1, 1, 1040, 8, 128),
         (1, 1, 1040, 8), (1, 1, 4, 128, 256), (1, 1, 32, 8, 128), (1, 1, 32, 8, 128), (1, 1, 32, 8)]


def shape_constants():
    import numpy as np

    f = np.float32
    ident = np.eye(P, dtype=f)
    mask = np.where(np.arange(P)[None, :] > np.arange(P)[:, None], f(NEG), f(0.0)).astype(f)
    pos = np.concatenate([np.arange(SEQ), NPAST + np.arange(NS), np.arange(NM) - NM]).astype(f)
    half = P // 2
    inv = (f(10000.0) ** (-np.arange(half, dtype=f) / f(half))).astype(f)
    ang = (pos[:, None] * inv[None, :]).astype(f)
    cos, sin = np.cos(ang).astype(f).T, np.sin(ang).astype(f).T
    cosT = np.concatenate([cos, cos], 0)
    sinT = np.concatenate([sin, -sin], 0)
    decay = np.zeros((RH, P, 264), f)
    n = np.arange(P, dtype=np.float64)
    for h in range(RH):
        lg = float(np.log(1.0 - 2.0 ** (-5.0 - h)))
        diff = n[None, :] - n[:, None]
        decay[h, :, 0:P] = np.where(diff >= 0, np.exp(lg * np.maximum(diff, 0)), 0) * SCALE
        decay[h, :, P:2 * P] = np.exp(lg * (n + 1))[None, :]
        decay[h, :, 2 * P + 0] = np.exp(lg * (P - 1 - n)) * SCALE
        decay[h, :, 2 * P + 1] = np.exp(lg * (NM - 1 - np.minimum(n, NM - 1))) * SCALE
        decay[h, :, 2 * P + 2] = np.exp(lg * (NS - 1 - np.minimum(n, NS - 1))) * SCALE
        decay[h, :, 2 * P + 3] = np.exp(lg * P)
        decay[h, :, 2 * P + 4] = np.exp(lg * NS)
    return {"ident": ident, "mask": mask, "cos": np.ascontiguousarray(cosT), "sin": np.ascontiguousarray(sinT),
            "decay": decay}


def kernel(**inputs):
    import numpy as np
    import concourse.bacc as _bacc
    from concourse.bass_utils import run_bass_kernel_spmd as _run

    nc = _bacc.Bacc("TRN2", target_bir_lowering=False, num_devices=1)
    arrays, args = {}, []
    named = [(n, inputs[n]) for n in _INS] + [(f"c_{n}", a) for n, a in shape_constants().items()]
    for name, a in named:
        a = np.ascontiguousarray(a)
        arrays[f"in_{name}"] = a
        args.append(nc.dram_tensor(f"in_{name}", a.shape, mybir.dt.from_np(a.dtype), kind="ExternalInput").ap())
    for i, shape in enumerate(_OUTS):
        args.append(nc.dram_tensor(f"out_{i}", shape, F32, kind="ExternalOutput").ap())
    hybrid_step(nc, *args)
    r = _run(nc, [arrays], core_ids=[0])
    return tuple(r.results[0][f"out_{i}"] for i in range(len(_OUTS)))
```

```python
from contextlib import ExitStack

import concourse.bass as bass
from concourse import mybir

F32 = mybir.dt.float32
F32R = mybir.dt.float32r
ALU = mybir.AluOpType
ACT = mybir.ActivationFunctionType
AX = mybir.AxisListType

P = 128
D = 1024
KC = D // P
SEQ = 1024
NT = SEQ // P
NS = 32
NM = 16
NPAST = 512
NC = NPAST // P
TOUT = SEQ + NS
TALL = TOUT + NM
TPAD = (NT + 1) * P
NQ = NT + 1
FH = 8
RH = 4
RV = 256
EPS = 1e-6
SCALE = float(P) ** -0.5
NEG = -1e30
W_RQ, W_RV, W_RG, W_FQ, W_FK, W_FV, W_FF, W_GA, W_GB = 0, 1024, 2048, 3072, 4096, 5120, 6144, 6152, 7176
UNIT = 1024
NB = 2


def hybrid_step(nc, x_prompt, x_sample, state_ret, cache_k, cache_v, cache_logf, meta, norm1_g, w_in,
                b_forget, q_norm_g, k_norm_g, ret_gn_g, w_ret_out, w_fox_out, w_o, norm2_g, w_ff1, w_ff2,
                c_ident, c_mask, c_cos, c_sin, c_decay,
                y_prompt, y_sample, p_state, p_k, p_v, p_logf, s_state, s_k, s_v, s_logf):
    ctx = ExitStack()

    def sb(name, shape, dt=F32, stack=ctx):
        return stack.enter_context(nc.sbuf_tensor(name, shape, dt))

    def sem(name):
        return ctx.enter_context(nc.semaphore(name))

    def wait(eng, s, value):
        if not isinstance(value, int) or value > 0:
            eng.wait_ge(s, value)

    xp = x_prompt.rearrange("a t d -> (a t) d")
    xs = x_sample.rearrange("a t d -> (a t) d")
    st_in = state_ret.rearrange("l b h d v -> (l b h) d v")
    ck = cache_k.rearrange("l b t h d -> (l b t) (h d)")
    cv = cache_v.rearrange("l b t h d -> (l b t) (h d)")
    clf = cache_logf.rearrange("l b t h -> (l b t) h")
    win = w_in.rearrange("l (k p) n -> p (l k) n", p=P)
    wro = w_ret_out.rearrange("l (k p) n -> p (l k) n", p=P)
    wfo = w_fox_out.rearrange("l (k p) n -> p (l k) n", p=P)
    wout = w_o.rearrange("l (k p) n -> p (l k) n", p=P)
    wf1 = w_ff1.rearrange("l (k p) n -> p (l k) n", p=P)
    wf2 = w_ff2.rearrange("l (k p) n -> p (l k) n", p=P)
    yp = y_prompt.rearrange("a t d -> (a t) d")
    ys = y_sample.rearrange("a t d -> (a t) d")
    pst = p_state.rearrange("l b h d v -> (l b h) d v")
    sst = s_state.rearrange("l b h d v -> (l b h) d v")
    pk = p_k.rearrange("l b t h d -> (l b t) (h d)")
    pv = p_v.rearrange("l b t h d -> (l b t) (h d)")
    plf = p_logf.rearrange("l b t h -> (l b t) h")
    sk = s_k.rearrange("l b t h d -> (l b t) (h d)")
    sv = s_v.rearrange("l b t h d -> (l b t) (h d)")
    slf = s_logf.rearrange("l b t h -> (l b t) h")

    def dram(name, shape, dt=F32):
        return nc.dram_tensor(name, shape, dt, kind="Internal").ap()

    pq = dram("q_rows", (NM + SEQ, D))
    sq = dram("q_rows_sample", (NS, D))
    prv = dram("rv_rows", (NM + SEQ, D))
    srv = dram("rv_rows_sample", (NS, D))
    rot = dram("rotated", (8, P, TALL))
    gates = dram("gates", (3 * KC, P, TOUT))
    negc = dram("neg_cumsum", (2, FH, SEQ + NM + NPAST + NS), F32R)
    foxT = dram("fox_out_T", (KC, P, TOUT))
    retT = dram("ret_out_T", (KC, P, TOUT))
    hrow = dram("h_rows", (TOUT, D))

    xh = sb("act_hi", [P, KC, TPAD], F32R)
    xl = sb("act_lo", [P, KC, TPAD], F32R)
    raw = sb("w_raw", [P, 2, UNIT])
    wh = sb("w_hi", [P, 4, UNIT], F32R)
    wl = sb("w_lo", [P, 4, UNIT], F32R)
    ident = sb("ident", [P, P])
    identr = sb("ident_r", [P, P], F32R)
    maskf = sb("mask", [P, P])
    maskr = sb("mask_r", [P, P], F32R)
    onesr = sb("ones_r", [P, P], F32R)
    stat = sb("stat", [P, 8, 18])
    gnT = sb("gn_gain", [P, KC])
    mx = sb("neg_max", [P, 2])
    lsum = sb("row_sum", [P, 2])
    linv = sb("row_sum_inv", [P, 2])
    bfT = sb("b_forget_col", [FH, 1])

    def arena(sizes):
        with ExitStack() as s:
            return [sb(n, shape, dt, s) for n, shape, dt in sizes]

    xt, xn, g1, xsq = arena([("x_rows", [P, NQ, D], F32), ("xn_rows", [P, 2, D], F32), ("norm1_bc", [P, D], F32), ("x_squares", [P, 2, D], F32)])
    lfc, cosT, sinT, rows, gq, gk, lf, cst, crow, lfr, nchl, junk = arena([
        ("lf_tmp", [FH, 2, TALL], F32), ("cos", [P, TALL], F32), ("sin", [P, TALL], F32),
        ("strip_rows", [P, 2, NQ, 256], F32), ("gq_bc", [P, P], F32), ("gk_bc", [P, P], F32), ("logf_T", [FH, TALL], F32),
        ("cumsum", [FH, TALL + NPAST], F32), ("cache_lf_rows", [P, NC, FH], F32),
        ("logf_rows", [P, NQ, FH], F32), ("negc_hl", [FH, 2, SEQ + NM + NPAST + NS], F32R), ("row_squares", [P, 18, P], F32)])
    (stage, _, _, prob, fst, rtmp, pT, ncr, qrow, qsrow, krow, kmrow, ksrow, kcrow, vrow, vmrow, vsrow, vcrow,
     qT, kT, kcT) = arena([
        ("stage", [P, 2, TALL], F32), ("cos_kept", [P, TALL], F32), ("sin_kept", [P, TALL], F32),
        ("probs", [P, 2, SEQ + NM], F32), ("fox_stage", [P, TOUT], F32), ("rot_tmp", [P, 2, 2, 360], F32),
        ("probsT", [P, NT + 1, P], F32), ("negc_rows", [P, SEQ + NM + NPAST + NS], F32R),
        ("fq_rows", [P, NT, P], F32), ("fq_rows_s", [NS, P], F32), ("fk_rows", [P, NT, P], F32),
        ("fk_rows_m", [NM, P], F32), ("fk_rows_s", [NS, P], F32), ("fk_rows_c", [P, NC, P], F32),
        ("fv_rows", [P, NT, P], F32), ("fv_rows_m", [NM, P], F32), ("fv_rows_s", [NS, P], F32),
        ("fv_rows_c", [P, NC, P], F32),
        ("fqT", [P, TOUT], F32), ("fkT", [P, SEQ + NM + NS], F32), ("fkcT", [P, NPAST], F32)])
    (_, mT, yraw, sTd, kd, qg, state, bns, rgT, rvrow, rvm, rvs, _, rqT, rkT, dec, s0s) = arena([
        ("stage_kept", [P, 2, TALL], F32), ("merged_T", [P, KC, TOUT], F32), ("y_raw", [P, NQ, RV], F32),
        ("scores_T", [P, 2, P], F32), ("k_decayed", [P, 2, P], F32), ("q_decayed", [P, 2, P], F32),
        ("ret_state", [P, RV], F32), ("bn_stats", [P, NQ, 8], F32), ("ret_gate_T", [P, 2, TOUT], F32),
        ("rv_rows_sb", [P, NT, RV], F32), ("rv_rows_m", [NM, RV], F32), ("rv_rows_s", [NS, RV], F32),
        ("attention_end", [P, 640], F32), ("rqT", [P, TALL], F32), ("rkT", [P, TALL], F32),
        ("decay", [P, 264], F32), ("sample_state", [P, RV], F32)])
    _, _, mtmp, _, araw = arena([
        ("stage_kept2", [P, 2, TALL], F32), ("merged_T_kept", [P, KC, TOUT], F32), ("gated", [P, 2, 352], F32),
        ("ret_gate_kept", [P, NQ * RV + 6 * P + RV + NQ * 8 + 2 * TOUT - 704], F32), ("act_raw", [P, 4, TOUT], F32)])
    hsb, xrow, hn, g2, hsq = arena([("h_sb", [P, NQ, D], F32), ("x_again", [P, 2, NQ, 256], F32),
                               ("hn_rows", [P, 2, D], F32), ("norm2_bc", [P, D], F32), ("h_squares", [P, 2, D], F32)])
    yT, uh, ul, relu, usq = arena([("y_T", [P, KC, TOUT], F32), ("u_hi", [P, 4, TOUT], F32R), ("u_lo", [P, 4, TOUT], F32R),
                                   ("relu", [P, 2, 352], F32), ("u", [P, 2, 352], F32)])
    _, hback, yout = arena([("y_T_kept", [P, KC, TOUT], F32), ("h_back", [P, 2, D], F32), ("y_rows", [P, 2, D], F32)])

    pd = ctx.enter_context(nc.psum_tensor("ps_dense", [P, NB, 512], F32))
    pt = ctx.enter_context(nc.psum_tensor("ps_turn", [P, 2, 512], F32))
    ps = ctx.enter_context(nc.psum_tensor("ps_scores", [P, 3 * 512], F32))
    po = ctx.enter_context(nc.psum_tensor("ps_out", [P, 512], F32))

    w_in_s = [sem(f"w_landed{i}") for i in range(2)]
    w_hi_s = sem("w_hi_ready")
    w_lo_s = sem("w_lo_ready")
    mm_done = sem("dense_done")
    bank_free = sem("dense_read")
    const_in = sem("const_landed")
    const_ok = sem("const_ready")
    pad_ok = sem("pad_zeroed")
    x_in = [sem(f"x_landed{i}") for i in range(NQ)]
    dch = sem("dve_chain")
    a_ssq = sem("ssq_ready")
    a_root = sem("root_ready")
    v_norm = sem("rows_normed")
    t_done = [sem("turned0"), sem("turned1")]
    t_read = [sem("turn_read0"), sem("turn_read1")]
    a_hi = sem("act_hi_ready")
    a_lo = sem("act_lo_ready")

    T3 = [(0, 358), (358, 358), (716, 356)]
    O3 = [(0, 352), (352, 352), (704, 352)]

    class At:

        def __init__(self, first, step=0, i=None):
            self.first, self.step, self.i = first, step, i

        def __add__(self, k):
            return At(self.first + k, self.step, self.i)

        def __sub__(self, k):
            return self + (-k)

        def mod(self, m):
            assert self.i is None or self.step % m == 0
            return self.first % m

        def times(self, m, plus=0):
            return At(self.first * m + plus, self.step * m, self.i).v

        def over(self, m):
            assert self.i is None or self.step % m == 0
            return At(self.first // m, self.step // m, self.i)

        @property
        def v(self):
            return self.first if self.i is None else self.i * self.step + self.first

    STRIPS = 16
    U_STRIP, N_STRIP = 1, 3
    U_TURN, N_TURN = U_STRIP + 2 * STRIPS, N_STRIP + NQ * STRIPS
    U_GB, N_GB = U_TURN + 3 * FH, N_TURN + 9 * FH
    U_FOX, N_FOX = U_GB + 8, N_GB + 24
    U_RET, N_RET = U_FOX + 8, N_FOX + 24
    U_WO, N_WO = U_RET + 8, N_RET + 24
    U_MLP, N_MLP = U_WO + 8, N_WO + 4 * NQ
    G_N = 36
    U_END = U_MLP + 64
    A_NORM1 = 2 * NQ
    A_FOX, A_RET, A_M, A_NORM2 = A_NORM1 + 8, A_NORM1 + 16, A_NORM1 + 24, A_NORM1 + 24 + 2 * NQ
    ST_STRIP = 48
    ST_TURN = ST_STRIP * STRIPS
    ST_GB = ST_TURN + 64 * FH
    ST_RET = ST_GB + 16 * 8

    def ring(u):
        return 1 + (u.first - U_TURN) % 3 if U_TURN <= u.first < U_GB else u.mod(4)

    def load_unit(sp, u, src):
        wait(sp, w_lo_s, (u - 1).v)
        k = src.shape[1]
        sp.dma_start(raw[:, u.mod(2), :].rearrange("p (k m) -> p k m", k=k), src).then_inc(w_in_s[u.mod(2)], 16)

    def split_hi(act, u, n):
        act.wait_ge(w_in_s[u.mod(2)], At(u.first // 2, u.step // 2, u.i).times(16, 16))
        wait(act, mm_done, n.v)
        nc.scalar.copy(wh[:, ring(u), :], raw[:, u.mod(2), :]).then_inc(w_hi_s, 1)

    def split_lo(dve, u):
        dve.wait_ge(w_hi_s, (u + 1).v)
        nc.vector.tensor_tensor(wl[:, ring(u), :], raw[:, u.mod(2), :], wh[:, ring(u), :],
                                ALU.subtract).then_inc(w_lo_s, 1)

    def turned_piece(pe, n, us, c, w, part, hi=xh, lo=xl, kc=KC, m0=0, parts=3):
        if part == 0:
            wait(pe, bank_free, (n - 1).v)
        width = UNIT // kc
        a, b = (x[:, us, :].rearrange("p (k m) -> p k m", m=width) for x in (wh, wl))
        each = 3 * kc // parts
        for x in range(part * each, (part + 1) * each):
            k = x // 3
            lhs, rhs = ((b, hi), (a, lo), (a, hi))[x % 3]
            mm = nc.tensor.matmul(pd[:, n.mod(NB), 0:w], lhs[:, k, m0:m0 + P], rhs[:, k, c:c + w],
                                  start=(x == 0), stop=(x == 3 * kc - 1))
        if part == parts - 1:
            mm.then_inc(mm_done, 1)

    def turned_step(pe, n, us, c, w, **kw):
        turned_piece(pe, n, us, c, w, 0, parts=1, **kw)

    def strip_step(pe, n, u, i):
        wait(pe, bank_free, (n - 1).v)
        for k in range(KC):
            us = (u + k // 4).mod(4)
            a, b = (x[:, us, 256 * (k % 4):256 * (k % 4) + 256] for x in (wh, wl))
            t = slice(i * P, i * P + P)
            for q, (lhs, rhs) in enumerate(((xh, b), (xl, a), (xh, a))):
                mm = nc.tensor.matmul(pd[:, n.mod(NB), 0:256], lhs[:, k, t], rhs,
                                      start=(k == 0 and q == 0), stop=(k == KC - 1 and q == 2))
        mm.then_inc(mm_done, 1)

    def strip_src(w, c):
        return [w[:, 4 * j:4 * j + 4, c] for j in range(2)]

    def link(dve, ins, chain):
        ins.then_inc(dch, 1)
        chain[0] = chain[0] + 1
        dve.wait_ge(dch, chain[0].v)

    def root_start(dve, src, w, inv, chain):
        link(dve, nc.vector.tensor_scalar(stat[:, 1, 0:w], src, inv, EPS, ALU.mult, ALU.add), chain)

    def root_end(dve, w, scale, chain):
        v, r, rr, e, t, o = stat[:, 1, 0:w], stat[:, 2, 0:w], stat[:, 3, 0:w], stat[:, 4, 0:w], stat[:, 6, 0:w], stat[:, 5, 0:w]
        link(dve, nc.vector.reciprocal(rr, r), chain)
        link(dve, nc.vector.tensor_tensor(e, rr, rr, ALU.mult), chain)
        link(dve, nc.vector.tensor_tensor(t, e, v, ALU.mult), chain)
        link(dve, nc.vector.tensor_scalar(e, t, -0.5, 1.5, ALU.mult, ALU.add), chain)
        link(dve, nc.vector.scalar_tensor_tensor(o, rr, scale, e, ALU.mult, ALU.mult), chain)

    def turn_rows_pe(pe, rows_ap, i, a_base, norm_base):
        pe.wait_ge(v_norm, norm_base + i + 1)
        for g in range(2):
            wait(pe, a_lo, a_base + max(2 * i + g - 1, 0))
            for c in range(4):
                mm = nc.tensor.transpose(pt[:, g, c * P:c * P + P],
                                         rows_ap[:, i % 2, (4 * g + c) * P:(4 * g + c + 1) * P], ident[:])
            mm.then_inc(t_done[g], 1)

    def act_cols(x, i, g):
        return x[:, 4 * g:4 * g + 4, i * P:i * P + P]

    def turn_rows_act(act, i, t_base):
        for g in range(2):
            act.wait_ge(t_done[g], t_base[g] + i + 1)
            nc.scalar.copy(act_cols(xh, i, g), pt[:, g, :].rearrange("p (c t) -> p c t", c=4)).then_inc(a_hi, 1)

    def turn_rows_dve(dve, i, h_base, l_base=None):
        for g in range(2):
            dve.wait_ge(a_hi, h_base + 2 * i + g + 1)
            nc.vector.tensor_tensor(act_cols(xl, i, g), pt[:, g, :].rearrange("p (c t) -> p c t", c=4),
                                    act_cols(xh, i, g), ALU.subtract).then_inc(a_lo, 1)

    def att_groups():
        out = []
        for q in range(6):
            out.append((-1, q, len(out) % 2))
        for j in range(NT):
            blocks = list(range(j + 1)) + [NT]
            for b in range(0, len(blocks), 4):
                out.append((j, blocks[b:b + 4], len(out) % 2))
        out.append((NT, list(range(NC + 1)), len(out) % 2))
        return out

    GROUPS = att_groups()
    PER_BANK = [sum(g[2] == b for g in GROUPS) for b in range(2)]
    T_ATT = [NQ + 1, NQ + 1]
    T_NORM2 = [T_ATT[b] + FH * PER_BANK[b] for b in range(2)]
    T_FIN = [T_NORM2[b] + NQ for b in range(2)]

    def nth(g):
        return sum(x[2] == GROUPS[g][2] for x in GROUPS[:g])

    def step_groups(j):
        return [g for g in range(len(GROUPS)) if GROUPS[g][0] == j]

    NKEY = SEQ + NM

    def turn_prologue(q):
        if q < 2:
            return [(qrow[:, 4 * q + x, :], x * P, P) for x in range(4)], [(qT[:, 512 * q:512 * q + 512], 0, 512)]
        if q < 4:
            z = q - 2
            return ([(krow[:, 4 * z + x, :], x * P, P) for x in range(4)],
                    [(kT[:, NM + 512 * z:NM + 512 * z + 512], 0, 512)])
        if q == 4:
            return ([(kcrow[:, 0, :], 0, P), (qsrow[:], P, NS), (kmrow[:], P + 32, NM), (ksrow[:], P + 64, NS)],
                    [(kcT[:, 0:P], 0, P), (qT[:, SEQ:TOUT], P, NS), (kT[:, 0:NM], P + 32, NM),
                     (kT[:, NKEY:NKEY + NS], P + 64, NS)])
        return [(kcrow[:, x + 1, :], x * P, P) for x in range(3)], [(kcT[:, P:], 0, 3 * P)]

    def prob_block(j, b):
        if j == NT:
            return b * P, (P if b < NC else NS)
        return (0, NM) if b == NT else (NM + b * P, P)

    def read_group(eng_copy, g):
        j, blocks, bank = GROUPS[g]
        if j < 0:
            for dst, c, w in turn_prologue(blocks)[1]:
                last = eng_copy(dst, pt[:, bank, c:c + w])
            return last
        if j == NT:
            eng_copy(pT[:, 0, 0:NS], pt[:, bank, 0:NS])
            eng_copy(pT[:, 1:NC, 0:NS], pt[:, bank, P:P + 3 * NS].rearrange("p (b w) -> p b w", b=3))
            return eng_copy(pT[0:NS, NC, 0:NS], pt[0:NS, bank, P + 3 * NS:P + 4 * NS])
        width = P
        full = [b for b in blocks if prob_block(j, b)[1] == P]
        if full:
            n = len(full)
            last = eng_copy(pT[:, full[0]:full[0] + n, 0:width],
                            pt[:, bank, 0:n * width].rearrange("p (b w) -> p b w", b=n))
        for x, b in enumerate(blocks):
            k = prob_block(j, b)[1]
            if k != P:
                last = eng_copy(pT[0:k, b, 0:width], pt[0:k, bank, x * width:x * width + width])
        return last

    ATT = FH * 9
    E0, O0 = 1, 1

    CH = [(TOUT, NM)] + [(i * P, P) for i in range(NT)] + [(SEQ, NS)]
    NCH = len(CH)
    D_GQ, D_COL = P, 2 * P
    C_KP, C_KM, C_KS, C_GP, C_GS = range(5)

    RT_GROUPS = [(e, [(e, 4 * z + x, P) for x in range(4)]) for e in range(2) for z in range(2)]
    RT_GROUPS.append((None, [(0, NT, P), (1, NT, P)]))
    CH_ROOT1 = 2

    small_in = sem("small_landed"); ssq_v = sem("strip_mean_square"); ncr_zero = sem("negc_rows_zero")
    yz_ok = sem("ret_pad_set"); hz_ok = sem("h_pad_zero"); ld_g = sem("gain_landed"); y_rd = sem("y_turn_read")
    strip_ok = sem("strip_ready")
    ssq2 = sem("strip_ssq")
    unit_v = sem("rotated_ready")
    g_ok = sem("gate_open")
    stored = sem("stored")
    lf_raw = sem("logf_raw"); lf_e = sem("logf_exp"); lf_ok = sem("logf_ready"); lf_c = sem("cache_logf_landed")
    lf_T = sem("logf_turned"); lf_r = sem("logf_rows_ready"); nc_ok = sem("negc_ready"); lf_st = sem("logf_stored")
    ld_qk = sem("qk_landed"); ld_v = sem("v_landed"); ld_n = sem("negc_landed")
    s_done = sem("scores_done"); m_done = sem("max_done"); e_done = sem("exp_done"); p_done = sem("probs_ready")
    o_done = sem("out_done"); o_read = sem("out_read"); f_done = sem("fox_head_ready")
    ld_r = sem("ret_qk_landed"); ld_rv = sem("ret_v_landed"); ld_s = sem("ret_gate_landed")
    r_a = sem("ret_scores_done"); r_ad = sem("ret_scores_read"); r_b = sem("ret_out_done"); r_bd = sem("ret_out_read")
    r_t = sem("ret_turned"); r_tr = sem("ret_turn_read"); r_n = sem("ret_normed"); r_ok = sem("ret_head_ready")
    r_v = sem("ret_var_ready"); r_g = sem("ret_gate_open"); r_sto = sem("ret_stored")
    ar_in = [sem(f"act_landed{i}") for i in range(4)]; f_in = sem("fox_landed")
    g_in = [sem("gate_landed0"), sem("gate_landed1")]
    m_ok = sem("merged_ready"); x2_in = [sem("x_again0"), sem("x_again1")]; g2_in = sem("norm2_landed")
    h_ok = sem("h_ready"); h_st = sem("h_stored"); hb_in = [sem("h_back0"), sem("h_back1")]
    u_relu = sem("relu_ready"); u_sq = sem("u_ready"); u_hi = sem("u_hi_ready"); u_lo = sem("u_lo_ready")
    y_acc = sem("y_accumulated"); y_ok = sem("y_rows_ready"); y_st = [sem("y_stored0"), sem("y_stored1")]

    block = ctx.enter_context(nc.Block())

    @block.sync
    def _(sp):
        sp.dma_start(ident[:], c_ident).then_inc(const_in, 16)
        sp.dma_start(maskf[:], c_mask).then_inc(const_in, 16)
        sp.dma_start(g1[:], norm1_g[0].partition_broadcast(P)).then_inc(const_in, 16)
        for i in range(NT):
            sp.dma_start(xt[:, i, :], xp[i * P:(i + 1) * P, :]).then_inc(x_in[i], 16)
        sp.wait_ge(pad_ok, 1)
        sp.dma_start(xt[0:NS, NT, :], xs).then_inc(x_in[NT], 16)
        sp.dma_start(xt[NS:NS + NM, NT, :], meta).then_inc(x_in[NT], 16)
        load_unit(sp, At(0), win[:, :, W_FF:W_FF + P])
        sp.dma_start(bfT[:], b_forget.rearrange("a h -> h a")).then_inc(small_in, 16)
        cols = [W_FQ, W_FK, W_FV, W_RV]

        def strip_units(u, c):
            for j in range(2):
                load_unit(sp, u + j, win[:, 4 * j:4 * j + 4, c])

        for s in range(2):
            strip_units(At(U_STRIP + 2 * s), slice(W_FQ + 256 * s, W_FQ + 256 * s + 256))
            if s == 0:
                sp.wait_ge(a_lo, A_NORM1)
                for dst, src in ((cosT[:], c_cos), (sinT[:], c_sin), (gq[:], q_norm_g[0].partition_broadcast(P)),
                                 (gk[:], k_norm_g[0].partition_broadcast(P)),
                                 (crow[:], clf.rearrange("(c p) h -> p c h", p=P))):
                    sp.dma_start(dst, src).then_inc(small_in, 16)
        for s in range(2, 4):
            strip_units(At(U_STRIP + 2 * s), slice(W_FQ + 256 * s, W_FQ + 256 * s + 256))
        for kind in range(1, 4):
            with sp.Fori(0, 2) as i:
                for s in range(2):
                    strip_units(At(U_STRIP + 8 * kind + 2 * s, 4, i), bass.ds(i * 512 + (cols[kind] + 256 * s), 256))
        def load_qk(h):
            hc = bass.ds(h.times(P), P)
            for dst, src in ((qrow[:], pq[NM:, hc].rearrange("(i p) d -> p i d", p=P)), (qsrow[:], sq[:, hc]),
                             (krow[:], pk[NM:, hc].rearrange("(i p) d -> p i d", p=P)), (kmrow[:], pk[0:NM, hc]),
                             (ksrow[:], sk[:, hc]), (kcrow[:], ck[:, hc].rearrange("(i p) d -> p i d", p=P))):
                sp.dma_start(dst, src).then_inc(ld_qk, 16)

        def load_v(h):
            hc = bass.ds(h.times(P), P)
            for dst, src in ((vrow[:], pv[NM:, hc].rearrange("(i p) d -> p i d", p=P)), (vmrow[:], pv[0:NM, hc]),
                             (vsrow[:], sv[:, hc]), (vcrow[:], cv[:, hc].rearrange("(i p) d -> p i d", p=P))):
                sp.dma_start(dst, src).then_inc(ld_v, 16)
            row = negc[:, bass.ds(h.v, 1), :].rearrange("a b n -> a (b n)")
            sp.dma_start(ncr[0:2, :].bitcast(F32), row.bitcast(F32)).then_inc(ld_n, 16)

        def turn_unit(h, q):
            load_unit(sp, At(U_TURN + 3 * h.first + q, 3 * h.step, h.i),
                      win[:, :, bass.ds(h.times(P, (W_RQ, W_RG, W_GA)[q]), P)])

        sp.wait_ge(stored, 8 * ST_STRIP)
        sp.wait_ge(lf_st, 64)
        load_qk(At(0))
        turn_unit(At(0), 0)
        turn_unit(At(0), 1)
        sp.wait_ge(stored, 12 * ST_STRIP)
        sp.wait_ge(ncr_zero, 1)
        load_v(At(0))
        turn_unit(At(0), 2)

        def next_head(h):
            turn_unit(h + 1, 0)
            turn_unit(h + 1, 1)
            sp.wait_ge(s_done, h.times(9, 1))
            load_qk(h + 1)
            turn_unit(h + 1, 2)
            sp.wait_ge(o_done, h.times(9, 9))
            load_v(h + 1)

        with sp.Fori(0, FH // 2 - 1) as i:
            for b in range(2):
                next_head(At(b, 2, i))
        next_head(At(FH - 2))
        def branch_unit(x):
            w, q = ((win, x), (wfo, x - 8), (wro, x - 16))[x // 8]
            c = q * P + (W_GB if w is win else 0)
            load_unit(sp, At(U_GB + x), w[:, :, c:c + P])

        def load_gate(x, kind):
            sp.wait_ge(bank_free, N_FOX + 3 * (x - 1))
            sp.dma_start(stage[:, x % 2, 0:TOUT], gates[3 * (x % 8) + kind]).then_inc(g_in[x % 2], 16)

        def load_ret_qk(r):
            for dst, src in ((rqT[:], rot[r]), (rkT[:], rot[RH + r]), (dec[:], c_decay[r])):
                sp.dma_start(dst, src).then_inc(ld_r, 16)

        def load_ret_v(r):
            c = slice(r * RV, r * RV + RV)
            for dst, src in ((rvrow[:], prv[NM:, c].rearrange("(i p) d -> p i d", p=P)), (rvm[:], prv[0:NM, c]),
                             (rvs[:], srv[:, c])):
                sp.dma_start(dst, src).then_inc(ld_rv, 16)

        def load_ret_gate(r):
            for dst, src in ((s0s[:], st_in[r]), (rgT[:, 0, :], gates[6 * r]), (rgT[:, 1, :], gates[6 * r + 3])):
                sp.dma_start(dst, src).then_inc(ld_s, 16)

        for x in range(2):
            branch_unit(x)
        sp.wait_ge(stored, ST_TURN + 64 * 7)
        load_ret_qk(0)
        sp.dma_start(gnT[:], ret_gn_g.rearrange("a (k p) -> p (a k)", p=P), allow_slow_non_contiguous=True).then_inc(ld_g, 16)
        branch_unit(2)
        sp.wait_ge(stored, ST_GB)
        load_ret_v(0)
        load_ret_gate(0)
        for k in range(KC):
            sp.dma_start(mT[:, k, :], foxT[k]).then_inc(f_in, 16)
        for r in range(RH):
            fox = r >= 2
            x = 4 * r
            branch_unit(x + 3)
            if fox:
                load_gate(x - 7, 2)
            branch_unit(x + 4)
            if fox:
                load_gate(x - 6, 2)
            branch_unit(x + 5)
            if fox:
                load_gate(x - 5, 2)
            sp.wait_ge(r_bd, NCH * (r + 1))
            if r + 1 < RH:
                load_ret_qk(r + 1)
                load_ret_v(r + 1)
            else:
                for k in range(4):
                    sp.dma_start(araw[:, k, :], retT[k]).then_inc(ar_in[k], 16)
            branch_unit(x + 6)
            if r == 1:
                sp.wait_ge(stored, ST_RET)
            if fox or r == 1:
                load_gate(x - 4, 2 if r < 3 else 1)
            sp.wait_ge(r_sto, 64 * (r + 1))
            if r + 1 < RH:
                load_ret_gate(r + 1)
        load_gate(9, 1)
        for k in range(4, KC):
            sp.wait_ge(a_lo, A_FOX + k - 3)
            sp.dma_start(araw[:, k % 4, :], retT[k]).then_inc(ar_in[k % 4], 16)
        for q in range(5):
            branch_unit(19 + q)
            load_gate(10 + q, 1)
        load_gate(15, 1)
        for j in range(2):
            load_unit(sp, At(U_WO + j), wout[:, 4 * j:4 * j + 4, 0:256])

        sp.wait_ge(a_lo, A_M)
        sp.wait_ge(hz_ok, 1)
        sp.dma_start(g2[:], norm2_g[0].partition_broadcast(P)).then_inc(g2_in, 16)
        for s in range(4):
            c = slice(256 * s, 256 * s + 256)
            if s >= 2:
                sp.wait_ge(bank_free, N_WO + NQ * (s - 1))
            sp.dma_start(xrow[:, s % 2, 0:NT, :], xp[:, c].rearrange("(i p) d -> p i d", p=P)).then_inc(x2_in[s % 2], 16)
            sp.dma_start(xrow[0:NS, s % 2, NT, :], xs[:, c]).then_inc(x2_in[s % 2], 16)
            for j in range(2 if s else 0):
                load_unit(sp, At(U_WO + 2 * s + j), wout[:, 4 * j:4 * j + 4, c])

        with sp.Fori(0, 8) as g:
            for q in range(4):
                load_unit(sp, At(U_MLP + q, 8, g), wf1[:, :, bass.ds(g * 512 + q * P, P)])
            for q in range(4):
                load_unit(sp, At(U_MLP + 4 + q, 8, g), wf2[:, bass.ds(g * 4, 4), 256 * q:256 * q + 256])

        sp.wait_ge(h_st, 32)
        sp.wait_ge(bank_free, N_MLP + 8 * G_N)

        def hload(i):
            n = P if i < NT else NS
            sp.dma_start(hback[0:n, i % 2, :], hrow[i * P:i * P + n, :]).then_inc(hb_in[i % 2], 16)

        hload(0)
        hload(1)
        for i in range(NQ):
            sp.wait_ge(y_rd, 2 * i + 2)
            n = P if i < NT else NS
            sp.dma_start(yp[i * P:i * P + P, :] if i < NT else ys, yout[0:n, i % 2, :]).then_inc(y_st[i % 2], 16)
            if i + 2 < NQ:
                hload(i + 2)
        sp.wait_ge(y_st[0], 16 * 5)
        sp.wait_ge(y_st[1], 16 * 4)
        sp.wait_ge(lf_st, 64)
        sp.wait_ge(stored, ST_RET)
        sp.wait_ge(r_sto, RH * 64)

    @block.gpsimd
    def _(pool):
        nc.gpsimd.memset(xt[:, NT, :], 0.0).then_inc(pad_ok, 1)

        def store_strip(s, prompt, sample, c, normed, n=None):
            if normed:
                pool.wait_ge(strip_ok, (s + 1).v)
            else:
                pool.wait_ge(bank_free, (n + NQ).v)
            src = rows[:, s.mod(2)]
            pool.dma_start(prompt[NM:, c].rearrange("(i p) d -> p i d", p=P), src[:, 0:NT, :]).then_inc(stored, 16)
            pool.dma_start(sample[:, c], src[0:NS, NT, :]).then_inc(stored, 16)
            pool.dma_start(prompt[0:NM, c], src[NS:NS + NM, NT, :]).then_inc(stored, 16)
            pool.wait_ge(stored, s.times(ST_STRIP, ST_STRIP))

        def store_logf():
            pool.wait_ge(nc_ok, 1)
            pool.dma_start(negc.rearrange("a h n -> h a n").bitcast(F32), nchl[:].bitcast(F32)).then_inc(lf_st, 16)
            pool.wait_ge(lf_r, 1)
            pool.dma_start(plf[NM:, :].rearrange("(i p) h -> p i h", p=P), lfr[:, 0:NT, :]).then_inc(lf_st, 16)
            pool.dma_start(slf, lfr[0:NS, NT, :]).then_inc(lf_st, 16)
            pool.dma_start(plf[0:NM, :], lfr[NS:NS + NM, NT, :]).then_inc(lf_st, 16)
            pool.wait_ge(lf_st, 64)

        store_logf()
        for s in range(4):
            store_strip(At(s), pq, sq, slice(256 * s, 256 * s + 256), True)
        for kind, (p_rows, s_rows) in ((1, (pk, sk)), (2, (pv, sv)), (3, (prv, srv))):
            with pool.Fori(0, 2) as i:
                for s in range(2):
                    store_strip(At(4 * kind + s, 2, i), p_rows, s_rows, bass.ds(i * 512 + 256 * s, 256), kind == 1,
                                At(N_STRIP + NQ * (4 * kind + s), 2 * NQ, i))
            if kind == 1:
                nc.gpsimd.memset(ncr[:].bitcast(F32), 0.0).then_inc(ncr_zero, 1)
        def row_of(x, h, m=1, k=0):
            return x[bass.ds(h.times(m, k), 1)].rearrange("a p n -> (a p) n")

        with pool.Fori(0, FH // 2) as i:
            for b in range(2):
                h = At(b, 2, i)
                pool.wait_ge(unit_v, h.times(1, 1))
                pool.dma_start(row_of(rot, h), stage[:, b, :]).then_inc(stored, 16)
                pool.wait_ge(stored, h.times(64, ST_TURN + 16))
                pool.wait_ge(bank_free, h.times(9, N_TURN + 6))
                pool.dma_start(row_of(gates, h, 3, 0), stage[:, 1 - b, 0:TOUT]).then_inc(stored, 16)
                pool.wait_ge(stored, h.times(64, ST_TURN + 32))
                pool.wait_ge(o_read, h.times(9, O0 + 9))
                pool.dma_start(row_of(foxT, h), fst[:]).then_inc(stored, 16)
                pool.wait_ge(stored, h.times(64, ST_TURN + 48))
                pool.wait_ge(bank_free, h.times(9, N_TURN + 9))
                pool.dma_start(row_of(gates, h, 3, 1), stage[:, b, 0:TOUT]).then_inc(stored, 16)
                pool.wait_ge(stored, h.times(64, ST_TURN + 64))
        nc.gpsimd.memset(yraw[:, NT, :], 0.0)
        nc.gpsimd.memset(bns[:, NT, :], 1.0).then_inc(yz_ok, 1)

        def ret_head(r, gb):
            def store_gb(q):
                pool.wait_ge(bank_free, r.times(12, N_GB + 3 * q + 3))
                pool.dma_start(row_of(gates, r, 12, 3 * q + 2), stage[:, q % 2, 0:TOUT]).then_inc(stored, 16)
                pool.wait_ge(stored, r.times(64, ST_GB + 16 * q + 16))

            if gb:
                store_gb(0)
                store_gb(1)
            pool.wait_ge(r_bd, r.times(NCH, NCH))
            pool.dma_start(row_of(pst, r), state[:]).then_inc(r_sto, 16)
            pool.dma_start(row_of(sst, r), s0s[:]).then_inc(r_sto, 16)
            pool.wait_ge(r_sto, r.times(64, 32))
            if gb:
                store_gb(2)
            pool.wait_ge(r_tr, r.times(5, 5))
            for e in range(2):
                pool.dma_start(row_of(retT, r, 2, e), rgT[:, e, :]).then_inc(r_sto, 16)
            pool.wait_ge(r_sto, r.times(64, 64))
            if gb:
                store_gb(3)

        for half in range(2):
            with pool.Fori(0, 2) as i:
                ret_head(At(2 * half, 1, i), half == 0)
        pool.wait_ge(a_lo, A_M)
        nc.gpsimd.memset(hsb[:, NT, :], 0.0).then_inc(hz_ok, 1)
        pool.wait_ge(bank_free, N_MLP)
        pool.dma_start(hrow[0:SEQ, :].rearrange("(i p) d -> p i d", p=P), hsb[:, 0:NT, :]).then_inc(h_st, 16)
        pool.dma_start(hrow[SEQ:, :], hsb[0:NS, NT, :]).then_inc(h_st, 16)
        pool.wait_ge(h_st, 32)

    @block.tensor
    def _(pe):
        pe.wait_ge(const_in, 48)
        for i in range(NQ):
            turn_rows_pe(pe, xn, i, 0, 0)
        pe.wait_ge(a_lo, A_NORM1)
        pe.wait_ge(w_lo_s, 1)
        for j, (c, w) in enumerate(T3):
            turned_step(pe, At(j), 0, c, w)

        def strip(u, n):
            pe.wait_ge(w_lo_s, (u + 2).v)
            for i in range(NQ):
                strip_step(pe, n + i, u, i)

        def logf_turns():
            pe.wait_ge(small_in, 96)
            for c in range(NC):
                mm = nc.tensor.transpose(pt[0:FH, 0, c * P:c * P + P], crow[:, c, :], ident[:])
            mm.then_inc(t_done[0], 1)
            pe.wait_ge(lf_ok, 1)
            for i in range(NQ):
                w = P if i < NT else NS + NM
                mm = nc.tensor.transpose(pt[0:w, 1, FH * i:FH * i + FH], lf[:, i * P:i * P + w], ident[0:FH, 0:FH])
            mm.then_inc(t_done[1], 1)

        for s in range(4):
            strip(At(U_STRIP + 2 * s), At(N_STRIP + NQ * s))
            if s == 0:
                logf_turns()
        for kind in range(1, 4):
            with pe.Fori(0, 2) as i:
                for s in range(2):
                    strip(At(U_STRIP + 8 * kind + 2 * s, 4, i), At(N_STRIP + NQ * (4 * kind + s), 2 * NQ, i))
        T_READ0 = (1, 1)

        def tgroup(h, g):
            j, blocks, bank = GROUPS[g]
            pe.wait_ge(t_read[bank], h.times(PER_BANK[bank], T_READ0[bank] + nth(g)))
            if j < 0:
                for src, c, n in turn_prologue(blocks)[0]:
                    mm = nc.tensor.transpose(pt[:, bank, c:c + n], src, ident[0:n, 0:n])
            else:
                for x, b in enumerate(blocks):
                    c, k = prob_block(j, b)
                    m, o = (NS, P + (x - 1) * NS) if j == NT and x else (P, x * P)
                    mm = nc.tensor.transpose(pt[0:k, bank, o:o + m], prob[0:m, j % 2, c:c + k], ident[0:m, 0:m])
            mm.then_inc(t_done[bank], 1)

        def turned_before(h, g):
            for b in range(2):
                pe.wait_ge(t_read[b], h.times(PER_BANK[b], T_READ0[b] + sum(x[2] == b for x in GROUPS[:g])))

        def scores(h, j):
            pe.wait_ge(e_done, h.times(9, E0 + j))
            if j == 0:
                turned_before(h, 6)
                pe.wait_ge(ld_n, h.times(16, 16))
            if j < NT:
                n = NM + P * (j + 1)
                for a in range(0, n, 512):
                    b = min(n, a + 512)
                    d0 = max(a, n - P)
                    nc.tensor.matmul(ps[:, a:b], qT[:, j * P:j * P + P], kT[:, a:b], start=True, stop=False)
                    mm = nc.tensor.matmul(ps[:, a:b], onesr[:], ncr[:, a:b], start=False, stop=(d0 >= b))
                    if d0 < b:
                        mm = nc.tensor.matmul(ps[:, d0:b], identr[:], maskr[:, d0 - n + P:b - n + P], start=False, stop=True)
            else:
                q, o1 = qT[:, SEQ:TOUT], onesr[:, 0:NS].bitcast(F32)
                nr = ncr[:].bitcast(F32)
                nc.tensor.matmul(ps[0:NS, 0:512], q, kcT[:], start=True, stop=False)
                nc.tensor.matmul(ps[0:NS, 0:512], o1, nr[:, NKEY:NKEY + NPAST], start=False, stop=True)
                nc.tensor.matmul(ps[0:NS, 512:512 + NS], q, kT[:, NKEY:NKEY + NS], start=True, stop=False)
                nc.tensor.matmul(ps[0:NS, 512:512 + NS], o1, nr[:, NKEY + NPAST:], start=False, stop=False)
                mm = nc.tensor.matmul(ps[0:NS, 512:512 + NS], ident[:, 0:NS], maskr[:, 0:NS].bitcast(F32), start=False, stop=True)
            mm.then_inc(s_done, 1)

        def turn_probs(h, j):
            pe.wait_ge(p_done, h.times(9, j + 1))
            for g in step_groups(j)[:2]:
                tgroup(h, g)

        def weigh(h, j):
            gs = step_groups(j)
            for g in gs[2:]:
                tgroup(h, g)
            early = [b for g in gs[:2] for b in GROUPS[g][1]]
            turned_before(h, gs[:2][-1] + 1)
            if j == 0:
                pe.wait_ge(ld_v, h.times(64, 64))
            pe.wait_ge(o_read, h.times(9, O0 + j))
            w = NS if j == NT else P
            if j == NT:
                parts = [(b, vcrow[:, b, :], pT[:, b, 0:w]) for b in range(NC)] + [(NC, vsrow[:], pT[0:NS, NC, 0:w])]
            else:
                parts = [(b, vrow[:, b, :], pT[:, b, 0:w]) for b in range(j + 1)] + [(NT, vmrow[:], pT[0:NM, NT, 0:w])]
            for x, (b, v, p) in enumerate(parts):
                if b not in early and parts[x - 1][0] in early:
                    turned_before(h, gs[-1] + 1)
                mm = nc.tensor.matmul(po[:, 0:w], v, p, start=(x == 0), stop=(x == len(parts) - 1))
            mm.then_inc(o_done, 1)

        def piece(h, p):
            x, j = p // 9, p // 3 % 3
            c, w = (T3 if x == 0 else O3)[j]
            u = At(U_TURN + 3 * h.first + x, 3 * h.step, h.i)
            if p % 9 == 0:
                pe.wait_ge(w_lo_s, (u + 1).v)
            turned_piece(pe, At(N_TURN + 9 * h.first + p // 3, 9 * h.step, h.i), ring(u), c, w, p % 3)

        with pe.Fori(0, FH // 2) as i:
            for b in range(2):
                h = At(b, 2, i)
                pe.wait_ge(ld_qk, h.times(96, 96))
                for g in range(6):
                    tgroup(h, g)
                    piece(h, g)
                scores(h, 0)
                for p in range(6, 9):
                    piece(h, p)
                for j in range(1, 9):
                    scores(h, j)
                    piece(h, 7 + 2 * j)
                    turn_probs(h, j - 1)
                    piece(h, 8 + 2 * j)
                    weigh(h, j - 1)
                piece(h, 25)
                turn_probs(h, 8)
                piece(h, 26)
                weigh(h, 8)
        def ret_a(r, c):
            c0, m = CH[c]
            if c:
                pe.wait_ge(r_ad, r.times(NCH, c))
                nc.tensor.matmul(ps[0:m, 0:m], rkT[:, c0:c0 + m], rqT[:, c0:c0 + m], start=True, stop=True)
            nc.tensor.transpose(pt[0:m, 0, 0:P], rkT[:, c0:c0 + m], ident[:]).then_inc(r_a, 1)

        def ret_b(r, c):
            c0, m = CH[c]
            pe.wait_ge(r_ad, r.times(NCH, c + 1))
            if c:
                pe.wait_ge(r_bd, r.times(NCH, c))
            v = rvm[:] if c == 0 else (rvs[:] if c == NCH - 1 else rvrow[:, c - 1, :])
            mm = nc.tensor.matmul(ps[:, 1024:1024 + RV], kd[0:m, c % 2, :], v, start=True, stop=True)
            if c == 0:
                mm.then_inc(r_b, 1)
            else:
                st = s0s if c == NCH - 1 else state
                nc.tensor.matmul(ps[0:m, 512:512 + RV], sTd[0:m, c % 2, 0:m], v, start=True, stop=False)
                nc.tensor.matmul(ps[0:m, 512:512 + RV], qg[:, c % 2, 0:m], st[:], start=False, stop=True).then_inc(r_b, 1)

        def ret_piece(r, p):
            x, (c, w) = p // 9, O3[p // 3 % 3]
            if p % 9 == 0:
                pe.wait_ge(w_lo_s, r.times(4, U_GB + x + 1))
            turned_piece(pe, At(N_GB + 12 * r.first + p // 3, 12 * r.step, r.i), (U_GB + x) % 4, c, w, p % 3)

        def ret_head(r):
            pe.wait_ge(ld_r, r.times(48, 48))
            ret_a(r, 0)
            ret_piece(r, 0)
            for c in range(1, NCH):
                ret_a(r, c)
                ret_piece(r, 2 * c - 1)
                if c == 1:
                    pe.wait_ge(ld_rv, r.times(48, 48))
                ret_b(r, c - 1)
                ret_piece(r, 2 * c)
            pe.wait_ge(ld_s, r.times(48, 48))
            ret_b(r, NCH - 1)
            for p in range(19, 27):
                ret_piece(r, p)
            pe.wait_ge(r_n, r.times(1, 1))
            for q, (e, tiles) in enumerate(RT_GROUPS):
                if q >= 2:
                    pe.wait_ge(r_tr, r.times(5, q - 1))
                for x, (ee, i, w) in enumerate(tiles):
                    mm = nc.tensor.transpose(pt[:, q % 2, P * x:P * x + w], yraw[0:w, i, ee * P:ee * P + P], ident[0:w, 0:w])
                mm.then_inc(r_t, 1)
                ret_piece(r, 27 + q)
            for p in range(32, 36):
                ret_piece(r, p)
            pe.wait_ge(r_tr, r.times(5, 5))

        for half in range(2):
            if half:
                pe.wait_ge(a_lo, A_FOX)
            with pe.Fori(0, 2) as i:
                ret_head(At(2 * half, 1, i))

        pe.wait_ge(a_lo, A_RET)
        with pe.Fori(0, 2) as i:
            for q in range(4):
                pe.wait_ge(w_lo_s, At(U_RET + q + 1, 4, i).v)
                for j, (c, w) in enumerate(O3):
                    turned_step(pe, At(N_RET + 3 * q + j, 12, i), (U_RET + q) % 4, c, w)
        pe.wait_ge(a_lo, A_M)
        for s in range(4):
            strip(At(U_WO + 2 * s), At(N_WO + NQ * s))
        for i in range(NQ):
            turn_rows_pe(pe, hn, i, A_M, NQ)
        pe.wait_ge(a_lo, A_NORM2)

        with pe.Fori(0, 8) as g:
            for q in range(4):
                pe.wait_ge(w_lo_s, At(U_MLP + q + 1, 8, g).v)
                for j, (c, w) in enumerate(O3):
                    turned_step(pe, At(N_MLP + 3 * q + j, G_N, g), (U_MLP + q) % 4, c, w)
            for q in range(4):
                pe.wait_ge(w_lo_s, At(U_MLP + 5 + q, 8, g).v)
                if q == 0:
                    pe.wait_ge(u_lo, At(12, 12, g).v)
                for m in range(2):
                    for j, (c, w) in enumerate(O3):
                        turned_step(pe, At(N_MLP + 12 + 6 * q + 3 * m + j, G_N, g), (U_MLP + q) % 4, c, w,
                                    hi=uh, lo=ul, kc=4, m0=m * P)
        pe.wait_ge(bank_free, N_MLP + 8 * G_N)
        for i in range(NQ):
            w = P if i < NT else NS
            for g in range(2):
                if i:
                    pe.wait_ge(y_rd, 2 * i + g - 1)
                for c in range(4):
                    mm = nc.tensor.transpose(pt[0:w, g, c * P:c * P + P], yT[:, 4 * g + c, i * P:i * P + w], ident[:])
                mm.then_inc(t_done[g], 1)

    @block.scalar
    def _(act):
        for i in range(NQ):
            act.wait_ge(x_in[i], 16 if i < NT else 32)
            wait(act, a_ssq, i - 1)
            nc.scalar.activation(xsq[:, i % 2, :], xt[:, i, :], ACT.Square, accum_out=stat[:, 0, i:i + 1]).then_inc(a_ssq, 1)
        act.wait_ge(dch, CH_ROOT1)
        nc.scalar.activation(stat[:, 2, 0:NQ], stat[:, 1, 0:NQ], ACT.Sqrt).then_inc(a_root, 1)
        for i in range(NQ):
            turn_rows_act(act, i, (0, 0))
        split_hi(act, At(0), At(0))
        split_hi(act, At(1), At(0))
        split_hi(act, At(2), At(0))
        act.wait_ge(lf_raw, 1)
        nc.scalar.activation(lfc[:, 0, :], lfc[:, 1, :], ACT.Exp, scale=-1.0).then_inc(e_done, 1)
        act.wait_ge(e_done, 1)
        nc.scalar.activation(lfc[:, 1, :], lfc[:, 0, :], ACT.Ln, bias=1.0).then_inc(lf_e, 1)

        def logf_rows():
            act.wait_ge(t_done[1], NQ + 1)
            nc.scalar.copy(lfr[:, 0:NT, :], pt[:, 1, 0:NT * FH].rearrange("p (i h) -> p i h", h=FH)).then_inc(t_read[1], 1)
            nc.scalar.copy(lfr[0:NS + NM, NT, :], pt[0:NS + NM, 1, NT * FH:NQ * FH]).then_inc(lf_r, 1)

        def strip(s, root, squares):
            u, n = At(U_STRIP + 2 * s.first, 2 * s.step, s.i), At(N_STRIP + NQ * s.first, NQ * s.step, s.i)
            for j in range(2):
                split_hi(act, u + 2 + j, n)
            if root:
                act.wait_ge(ssq_v, s.v)
                nc.scalar.activation(stat[:, 2, :], stat[:, 1, :], ACT.Sqrt).then_inc(a_root, 1)
            if squares:
                for i in range(NQ):
                    act.wait_ge(bank_free, (n + i + 1).v)
                    for e in range(2):
                        ins = nc.scalar.activation(junk[:, 2 * i + e, :], rows[:, s.mod(2), i, e * P:e * P + P], ACT.Square,
                                                   accum_out=stat[:, 0, 2 * i + e:2 * i + e + 1])
                ins.then_inc(ssq2, 1)

        strip(At(0), False, True)
        logf_rows()
        with act.Fori(0, 3) as i:
            for s in range(2):
                strip(At(1 + s, 2, i), True, True)
        strip(At(7), True, True)
        strip(At(8), True, False)
        strip(At(9), False, False)
        with act.Fori(0, 3) as i:
            for s in range(2):
                strip(At(10 + s, 2, i), False, False)

        def exps(h, j):
            act.wait_ge(m_done, h.times(9, j + 1))
            m, n = (P, NM + P * (j + 1)) if j < NT else (NS, NPAST + NS)
            nc.scalar.activation(prob[0:m, j % 2, 0:n], ps[0:m, 0:n], ACT.Exp, bias=mx[0:m, j % 2:j % 2 + 1],
                                 accum_out=lsum[0:m, j % 2:j % 2 + 1]).then_inc(e_done, 1)

        def reads(h, gs):
            for g in gs:
                if GROUPS[g][2] == 1:
                    act.wait_ge(t_done[1], h.times(PER_BANK[1], T_ATT[1] + nth(g) + 1))
                    read_group(lambda o, i_: nc.scalar.copy(o, i_), g).then_inc(t_read[1], 1)

        def turn_split(h, x):
            split_hi(act, At(U_TURN + 3 * h.first + x, 3 * h.step, h.i),
                     At(N_TURN + 9 * h.first + 3 * x - 6, 9 * h.step, h.i))

        with act.Fori(0, FH // 2) as i:
            for b in range(2):
                h = At(b, 2, i)
                reads(h, range(6))
                exps(h, 0)
                for j in range(1, 9):
                    exps(h, j)
                    reads(h, step_groups(j - 1))
                    if j in (1, 3, 5):
                        turn_split(h, {1: 2, 3: 3, 5: 4}[j])
                reads(h, step_groups(8))
        def open_gate(x, i=None, step=0):
            act.wait_ge(g_in[x % 2], At(16 * (x // 2 + 1), 8 * step, i).v)
            nc.scalar.activation(stage[:, x % 2, 0:TOUT], stage[:, x % 2, 0:TOUT], ACT.Sigmoid).then_inc(g_ok, 1)

        def ret_head(r, fox):
            def split(x):
                split_hi(act, At(U_GB + 4 * r.first + x, 4, r.i), At(N_GB + 12 * r.first + 3 * x - 6, 12, r.i))

            if fox:
                open_gate(0, r.i, 4)
            split(2)
            if fox:
                open_gate(1, r.i, 4)
            act.wait_ge(ld_s, r.times(48, 48))
            nc.scalar.activation(rgT[:], rgT[:], ACT.Silu).then_inc(r_g, 1)
            split(3)
            if fox:
                open_gate(2, r.i, 4)
            split(4)
            act.wait_ge(r_v, r.times(1, 1))
            nc.scalar.activation(stat[:, 2, 0:NQ], stat[:, 1, 0:NQ], ACT.Sqrt).then_inc(a_root, 1)
            if fox:
                open_gate(3, r.i, 4)
            split(5)

        with act.Fori(0, 2) as i:
            ret_head(At(0, 1, i), False)
        act.wait_ge(f_in, 16 * KC)
        act.wait_ge(mm_done, N_FOX)
        for k in range(KC):
            nc.scalar.copy(xh[:, k, 0:TOUT], mT[:, k, :]).then_inc(a_hi, 1)
        with act.Fori(0, 2) as i:
            ret_head(At(2, 1, i), True)
        for k in range(KC):
            act.wait_ge(ar_in[k % 4], 16 * (k // 4 + 1))
            act.wait_ge(mm_done, N_RET)
            nc.scalar.copy(xh[:, k, 0:TOUT], araw[:, k % 4, :]).then_inc(a_hi, 1)
        with act.Fori(0, 2) as i:
            for q in range(4):
                open_gate(8 + q, i, 4)
                split_hi(act, At(U_RET + q + 2, 4, i), At(N_RET + 3 * q, 12, i))
        for k in range(KC):
            act.wait_ge(mm_done, N_WO)
            act.wait_ge(m_ok, 3 * KC)
            nc.scalar.copy(xh[:, k, 0:TOUT], mT[:, k, :]).then_inc(a_hi, 1)
        for s in range(4):
            for j in range(2):
                split_hi(act, At(U_WO + 2 * s + 2 + j), At(N_WO + NQ * s))
        act.wait_ge(bank_free, N_MLP)
        for i in range(NQ):
            wait(act, a_ssq, NQ + i - 1)
            nc.scalar.activation(hsq[:, i % 2, :], hsb[:, i, :], ACT.Square, accum_out=stat[:, 0, i:i + 1]).then_inc(a_ssq, 1)
        act.wait_ge(r_v, RH + 1)
        nc.scalar.activation(stat[:, 2, 0:NQ], stat[:, 1, 0:NQ], ACT.Sqrt).then_inc(a_root, 1)
        for i in range(NQ):
            turn_rows_act(act, i, T_NORM2)

        def mlp_group(g, tail):
            for q in range(4):
                split_hi(act, At(U_MLP + q + 2, 8, g), At(N_MLP + 3 * q, G_N, g))
                for j, (c, w) in enumerate(O3):
                    n = At(N_MLP + 3 * q + j, G_N, g)
                    act.wait_ge(mm_done, (n + 1).v)
                    par = (3 * q + j) % 2
                    nc.scalar.activation(relu[:, par, 0:w], pd[:, n.mod(NB), 0:w], ACT.Relu).then_inc(u_relu, 1)
                    act.wait_ge(bank_free, (n + 1).v)
                    nc.scalar.copy(uh[:, q, c:c + w], usq[:, par, 0:w]).then_inc(u_hi, 1)
            for q in range(4):
                if q < 2 or not tail:
                    split_hi(act, At(U_MLP + 6 + q, 8, g), At(N_MLP + 12 + 6 * q, G_N, g))

        with act.Fori(0, 7) as g:
            mlp_group(g, False)
        mlp_group(7, True)

    @block.vector
    def _(dve):
        ch = [At(0)]
        dve.wait_ge(const_in, 48)
        nc.vector.tensor_copy(identr[:], ident[:])
        nc.vector.tensor_copy(maskr[:], maskf[:])
        link(dve, nc.vector.memset(onesr[:].bitcast(F32), 0.0), ch)
        nc.vector.memset(onesr[0:2, :].bitcast(F32), 1.0).then_inc(const_ok, 1)
        dve.wait_ge(a_ssq, NQ)
        root_start(dve, stat[:, 0, 0:NQ], NQ, 1.0 / D, ch)
        assert ch[0].v == CH_ROOT1
        dve.wait_ge(a_root, 1)
        root_end(dve, NQ, 1.0, ch)

        def norm_row(i, src, dst, gain, t_base):
            if i >= 2:
                for g in range(2):
                    dve.wait_ge(t_done[g], t_base[g] + i - 1)
            nc.vector.scalar_tensor_tensor(dst[:, i % 2, :], src[:, i, :], stat[:, 5, i:i + 1], gain[:],
                                           ALU.mult, ALU.mult).then_inc(v_norm, 1)

        for i in range(NQ):
            norm_row(i, xt, xn, g1, (0, 0))
            if i:
                turn_rows_dve(dve, i - 1, 0)
        turn_rows_dve(dve, NQ - 1, 0)
        for u in range(3):
            split_lo(dve, At(u))
        dve.wait_ge(small_in, 96)
        for j, (c, w) in enumerate(T3):
            dve.wait_ge(mm_done, j + 1)
            ins = nc.vector.tensor_scalar(lf[:, c:c + w], pd[0:FH, j % NB, 0:w], bfT[:, 0:1], None, ALU.add)
            ins.then_inc(bank_free, 1)
        dve.wait_ge(bank_free, 3)
        nc.vector.scalar_tensor_tensor(lfc[:, 1, :], lf[:], -1.0, lf[:], ALU.mult, ALU.max).then_inc(lf_raw, 1)

        def logf_rest():
            dve.wait_ge(lf_e, 1)
            link(dve, nc.vector.memset(lfc[:, 0, :], 1.0), ch)
            nc.vector.scalar_tensor_tensor(lf[:], lf[:], 0.0, lfc[:, 1, :], ALU.min, ALU.subtract).then_inc(lf_ok, 1)
            dve.wait_ge(lf_ok, 1)
            one = lfc[:, 0, :]
            dve.wait_ge(t_done[0], NQ + 1)
            nc.vector.tensor_copy(cst[:, NKEY:NKEY + NPAST], pt[0:FH, 0, :]).then_inc(t_read[0], 1)
            dve.wait_ge(t_read[0], 1)
            nc.vector.tensor_tensor_scan(cst[:, 0:NM], one[:, 0:NM], lf[:, TOUT:TALL], 0.0, ALU.mult, ALU.add).then_inc(o_read, 1)
            dve.wait_ge(o_read, 1)
            link(dve, nc.vector.tensor_tensor_scan(cst[:, NM:NKEY], one[:, 0:SEQ], lf[:, 0:SEQ], cst[:, NM - 1:NM], ALU.mult, ALU.add), ch)
            link(dve, nc.vector.tensor_tensor_scan(cst[:, NKEY:NKEY + NPAST], one[:, 0:NPAST], cst[:, NKEY:NKEY + NPAST], 0.0, ALU.mult, ALU.add), ch)
            link(dve, nc.vector.tensor_tensor_scan(cst[:, NKEY + NPAST:], one[:, 0:NS], lf[:, SEQ:TOUT], cst[:, NKEY + NPAST - 1:NKEY + NPAST], ALU.mult, ALU.add), ch)
            link(dve, nc.vector.tensor_scalar(nchl[:, 0, :], cst[:], -1.0, None, ALU.mult), ch)
            nc.vector.scalar_tensor_tensor(nchl[:, 1, :], cst[:], -1.0, nchl[:, 0, :], ALU.mult, ALU.subtract).then_inc(nc_ok, 1)

        def strip(s, gain=None, scale=None):
            u, n = At(U_STRIP + 2 * s.first, 2 * s.step, s.i), At(N_STRIP + NQ * s.first, NQ * s.step, s.i)
            for j in range(2):
                split_lo(dve, u + 2 + j)
            for i in range(NQ):
                if i == 0:
                    wait(dve, stored, s.times(ST_STRIP, -ST_STRIP) if s.i is not None or s.first > 1 else 0)
                dve.wait_ge(mm_done, (n + i + 1).v)
                nc.vector.tensor_copy(rows[:, s.mod(2), i, :], pd[:, (n + i).mod(NB), 0:256]).then_inc(bank_free, 1)
                if gain is None:
                    continue
                if i == 0:
                    dve.wait_ge(ssq2, s.v)
                    nc.vector.tensor_scalar(stat[:, 1, :], stat[:, 0, :], 1.0 / P, EPS, ALU.mult, ALU.add).then_inc(ssq_v, 1)
                if i == 1:
                    dve.wait_ge(a_root, (s + 1).v)
                    root_end(dve, 18, scale, ch)
                if 1 <= i <= 3:
                    for x in range(3 * i - 3, 3 * i):
                        for e in range(2):
                            r = rows[:, 1 - s.mod(2), x, e * P:e * P + P]
                            ins = nc.vector.scalar_tensor_tensor(r, r, stat[:, 5, 2 * x + e:2 * x + e + 1], gain[:], ALU.mult, ALU.mult)
                if i == 3:
                    ins.then_inc(strip_ok, 1)

        strip(At(0))
        logf_rest()
        for first, gain, scale in ((1, gq, SCALE), (5, gk, 1.0)):
            c0 = ch[0]
            with dve.Fori(0, 2) as i:
                ch[0] = At(c0.first, 10, i)
                for s in range(2):
                    strip(At(first + s, 2, i), gain, scale)
                assert ch[0].first == c0.first + 10
            ch[0] = At(c0.first + 20)
        strip(At(9))
        with dve.Fori(0, 3) as i:
            for s in range(2):
                strip(At(10 + s, 2, i))

        def maxes(h, j):
            dve.wait_ge(s_done, h.times(9, j + 1))
            m, n = (P, NM + P * (j + 1)) if j < NT else (NS, NPAST + NS)
            nc.vector.tensor_reduce(mx[0:m, j % 2:j % 2 + 1], ps[0:m, 0:n], AX.X, ALU.max, negate=True).then_inc(m_done, 1)

        def scale_probs(h, j):
            dve.wait_ge(e_done, h.times(9, E0 + j + 1))
            m, n = (P, NM + P * (j + 1)) if j < NT else (NS, NPAST + NS)
            link(dve, nc.vector.reciprocal(linv[0:m, j % 2:j % 2 + 1], lsum[0:m, j % 2:j % 2 + 1]), ch)
            nc.vector.tensor_scalar(prob[0:m, j % 2, 0:n], prob[0:m, j % 2, 0:n], linv[0:m, j % 2:j % 2 + 1], None,
                                    ALU.mult).then_inc(p_done, 1)

        def reads(h, gs):
            for g in gs:
                if GROUPS[g][2] == 0:
                    dve.wait_ge(t_done[0], h.times(PER_BANK[0], T_ATT[0] + nth(g) + 1))
                    read_group(lambda o, i_: nc.vector.tensor_copy(o, i_), g).then_inc(t_read[0], 1)

        def out_read(h, j):
            dve.wait_ge(o_done, h.times(9, j + 1))
            if j == 0:
                dve.wait_ge(stored, h.times(64, ST_TURN - 16))
            w = NS if j == NT else P
            nc.vector.tensor_copy(fst[:, j * P:j * P + w], po[:, 0:w]).then_inc(o_read, 1)

        def turn_split(h, x):
            split_lo(dve, At(U_TURN + 3 * h.first + x, 3 * h.step, h.i))

        def turn_read(h, t):
            x, j = t // 3, t % 3
            c, w = (T3 if x == 0 else O3)[j]
            n = At(N_TURN + 9 * h.first + t, 9 * h.step, h.i)
            slot = (h.first + x) % 2
            if j == 0:
                dve.wait_ge(stored, h.times(64, ST_TURN + (-32, 0, 16)[x]))
            dve.wait_ge(mm_done, (n + 1).v)
            z = pd[:, n.mod(NB), 0:w]
            if x:
                nc.vector.tensor_copy(stage[:, slot, c:c + w], z).then_inc(bank_free, 1)
                return
            tmp = rtmp[:, n.mod(2)]
            nc.vector.tensor_tensor(tmp[:, 0, 0:w], z, cosT[:, c:c + w], ALU.mult)
            nc.vector.tensor_tensor(tmp[0:64, 1, 0:w], z[64:P], sinT[64:P, c:c + w], ALU.mult)
            nc.vector.tensor_tensor(tmp[64:P, 1, 0:w], z[0:64], sinT[0:64, c:c + w], ALU.mult).then_inc(bank_free, 1)
            dve.wait_ge(bank_free, (n + 1).v)
            ins = nc.vector.tensor_tensor(stage[:, slot, c:c + w], tmp[:, 0, 0:w], tmp[:, 1, 0:w], ALU.add)
            if j == 2:
                ins.then_inc(unit_v, 1)

        dve.wait_ge(stored, ST_TURN)
        c0 = ch[0]
        with dve.Fori(0, FH // 2) as i:
            for b in range(2):
                h = At(b, 2, i)
                ch[0] = At(c0.first + 9 * b, 18, i)
                reads(h, range(3))
                turn_read(h, 0)
                reads(h, range(3, 6))
                maxes(h, 0)
                turn_read(h, 1)
                for j in range(1, 9):
                    scale_probs(h, j - 1)
                    maxes(h, j)
                    if j in (2, 5, 8):
                        turn_read(h, {2: 3, 5: 5, 8: 7}[j])
                    reads(h, step_groups(j - 1))
                    if j in (1, 3, 6):
                        turn_read(h, {1: 2, 3: 4, 6: 6}[j])
                    out_read(h, j - 1)
                    if j in (1, 3, 5):
                        turn_split(h, {1: 2, 3: 3, 5: 4}[j])
                scale_probs(h, 8)
                reads(h, step_groups(8))
                turn_read(h, 8)
                out_read(h, 8)
        ch[0] = At(c0.first + 9 * FH)
        def ret_ad(r, c):
            c0_, m = CH[c]
            dve.wait_ge(r_a, r.times(NCH, c + 1))
            if c >= 2:
                dve.wait_ge(r_b, r.times(NCH, c - 1))
            kcol = D_COL + (C_KM if c == 0 else (C_KS if c == NCH - 1 else C_KP))
            if c:
                nc.vector.tensor_tensor(sTd[0:m, c % 2, 0:m], ps[0:m, 0:m], dec[0:m, 0:m], ALU.mult)
                nc.vector.tensor_tensor(qg[:, c % 2, 0:m], rqT[:, c0_:c0_ + m], dec[:, D_GQ:D_GQ + m], ALU.mult)
            nc.vector.tensor_scalar(kd[0:m, c % 2, :], pt[0:m, 0, 0:P], dec[0:m, kcol:kcol + 1], None, ALU.mult).then_inc(r_ad, 1)

        def ret_bd(r, c):
            c0_, m = CH[c]
            dve.wait_ge(r_b, r.times(NCH, c + 1))
            U = ps[:, 1024:1024 + RV]
            if c == 0:
                nc.vector.tensor_copy(state[:], U).then_inc(r_bd, 1)
                return
            i = c - 1
            nc.vector.tensor_copy(yraw[0:m, i, :], ps[0:m, 512:512 + RV])
            link(dve, nc.vector.bn_stats(bns[0:m, i, 0:6], ps[0:m, 512:512 + RV]), ch)
            st, gcol = (s0s, C_GS) if c == NCH - 1 else (state, C_GP)
            nc.vector.scalar_tensor_tensor(st[:], st[:], dec[:, D_COL + gcol:D_COL + gcol + 1], U, ALU.mult, ALU.add)
            nc.vector.bn_aggr(bns[0:m, i, 6:8], bns[0:m, i, 0:6]).then_inc(r_bd, 1)
            dve.wait_ge(r_bd, r.times(NCH, c + 1))

        def gated(n, gate_count, slot, m, c, w, first):
            dve.wait_ge(g_ok, gate_count)
            dve.wait_ge(mm_done, (n + 1).v)
            z, gt = pd[:, n.mod(NB), 0:w], stage[:, slot, c:c + w]
            if first:
                nc.vector.tensor_tensor(m, z, gt, ALU.mult).then_inc(bank_free, 1)
                return
            nc.vector.tensor_tensor(mtmp[:, n.mod(2), 0:w], z, gt, ALU.mult).then_inc(bank_free, 1)
            dve.wait_ge(bank_free, (n + 1).v)
            nc.vector.tensor_tensor(m, m, mtmp[:, n.mod(2), 0:w], ALU.add).then_inc(m_ok, 1)

        c0 = ch[0]
        PER_R = 9 + 5

        def ret_head(r, fox):
            ch[0] = At(c0.first + PER_R * r.first, PER_R, r.i)

            def read(t):
                q, (c, w) = t // 3, O3[t % 3]
                n = At(N_GB + 12 * r.first + t, 12, r.i)
                if fox:
                    m = mT[:, bass.ds(r.times(4, q - 8), 1), c:c + w].rearrange("p a n -> p (a n)")
                    gated(n, r.times(4, q - 7), q % 2, m, c, w, True)
                    return
                if t % 3 == 0:
                    dve.wait_ge(stored, r.times(64, ST_GB + 16 * (q - 1)))
                dve.wait_ge(mm_done, (n + 1).v)
                nc.vector.tensor_copy(stage[:, q % 2, c:c + w], pd[:, n.mod(NB), 0:w]).then_inc(bank_free, 1)

            def split(x):
                split_lo(dve, At(U_GB + 4 * r.first + x, 4, r.i))

            dve.wait_ge(ld_r, r.times(48, 48))
            ret_ad(r, 0)
            split(2)
            for c in range(1, NCH):
                ret_ad(r, c)
                if c in (3, 6, 9):
                    read({3: 1, 6: 3, 9: 5}[c])
                ret_bd(r, c - 1)
                if c in (1, 4, 7):
                    read({1: 0, 4: 2, 7: 4}[c])
                if c == 5:
                    split(3)
            dve.wait_ge(ld_s, r.times(48, 48))
            dve.wait_ge(yz_ok, 1)
            ret_bd(r, NCH - 1)
            read(6)
            nc.vector.tensor_scalar(stat[:, 1, 0:NQ], bns[:, :, 7], 1.0, EPS, ALU.mult, ALU.add).then_inc(r_v, 1)
            split(4)
            dve.wait_ge(a_root, r.times(1, 10))
            root_end(dve, NQ, 1.0, ch)
            read(7)
            for i in range(NQ):
                m = P if i < NT else NS
                ins = nc.vector.tensor_scalar(yraw[0:m, i, :], yraw[0:m, i, :], bns[0:m, i, 6:7], stat[0:m, 5, i:i + 1],
                                              ALU.subtract, ALU.mult)
            ins.then_inc(r_n, 1)
            read(8)
            dve.wait_ge(r_g, r.times(1, 1))
            dve.wait_ge(ld_g, 16)
            for q, (e, tiles) in enumerate(RT_GROUPS):
                dve.wait_ge(r_t, r.times(5, q + 1))
                gain = lambda ee: gnT[:, bass.ds(r.times(2, ee), 1)]
                if e is not None:
                    t0 = tiles[0][1] * P
                    ins = nc.vector.scalar_tensor_tensor(rgT[:, e, t0:t0 + 512], pt[:, q % 2, :], gain(e),
                                                         rgT[:, e, t0:t0 + 512], ALU.mult, ALU.mult)
                else:
                    for ee in range(2):
                        ins = nc.vector.scalar_tensor_tensor(rgT[:, ee, SEQ:TOUT], pt[:, q % 2, P * ee:P * ee + NS],
                                                             gain(ee), rgT[:, ee, SEQ:TOUT], ALU.mult, ALU.mult)
                ins.then_inc(r_tr, 1)
                if q == 2:
                    read(9)
            split(5)
            read(10)
            read(11)
            dve.wait_ge(r_sto, r.times(64, 32))
            assert ch[0].first == c0.first + PER_R * (r.first + 1)

        with dve.Fori(0, 2) as i:
            ret_head(At(0, 1, i), False)
        for k in range(KC):
            dve.wait_ge(a_hi, A_NORM1 + k + 1)
            nc.vector.tensor_tensor(xl[:, k, 0:TOUT], mT[:, k, :], xh[:, k, 0:TOUT], ALU.subtract).then_inc(a_lo, 1)
        with dve.Fori(0, 2) as i:
            ret_head(At(2, 1, i), True)
        ch[0] = At(c0.first + PER_R * RH)

        for k in range(KC):
            dve.wait_ge(a_hi, A_FOX + k + 1)
            nc.vector.tensor_tensor(xl[:, k, 0:TOUT], araw[:, k % 4, :], xh[:, k, 0:TOUT], ALU.subtract).then_inc(a_lo, 1)
        with dve.Fori(0, 2) as i:
            for q in range(4):
                split_lo(dve, At(U_RET + q + 2, 4, i))
                for j, (c, w) in enumerate(O3):
                    m = mT[:, bass.ds(i * 4 + q, 1), c:c + w].rearrange("p a n -> p (a n)")
                    gated(At(N_RET + 3 * q + j, 12, i), At(9 + q, 4, i).v, q % 2, m, c, w, False)
        for k in range(KC):
            dve.wait_ge(a_hi, A_RET + k + 1)
            nc.vector.tensor_tensor(xl[:, k, 0:TOUT], mT[:, k, :], xh[:, k, 0:TOUT], ALU.subtract).then_inc(a_lo, 1)

        dve.wait_ge(hz_ok, 1)
        for s in range(4):
            for j in range(2):
                split_lo(dve, At(U_WO + 2 * s + 2 + j))
            dve.wait_ge(x2_in[s % 2], 32 * (s // 2 + 1))
            for i in range(NQ):
                n = At(N_WO + NQ * s + i)
                dve.wait_ge(mm_done, (n + 1).v)
                m = P if i < NT else NS
                nc.vector.tensor_tensor(hsb[0:m, i, 256 * s:256 * s + 256], pd[0:m, n.mod(NB), 0:256],
                                        xrow[0:m, s % 2, i, :], ALU.add).then_inc(bank_free, 1)
        dve.wait_ge(a_ssq, 2 * NQ)
        nc.vector.tensor_scalar(stat[:, 1, 0:NQ], stat[:, 0, 0:NQ], 1.0 / D, EPS, ALU.mult, ALU.add).then_inc(r_v, 1)
        dve.wait_ge(a_root, 10 + RH)
        root_end(dve, NQ, 1.0, ch)
        dve.wait_ge(g2_in, 16)
        for i in range(NQ):
            norm_row(i, hsb, hn, g2, T_NORM2)
            if i:
                turn_rows_dve(dve, i - 1, A_M)
        turn_rows_dve(dve, NQ - 1, A_M)

        dve.wait_ge(h_st, 32)
        link(dve, nc.vector.memset(yT[:], 0.0), ch)
        def mlp_group(g, tail):
            for q in range(4):
                split_lo(dve, At(U_MLP + q + 2, 8, g))
                for j, (c, w) in enumerate(O3):
                    n = At(N_MLP + 3 * q + j, G_N, g)
                    par = (3 * q + j) % 2
                    dve.wait_ge(u_relu, At(3 * q + j + 1, 12, g).v)
                    nc.vector.scalar_tensor_tensor(usq[:, par, 0:w], pd[:, n.mod(NB), 0:w], 0.0, relu[:, par, 0:w],
                                                   ALU.max, ALU.mult).then_inc(bank_free, 1)
                    dve.wait_ge(u_hi, At(3 * q + j + 1, 12, g).v)
                    nc.vector.tensor_tensor(ul[:, q, c:c + w], usq[:, par, 0:w], uh[:, q, c:c + w], ALU.subtract).then_inc(u_lo, 1)
            for q in range(4):
                if q < 2 or not tail:
                    split_lo(dve, At(U_MLP + 6 + q, 8, g))
                for m in range(2):
                    for j, (c, w) in enumerate(O3):
                        n = At(N_MLP + 12 + 6 * q + 3 * m + j, G_N, g)
                        dve.wait_ge(mm_done, (n + 1).v)
                        dve.wait_ge(bank_free, n.v)
                        y = yT[:, 2 * q + m, c:c + w]
                        nc.vector.tensor_tensor(y, y, pd[:, n.mod(NB), 0:w], ALU.add).then_inc(bank_free, 1)

        with dve.Fori(0, 7) as g:
            mlp_group(g, False)
        mlp_group(7, True)
        for i in range(NQ):
            w = P if i < NT else NS
            dve.wait_ge(hb_in[i % 2], 16 * (i // 2 + 1))
            if i >= 2:
                dve.wait_ge(y_st[i % 2], 16 * (i // 2))
            for g in range(2):
                dve.wait_ge(t_done[g], T_FIN[g] + i + 1)
                nc.vector.tensor_tensor(yout[0:w, i % 2, 512 * g:512 * g + 512], pt[0:w, g, :],
                                        hback[0:w, i % 2, 512 * g:512 * g + 512], ALU.add).then_inc(y_rd, 1)

    ctx.close()


_INS = ["x_prompt", "x_sample", "state_ret", "cache_fox_k", "cache_fox_v", "cache_fox_logf", "meta_tokens",
        "norm1_g", "w_in", "b_forget", "q_norm_g", "k_norm_g", "ret_gn_g", "w_ret_out", "w_fox_out", "w_o",
        "norm2_g", "w_ff1", "w_ff2"]
_OUTS = [(1, 1024, 1024), (1, 32, 1024), (1, 1, 4, 128, 256), (1, 1, 1040, 8, 128), (1, 1, 1040, 8, 128),
         (1, 1, 1040, 8), (1, 1, 4, 128, 256), (1, 1, 32, 8, 128), (1, 1, 32, 8, 128), (1, 1, 32, 8)]


def shape_constants():
    import numpy as np

    f = np.float32
    ident = np.eye(P, dtype=f)
    mask = np.where(np.arange(P)[None, :] > np.arange(P)[:, None], f(NEG), f(0.0)).astype(f)
    pos = np.concatenate([np.arange(SEQ), NPAST + np.arange(NS), np.arange(NM) - NM]).astype(f)
    half = P // 2
    inv = (f(10000.0) ** (-np.arange(half, dtype=f) / f(half))).astype(f)
    ang = (pos[:, None] * inv[None, :]).astype(f)
    cos, sin = np.cos(ang).astype(f).T, np.sin(ang).astype(f).T
    cosT = np.concatenate([cos, cos], 0)
    sinT = np.concatenate([sin, -sin], 0)
    decay = np.zeros((RH, P, 264), f)
    n = np.arange(P, dtype=np.float64)
    for h in range(RH):
        lg = float(np.log(1.0 - 2.0 ** (-5.0 - h)))
        diff = n[None, :] - n[:, None]
        decay[h, :, 0:P] = np.where(diff >= 0, np.exp(lg * np.maximum(diff, 0)), 0) * SCALE
        decay[h, :, P:2 * P] = np.exp(lg * (n + 1))[None, :]
        decay[h, :, 2 * P + 0] = np.exp(lg * (P - 1 - n)) * SCALE
        decay[h, :, 2 * P + 1] = np.exp(lg * (NM - 1 - np.minimum(n, NM - 1))) * SCALE
        decay[h, :, 2 * P + 2] = np.exp(lg * (NS - 1 - np.minimum(n, NS - 1))) * SCALE
        decay[h, :, 2 * P + 3] = np.exp(lg * P)
        decay[h, :, 2 * P + 4] = np.exp(lg * NS)
    return {"ident": ident, "mask": mask, "cos": np.ascontiguousarray(cosT), "sin": np.ascontiguousarray(sinT),
            "decay": decay}


def kernel(**inputs):
    import numpy as np
    import concourse.bacc as _bacc
    from concourse.bass_utils import run_bass_kernel_spmd as _run

    nc = _bacc.Bacc("TRN2", target_bir_lowering=False, num_devices=1)
    arrays, args = {}, []
    named = [(n, inputs[n]) for n in _INS] + [(f"c_{n}", a) for n, a in shape_constants().items()]
    for name, a in named:
        a = np.ascontiguousarray(a)
        arrays[f"in_{name}"] = a
        args.append(nc.dram_tensor(f"in_{name}", a.shape, mybir.dt.from_np(a.dtype), kind="ExternalInput").ap())
    for i, shape in enumerate(_OUTS):
        args.append(nc.dram_tensor(f"out_{i}", shape, F32, kind="ExternalOutput").ap())
    hybrid_step(nc, *args)
    r = _run(nc, [arrays], core_ids=[0])
    return tuple(r.results[0][f"out_{i}"] for i in range(len(_OUTS)))
```

```python
from contextlib import ExitStack

import concourse.bass as bass
from concourse import mybir

F32 = mybir.dt.float32
F32R = mybir.dt.float32r
ALU = mybir.AluOpType
ACT = mybir.ActivationFunctionType
AX = mybir.AxisListType

P = 128
D = 1024
KC = D // P
SEQ = 1024
NT = SEQ // P
NS = 32
NM = 16
NPAST = 512
NC = NPAST // P
TOUT = SEQ + NS
TALL = TOUT + NM
TPAD = (NT + 1) * P
NQ = NT + 1
FH = 8
RH = 4
RV = 256
EPS = 1e-6
SCALE = float(P) ** -0.5
NEG = -1e30
W_RQ, W_RV, W_RG, W_FQ, W_FK, W_FV, W_FF, W_GA, W_GB = 0, 1024, 2048, 3072, 4096, 5120, 6144, 6152, 7176
UNIT = 1024
NB = 2


def hybrid_step(nc, x_prompt, x_sample, state_ret, cache_k, cache_v, cache_logf, meta, norm1_g, w_in,
                b_forget, q_norm_g, k_norm_g, ret_gn_g, w_ret_out, w_fox_out, w_o, norm2_g, w_ff1, w_ff2,
                c_ident, c_mask, c_cos, c_sin, c_decay,
                y_prompt, y_sample, p_state, p_k, p_v, p_logf, s_state, s_k, s_v, s_logf):
    ctx = ExitStack()

    def sb(name, shape, dt=F32, stack=ctx):
        return stack.enter_context(nc.sbuf_tensor(name, shape, dt))

    def sem(name):
        return ctx.enter_context(nc.semaphore(name))

    def wait(eng, s, value):
        if not isinstance(value, int) or value > 0:
            eng.wait_ge(s, value)

    xp = x_prompt.rearrange("a t d -> (a t) d")
    xs = x_sample.rearrange("a t d -> (a t) d")
    st_in = state_ret.rearrange("l b h d v -> (l b h) d v")
    ck = cache_k.rearrange("l b t h d -> (l b t) (h d)")
    cv = cache_v.rearrange("l b t h d -> (l b t) (h d)")
    clf = cache_logf.rearrange("l b t h -> (l b t) h")
    win = w_in.rearrange("l (k p) n -> p (l k) n", p=P)
    wro = w_ret_out.rearrange("l (k p) n -> p (l k) n", p=P)
    wfo = w_fox_out.rearrange("l (k p) n -> p (l k) n", p=P)
    wout = w_o.rearrange("l (k p) n -> p (l k) n", p=P)
    wf1 = w_ff1.rearrange("l (k p) n -> p (l k) n", p=P)
    wf2 = w_ff2.rearrange("l (k p) n -> p (l k) n", p=P)
    yp = y_prompt.rearrange("a t d -> (a t) d")
    ys = y_sample.rearrange("a t d -> (a t) d")
    pst = p_state.rearrange("l b h d v -> (l b h) d v")
    sst = s_state.rearrange("l b h d v -> (l b h) d v")
    pk = p_k.rearrange("l b t h d -> (l b t) (h d)")
    pv = p_v.rearrange("l b t h d -> (l b t) (h d)")
    plf = p_logf.rearrange("l b t h -> (l b t) h")
    sk = s_k.rearrange("l b t h d -> (l b t) (h d)")
    sv = s_v.rearrange("l b t h d -> (l b t) (h d)")
    slf = s_logf.rearrange("l b t h -> (l b t) h")

    def dram(name, shape, dt=F32):
        return nc.dram_tensor(name, shape, dt, kind="Internal").ap()

    pq = dram("q_rows", (NM + SEQ, D))
    sq = dram("q_rows_sample", (NS, D))
    prv = dram("rv_rows", (NM + SEQ, D))
    srv = dram("rv_rows_sample", (NS, D))
    rot = dram("rotated", (8, P, TALL))
    gates = dram("gates", (3 * KC, P, TOUT))
    negc = dram("neg_cumsum", (FH, SEQ + NM + NPAST + NS))
    foxT = dram("fox_out_T", (KC, P, TOUT))
    retT = dram("ret_out_T", (KC, P, TOUT))
    hrow = dram("h_rows", (TOUT, D))

    xh = sb("act_hi", [P, KC, TPAD], F32R)
    xl = sb("act_lo", [P, KC, TPAD], F32R)
    raw = sb("w_raw", [P, 2, UNIT])
    wh = sb("w_hi", [P, 4, UNIT], F32R)
    wl = sb("w_lo", [P, 4, UNIT], F32R)
    ident = sb("ident", [P, P])
    identr = sb("ident_r", [P, P], F32R)
    maskf = sb("mask", [P, P])
    maskr = sb("mask_r", [P, P], F32R)
    stat = sb("stat", [P, 8, 18])
    gnT = sb("gn_gain", [P, KC])
    mx = sb("neg_max", [P, 2])
    lsum = sb("row_sum", [P, 2])
    linv = sb("row_sum_inv", [P, 2])
    bfT = sb("b_forget_col", [FH, 1])

    def arena(sizes):
        with ExitStack() as s:
            return [sb(n, shape, dt, s) for n, shape, dt in sizes]

    xt, xn, g1, xsq = arena([("x_rows", [P, NQ, D], F32), ("xn_rows", [P, 2, D], F32), ("norm1_bc", [P, D], F32), ("x_squares", [P, 2, D], F32)])
    lfc, cosT, sinT, gq, gk, cst, crow, lfr, ncum, _, junk, lf, _, rows = arena([
        ("lf_tmp", [FH, 2, TALL], F32), ("cos", [P, TALL], F32), ("sin", [P, TALL], F32),
        ("gq_bc", [P, P], F32), ("gk_bc", [P, P], F32), ("cumsum", [FH, TALL + NPAST], F32),
        ("cache_lf_rows", [P, NC, FH], F32), ("logf_rows", [P, NQ, FH], F32),
        ("neg_cumsum_sb", [FH, SEQ + NM + NPAST + NS], F32), ("norm1_end", [P, 6520], F32),
        ("row_squares", [P, 18, P], F32), ("logf_T", [FH, TALL], F32), ("values_end", [P, 208], F32), ("strip_rows", [P, 2, NQ, 256], F32)])
    (stage, _, _, prob, qT, pT, kcT, rtmp, kT, qrow, qsrow, krow, kmrow, ksrow, kcrow, ncr, vrow, vmrow, vsrow, vcrow,
     fst) = arena([
        ("stage", [P, 2, TALL], F32), ("cos_kept", [P, TALL], F32), ("sin_kept", [P, TALL], F32),
        ("probs", [P, 2, SEQ + NM], F32), ("fqT", [P, TOUT], F32), ("probsT", [P, NT + 1, P], F32),
        ("fkcT", [P, NPAST], F32), ("rot_tmp", [P, 2, 2, 360], F32), ("fkT", [P, SEQ + NM + NS], F32),
        ("fq_rows", [P, NT, P], F32), ("fq_rows_s", [NS, P], F32), ("fk_rows", [P, NT, P], F32),
        ("fk_rows_m", [NM, P], F32), ("fk_rows_s", [NS, P], F32), ("fk_rows_c", [P, NC, P], F32),
        ("negc_rows", [P, SEQ + NM + NPAST + NS], F32), ("fv_rows", [P, NT, P], F32), ("fv_rows_m", [NM, P], F32), ("fv_rows_s", [NS, P], F32),
        ("fv_rows_c", [P, NC, P], F32),
        ("fox_stage", [P, TOUT], F32)])
    (_, mT, state, sTd, kd, qg, rvrow, rvm, rvs, yraw, bns, rgT, _, s0s, rqT, rkT, dec) = arena([
        ("stage_kept", [P, 2, TALL], F32), ("merged_T", [P, KC, TOUT], F32), ("ret_state", [P, RV], F32),
        ("scores_T", [P, 2, P], F32), ("k_decayed", [P, 2, P], F32), ("q_decayed", [P, 2, P], F32),
        ("rv_rows_sb", [P, NT, RV], F32), ("rv_rows_m", [NM, RV], F32), ("rv_rows_s", [NS, RV], F32),
        ("y_raw", [P, NQ, RV], F32), ("bn_stats", [P, NQ, 8], F32), ("ret_gate_T", [P, 2, TOUT], F32),
        ("attention_end", [P, 312], F32), ("sample_state", [P, RV], F32), ("rqT", [P, TALL], F32),
        ("rkT", [P, TALL], F32), ("decay", [P, 264], F32)])
    _, _, _, araw0, _, mtmp, _, araw1 = arena([
        ("stage_kept2", [P, 2, TALL], F32), ("merged_T_kept", [P, KC, TOUT], F32), ("ret_state_kept", [P, RV], F32),
        ("ret_out_back0", [P, 3, TOUT], F32), ("x_again_kept", [P, 3008], F32), ("gated", [P, 2, 352], F32),
        ("kept", [P, 1504], F32), ("ret_out_back1", [P, 3, TOUT], F32)])
    hsb, hn, xrow, g2, hsq = arena([("h_sb", [P, NQ, D], F32), ("hn_rows", [P, 2, D], F32),
                               ("x_again", [P, 2, NQ, 256], F32), ("norm2_bc", [P, D], F32), ("h_squares", [P, 2, D], F32)])
    yT, hback, yout, uh, ul, relu, usq = arena([
        ("y_T", [P, KC, TOUT], F32), ("h_back", [P, 2, D], F32), ("y_rows", [P, 2, D], F32),
        ("u_hi", [P, 4, TOUT], F32R), ("u_lo", [P, 4, TOUT], F32R), ("relu", [P, 2, 352], F32), ("u", [P, 2, 352], F32)])

    pd = ctx.enter_context(nc.psum_tensor("ps_dense", [P, NB, 512], F32))
    pt = ctx.enter_context(nc.psum_tensor("ps_turn", [P, 2, 512], F32))
    ps = ctx.enter_context(nc.psum_tensor("ps_scores", [P, 3 * 512], F32))
    po = ctx.enter_context(nc.psum_tensor("ps_out", [P, 512], F32))

    w_in_s = [sem(f"w_landed{i}") for i in range(2)]
    w_hi_s = sem("w_hi_ready")
    w_lo_s = sem("w_lo_ready")
    mm_done = sem("dense_done")
    bank_free = sem("dense_read")
    const_in = sem("const_landed")
    const_ok = sem("const_ready")
    pad_ok = sem("pad_zeroed")
    x_in = [sem(f"x_landed{i}") for i in range(NQ)]
    dch = sem("dve_chain")
    a_ssq = sem("ssq_ready")
    a_root = sem("root_ready")
    v_norm = sem("rows_normed")
    t_done = [sem("turned0"), sem("turned1")]
    t_read = [sem("turn_read0"), sem("turn_read1")]
    a_hi = sem("act_hi_ready")
    a_lo = sem("act_lo_ready")

    T3 = [(0, 358), (358, 358), (716, 356)]
    O3 = [(0, 352), (352, 352), (704, 352)]

    class At:

        def __init__(self, first, step=0, i=None):
            self.first, self.step, self.i = first, step, i

        def __add__(self, k):
            return At(self.first + k, self.step, self.i)

        def __sub__(self, k):
            return self + (-k)

        def mod(self, m):
            assert self.i is None or self.step % m == 0
            return self.first % m

        def times(self, m, plus=0):
            return At(self.first * m + plus, self.step * m, self.i).v

        @property
        def v(self):
            return self.first if self.i is None else self.i * self.step + self.first

    STRIPS = 16
    U_FF, N_FF = 2, NQ
    U_STRIP, N_STRIP = 1, 3
    U_TURN, N_TURN = U_STRIP + 2 * STRIPS, N_STRIP + NQ * STRIPS
    U_GB, N_GB = U_TURN + 3 * FH, N_TURN + 9 * FH
    U_FOX, N_FOX = U_GB + 8, N_GB + 24
    U_RET, N_RET = U_FOX + 8, N_FOX + 24
    U_WO, N_WO = U_RET + 8, N_RET + 24
    U_MLP, N_MLP = U_WO + 8, N_WO + 4 * NQ
    G_N = 36
    U_END = U_MLP + 64
    A_NORM1 = 2 * NQ
    A_FOX, A_RET, A_M, A_NORM2 = A_NORM1 + 24, A_NORM1 + 48, A_NORM1 + 72, A_NORM1 + 72 + 2 * NQ
    ST_STRIP = 48
    ST_TURN = ST_STRIP * STRIPS
    ST_GB = ST_TURN + 64 * FH
    ST_RET = ST_GB + 16 * 8

    def ring(u):
        return 1 + (u.first - U_TURN) % 3 if U_TURN <= u.first < U_GB else u.mod(4)

    def load_unit(sp, u, src):
        wait(sp, w_lo_s, (u - 1).v)
        k = src.shape[1]
        sp.dma_start(raw[:, u.mod(2), :].rearrange("p (k m) -> p k m", k=k), src).then_inc(w_in_s[u.mod(2)], 16)

    def split_hi(act, u, n):
        act.wait_ge(w_in_s[u.mod(2)], At(u.first // 2, u.step // 2, u.i).times(16, 16))
        wait(act, mm_done, n.v)
        nc.scalar.copy(wh[:, ring(u), :], raw[:, u.mod(2), :]).then_inc(w_hi_s, 1)

    def split_lo(dve, u):
        dve.wait_ge(w_hi_s, (u + 1).v)
        nc.vector.tensor_tensor(wl[:, ring(u), :], raw[:, u.mod(2), :], wh[:, ring(u), :],
                                ALU.subtract).then_inc(w_lo_s, 1)

    def turned_piece(pe, n, us, c, w, part, hi=xh, lo=xl, kc=KC, m0=0, parts=3):
        if part == 0:
            wait(pe, bank_free, (n - 1).v)
        width = UNIT // kc
        a, b = (x[:, us, :].rearrange("p (k m) -> p k m", m=width) for x in (wh, wl))
        each = 3 * kc // parts
        for x in range(part * each, (part + 1) * each):
            k = x // 3
            lhs, rhs = ((b, hi), (a, lo), (a, hi))[x % 3]
            mm = nc.tensor.matmul(pd[:, n.mod(NB), 0:w], lhs[:, k, m0:m0 + P], rhs[:, k, c:c + w],
                                  start=(x == 0), stop=(x == 3 * kc - 1))
        if part == parts - 1:
            mm.then_inc(mm_done, 1)

    def turned_step(pe, n, us, c, w, **kw):
        turned_piece(pe, n, us, c, w, 0, parts=1, **kw)

    def strip_step(pe, n, u, i):
        wait(pe, bank_free, (n - 1).v)
        for k in range(KC):
            us = (u + k // 4).mod(4)
            a, b = (x[:, us, 256 * (k % 4):256 * (k % 4) + 256] for x in (wh, wl))
            t = slice(i * P, i * P + P)
            for q, (lhs, rhs) in enumerate(((xh, b), (xl, a), (xh, a))):
                mm = nc.tensor.matmul(pd[:, n.mod(NB), 0:256], lhs[:, k, t], rhs,
                                      start=(k == 0 and q == 0), stop=(k == KC - 1 and q == 2))
        mm.then_inc(mm_done, 1)

    def link(dve, ins, chain):
        ins.then_inc(dch, 1)
        chain[0] = chain[0] + 1
        dve.wait_ge(dch, chain[0].v)

    def root_end(dve, w, scale, chain, c0=0):
        v, r, rr, e, t, o = (stat[:, x, c0:c0 + w] for x in (1, 2, 3, 4, 6, 5))
        link(dve, nc.vector.reciprocal(rr, r), chain)
        link(dve, nc.vector.tensor_tensor(e, rr, rr, ALU.mult), chain)
        link(dve, nc.vector.tensor_tensor(t, e, v, ALU.mult), chain)
        link(dve, nc.vector.tensor_scalar(e, t, -0.5, 1.5, ALU.mult, ALU.add), chain)
        link(dve, nc.vector.scalar_tensor_tensor(o, rr, scale, e, ALU.mult, ALU.mult), chain)

    def turn_rows_pe(pe, rows_ap, i, a_base, norm_base):
        pe.wait_ge(v_norm, norm_base + i + 1)
        for g in range(2):
            wait(pe, a_lo, a_base + max(2 * i + g - 1, 0))
            for c in range(4):
                mm = nc.tensor.transpose(pt[:, g, c * P:c * P + P],
                                         rows_ap[:, i % 2, (4 * g + c) * P:(4 * g + c + 1) * P], ident[:])
            mm.then_inc(t_done[g], 1)

    def resplit_hi(j, src):
        c, w = O3[j]
        for k in range(KC):
            nc.scalar.copy(xh[:, k, c:c + w], src[k][:, c:c + w]).then_inc(a_hi, 1)

    def resplit_lo(dve, j, src, base):
        c, w = O3[j]
        for k in range(KC):
            dve.wait_ge(a_hi, base + KC * j + k + 1)
            nc.vector.tensor_tensor(xl[:, k, c:c + w], src[k][:, c:c + w], xh[:, k, c:c + w], ALU.subtract).then_inc(a_lo, 1)
        if j == 2:
            dve.wait_ge(a_lo, base + 3 * KC)

    def third_of(i):
        return min(2, (P * (i + 1) - 1) // O3[0][1])

    def third_last(j):
        return (O3[j][0] + O3[j][1] - 1) // P

    LAST_TURNS = [[[], [], []], [[0], [1], []], [[2], [3], [4]]]

    m_rows = [mT[:, k, :] for k in range(KC)]
    ret_rows = [(araw0, araw1)[k // 3][:, k % 3, :] for k in range(6)] + [rgT[:, e, :] for e in range(2)]

    def act_cols(x, i, g):
        return x[:, 4 * g:4 * g + 4, i * P:i * P + P]

    def turn_rows_act(act, i, t_base):
        for g in range(2):
            act.wait_ge(t_done[g], t_base[g] + i + 1)
            nc.scalar.copy(act_cols(xh, i, g), pt[:, g, :].rearrange("p (c t) -> p c t", c=4)).then_inc(a_hi, 1)

    def turn_rows_dve(dve, i, h_base):
        for g in range(2):
            dve.wait_ge(a_hi, h_base + 2 * i + g + 1)
            nc.vector.tensor_tensor(act_cols(xl, i, g), pt[:, g, :].rearrange("p (c t) -> p c t", c=4),
                                    act_cols(xh, i, g), ALU.subtract).then_inc(a_lo, 1)

    def att_groups():
        out = []
        for q in range(6):
            out.append((-1, q, len(out) % 2))
        for j in range(NT):
            blocks = list(range(j + 1)) + [NT]
            for b in range(0, len(blocks), 4):
                out.append((j, blocks[b:b + 4], len(out) % 2))
        out.append((NT, list(range(NC + 1)), len(out) % 2))
        return out

    GROUPS = att_groups()
    PER_BANK = [sum(g[2] == b for g in GROUPS) for b in range(2)]
    T_ATT = [NQ + 1, NQ + 1]
    T_NORM2 = [T_ATT[b] + FH * PER_BANK[b] for b in range(2)]
    T_FIN = [T_NORM2[b] + NQ for b in range(2)]

    def nth(g):
        return sum(x[2] == GROUPS[g][2] for x in GROUPS[:g])

    def step_groups(j):
        return [g for g in range(len(GROUPS)) if GROUPS[g][0] == j]

    NKEY = SEQ + NM

    def turn_prologue(q):
        if q < 2:
            return [(qrow[:, 4 * q + x, :], x * P, P) for x in range(4)], [(qT[:, 512 * q:512 * q + 512], 0, 512)]
        if q < 4:
            z = q - 2
            return ([(krow[:, 4 * z + x, :], x * P, P) for x in range(4)],
                    [(kT[:, NM + 512 * z:NM + 512 * z + 512], 0, 512)])
        if q == 4:
            return ([(kcrow[:, 0, :], 0, P), (qsrow[:], P, NS), (kmrow[:], P + 32, NM), (ksrow[:], P + 64, NS)],
                    [(kcT[:, 0:P], 0, P), (qT[:, SEQ:TOUT], P, NS), (kT[:, 0:NM], P + 32, NM),
                     (kT[:, NKEY:NKEY + NS], P + 64, NS)])
        return [(kcrow[:, x + 1, :], x * P, P) for x in range(3)], [(kcT[:, P:], 0, 3 * P)]

    def prob_block(j, b):
        if j == NT:
            return b * P, (P if b < NC else NS)
        return (0, NM) if b == NT else (NM + b * P, P)

    def read_group(eng_copy, g):
        j, blocks, bank = GROUPS[g]
        if j < 0:
            for dst, c, w in turn_prologue(blocks)[1]:
                last = eng_copy(dst, pt[:, bank, c:c + w])
            return last
        if j == NT:
            eng_copy(pT[:, 0, 0:NS], pt[:, bank, 0:NS])
            eng_copy(pT[:, 1:NC, 0:NS], pt[:, bank, P:P + 3 * NS].rearrange("p (b w) -> p b w", b=3))
            return eng_copy(pT[0:NS, NC, 0:NS], pt[0:NS, bank, P + 3 * NS:P + 4 * NS])
        width = P
        full = [b for b in blocks if prob_block(j, b)[1] == P]
        if full:
            n = len(full)
            last = eng_copy(pT[:, full[0]:full[0] + n, 0:width],
                            pt[:, bank, 0:n * width].rearrange("p (b w) -> p b w", b=n))
        for x, b in enumerate(blocks):
            k = prob_block(j, b)[1]
            if k != P:
                last = eng_copy(pT[0:k, b, 0:width], pt[0:k, bank, x * width:x * width + width])
        return last

    S0, E0, O0 = 1, 1, 1

    CH = [(TOUT, NM)] + [(i * P, P) for i in range(NT)] + [(SEQ, NS)]
    NCH = len(CH)
    D_GQ, D_COL = P, 2 * P
    C_KP, C_KM, C_KS, C_GP, C_GS = range(5)

    RT_GROUPS = [(e, [(e, 4 * z + x, P) for x in range(4)]) for e in range(2) for z in range(2)]
    RT_GROUPS.append((None, [(0, NT, P), (1, NT, P)]))

    bf_in = sem("b_forget_landed")
    small_in = sem("small_landed")
    ms_ok = sem("mean_square_ready")
    ssq2 = sem("strip_ssq")
    ssq_v = sem("strip_mean_square")
    strip_ok = sem("strip_ready")
    stored = sem("stored")
    unit_v = sem("rotated_ready")
    lf_raw = sem("logf_raw")
    lf_e = sem("logf_exp")
    lf_ok = sem("logf_ready")
    lf_r = sem("logf_rows_ready")
    lf_st = sem("logf_stored")
    ld_qk = sem("qk_landed"); ld_v = sem("v_landed"); ld_n = sem("negc_landed")
    s_done = sem("scores_done")
    s_read = sem("scores_read")
    m_done = sem("max_done")
    e_done = sem("exp_done")
    p_done = sem("probs_ready")
    o_done = sem("out_done")
    o_read = sem("out_read")
    ld_r = sem("ret_qk_landed"); ld_rv = sem("ret_v_landed"); ld_s = sem("ret_gate_landed")
    ld_g = sem("gain_landed")
    yz_ok = sem("ret_pad_set")
    r_a = sem("ret_scores_done")
    r_ad = sem("ret_scores_read")
    r_b = sem("ret_out_done")
    r_bd = sem("ret_out_read")
    r_v = sem("ret_var_ready")
    r_n = sem("ret_normed")
    r_g = sem("ret_gate_open")
    r_t = sem("ret_turned")
    r_tr = sem("ret_turn_read")
    r_sto = sem("ret_stored")
    f_in = sem("fox_landed"); ar_in = sem("ret_out_back")
    g_in = [sem("gate_landed0"), sem("gate_landed1")]
    g_ok = sem("gate_open")
    m_ok = sem("merged_ready")
    x2_in = [sem("x_again0"), sem("x_again1")]; g2_in = sem("norm2_landed")
    hz_ok = sem("h_pad_zero")
    h_st = sem("h_stored"); hb_in = [sem("h_back0"), sem("h_back1")]
    u_relu = sem("relu_ready")
    u_hi = sem("u_hi_ready")
    u_lo = sem("u_lo_ready")
    y_zero = sem("y_T_zero")
    y_rd = sem("y_turn_read")
    y_st = [sem("y_stored0"), sem("y_stored1")]

    block = ctx.enter_context(nc.Block())

    @block.sync
    def _(sp):
        sp.dma_start(ident[:], c_ident).then_inc(const_in, 16)

        def load_xrows(i):
            sp.dma_start(xt[:, i, :], xp[i * P:(i + 1) * P, :]).then_inc(x_in[i], 16)

        for i in range(3):
            load_xrows(i)
        sp.dma_start(g1[:], norm1_g[0].partition_broadcast(P)).then_inc(const_in, 16)
        sp.dma_start(maskf[:], c_mask).then_inc(const_in, 16)
        for i in range(3, 6):
            load_xrows(i)
        for j in range(2):
            load_unit(sp, At(j), win[:, 4 * j:4 * j + 4, W_FQ:W_FQ + 256])
        for i in range(6, NT):
            load_xrows(i)
        sp.wait_ge(pad_ok, 1)
        sp.dma_start(xt[0:NS, NT, :], xs).then_inc(x_in[NT], 16)
        sp.dma_start(xt[NS:NS + NM, NT, :], meta).then_inc(x_in[NT], 16)
        cols = [W_FQ, W_FK, W_FV, W_RV]

        def strip_units(u, c):
            for j in range(2):
                load_unit(sp, u + j, win[:, 4 * j:4 * j + 4, c])

        load_unit(sp, At(U_FF), win[:, :, W_FF:W_FF + P])
        sp.dma_start(bfT[:], b_forget.rearrange("a h -> h a")).then_inc(bf_in, 16)
        strip_units(At(U_STRIP + 2), slice(W_FQ + 256, W_FQ + 512))
        sp.wait_ge(a_lo, A_NORM1)
        for dst, src in ((crow[:], clf.rearrange("(c p) h -> p c h", p=P)), (gq[:], q_norm_g[0].partition_broadcast(P)),
                         (gk[:], k_norm_g[0].partition_broadcast(P)), (cosT[:], c_cos), (sinT[:], c_sin)):
            sp.dma_start(dst, src).then_inc(small_in, 16)
        for s in range(2, 4):
            strip_units(At(U_STRIP + 2 * s), slice(W_FQ + 256 * s, W_FQ + 256 * s + 256))
        for kind in range(1, 4):
            with sp.Fori(0, 2) as i:
                for s in range(2):
                    strip_units(At(U_STRIP + 8 * kind + 2 * s, 4, i), bass.ds(i * 512 + (cols[kind] + 256 * s), 256))
        def load_qk(h):
            hc = bass.ds(h.times(P), P)
            for dst, src in ((qrow[:], pq[NM:, hc].rearrange("(i p) d -> p i d", p=P)), (qsrow[:], sq[:, hc]),
                             (krow[:], pk[NM:, hc].rearrange("(i p) d -> p i d", p=P)), (kmrow[:], pk[0:NM, hc]),
                             (ksrow[:], sk[:, hc]), (kcrow[:], ck[:, hc].rearrange("(i p) d -> p i d", p=P))):
                sp.dma_start(dst, src).then_inc(ld_qk, 16)

        def load_v(h):
            hc = bass.ds(h.times(P), P)
            for dst, src in ((vrow[:], pv[NM:, hc].rearrange("(i p) d -> p i d", p=P)), (vmrow[:], pv[0:NM, hc]),
                             (vsrow[:], sv[:, hc]), (vcrow[:], cv[:, hc].rearrange("(i p) d -> p i d", p=P))):
                sp.dma_start(dst, src).then_inc(ld_v, 16)
            row = negc[bass.ds(h.v, 1), :].rearrange("a n -> (a n)")
            sp.dma_start(ncr[:], row.partition_broadcast(P)).then_inc(ld_n, 16)

        def turn_unit(h, q):
            load_unit(sp, At(U_TURN + 3 * h.first + q, 3 * h.step, h.i),
                      win[:, :, bass.ds(h.times(P, (W_RQ, W_RG, W_GA)[q]), P)])

        sp.wait_ge(stored, 8 * ST_STRIP)
        sp.wait_ge(lf_st, 64)
        load_qk(At(0))
        turn_unit(At(0), 0)
        turn_unit(At(0), 1)
        sp.wait_ge(stored, 12 * ST_STRIP)
        load_v(At(0))
        turn_unit(At(0), 2)

        def next_head(h):
            turn_unit(h + 1, 0)
            turn_unit(h + 1, 1)
            sp.wait_ge(s_done, h.times(9, 1))
            load_qk(h + 1)
            turn_unit(h + 1, 2)
            sp.wait_ge(o_done, h.times(9, 9))
            load_v(h + 1)

        with sp.Fori(0, FH // 2 - 1) as i:
            for b in range(2):
                next_head(At(b, 2, i))
        next_head(At(FH - 2))
        def branch_unit(x):
            w, q = ((win, x), (wfo, x - 8), (wro, x - 16))[x // 8]
            c = q * P + (W_GB if w is win else 0)
            load_unit(sp, At(U_GB + x), w[:, :, c:c + P])

        def load_gate(x, kind):
            sp.wait_ge(bank_free, N_FOX + 3 * (x - 1))
            sp.dma_start(stage[:, x % 2, 0:TOUT], gates[3 * (x % 8) + kind]).then_inc(g_in[x % 2], 16)

        def load_ret_qk(r):
            for dst, src in ((rqT[:], rot[r]), (rkT[:], rot[RH + r]), (dec[:], c_decay[r])):
                sp.dma_start(dst, src).then_inc(ld_r, 16)

        def load_ret_v(r):
            c = slice(r * RV, r * RV + RV)
            for dst, src in ((rvrow[:], prv[NM:, c].rearrange("(i p) d -> p i d", p=P)), (rvm[:], prv[0:NM, c]),
                             (rvs[:], srv[:, c])):
                sp.dma_start(dst, src).then_inc(ld_rv, 16)

        def load_ret_gate(r):
            for dst, src in ((s0s[:], st_in[r]), (rgT[:, 0, :], gates[6 * r]), (rgT[:, 1, :], gates[6 * r + 3])):
                sp.dma_start(dst, src).then_inc(ld_s, 16)

        for x in range(2):
            branch_unit(x)
        sp.wait_ge(stored, ST_TURN + 64 * 7)
        load_ret_qk(0)
        sp.dma_start(gnT[:], ret_gn_g.rearrange("a (k p) -> p (a k)", p=P), allow_slow_non_contiguous=True).then_inc(ld_g, 16)
        branch_unit(2)
        sp.wait_ge(s_done, 9 * (FH - 1) + 1)
        load_ret_v(0)
        branch_unit(3)
        sp.wait_ge(stored, ST_GB)
        load_ret_gate(0)
        for r in range(RH):
            fox = r >= 2
            x = 4 * r
            if r:
                branch_unit(x + 3)
            if r == 2:
                sp.wait_ge(stored, ST_RET)
            if fox:
                load_gate(x - 7, 2)
            branch_unit(x + 4)
            if fox:
                load_gate(x - 6, 2)
            branch_unit(x + 5)
            if r == 0:
                for k in range(KC):
                    sp.dma_start(mT[:, k, :], foxT[k]).then_inc(f_in, 16)
            if fox:
                load_gate(x - 5, 2)
            sp.wait_ge(r_bd, NCH * (r + 1))
            if r + 1 < RH:
                load_ret_qk(r + 1)
                load_ret_v(r + 1)
            else:
                for k in range(6):
                    sp.dma_start(ret_rows[k], retT[k]).then_inc(ar_in, 16)
            branch_unit(x + 6)
            if r == 1:
                sp.wait_ge(stored, ST_RET - 16)
            if fox or r == 1:
                load_gate(x - 4, 2 if r < 3 else 1)
            if r + 1 < RH:
                sp.wait_ge(r_sto, 64 * (r + 1))
                load_ret_gate(r + 1)
        load_gate(9, 1)

        def load_x(s):
            c = slice(256 * s, 256 * s + 256)
            sp.dma_start(xrow[:, s % 2, 0:NT, :], xp[:, c].rearrange("(i p) d -> p i d", p=P)).then_inc(x2_in[s % 2], 16)
            sp.dma_start(xrow[0:NS, s % 2, NT, :], xs[:, c]).then_inc(x2_in[s % 2], 16)

        def wo_units(s):
            for j in range(2):
                load_unit(sp, At(U_WO + 2 * s + j), wout[:, 4 * j:4 * j + 4, 256 * s:256 * s + 256])

        for q in range(5):
            branch_unit(19 + q)
            load_gate(10 + q, 1)
            if q == 1:
                sp.wait_ge(a_lo, A_RET)
                sp.dma_start(g2[:], norm2_g[0].partition_broadcast(P)).then_inc(g2_in, 16)
                load_x(0)
                load_x(1)
        load_gate(15, 1)
        for s in range(3):
            wo_units(s)
        sp.wait_ge(bank_free, N_WO + NQ)
        load_x(2)
        wo_units(3)
        sp.wait_ge(bank_free, N_WO + 2 * NQ)
        load_x(3)

        with sp.Fori(0, 8) as g:
            for q in range(4):
                load_unit(sp, At(U_MLP + q, 8, g), wf1[:, :, bass.ds(g * 512 + q * P, P)])
            for q in range(4):
                load_unit(sp, At(U_MLP + 4 + q, 8, g), wf2[:, bass.ds(g * 4, 4), 256 * q:256 * q + 256])

        sp.wait_ge(h_st, 128)
        sp.wait_ge(a_lo, A_NORM2)

        def hload(i):
            n = P if i < NT else NS
            sp.dma_start(hback[0:n, i % 2, :], hrow[i * P:i * P + n, :]).then_inc(hb_in[i % 2], 16)

        hload(0)
        hload(1)
        for i in range(NQ):
            sp.wait_ge(y_rd, 2 * i + 2)
            n = P if i < NT else NS
            sp.dma_start(yp[i * P:i * P + P, :] if i < NT else ys, yout[0:n, i % 2, :]).then_inc(y_st[i % 2], 16)
            if i + 2 < NQ:
                hload(i + 2)
        sp.wait_ge(y_st[0], 16 * 5)
        sp.wait_ge(y_st[1], 16 * 4)
        sp.wait_ge(lf_st, 64)
        sp.wait_ge(stored, ST_RET)
        sp.wait_ge(r_sto, RH * 64)

    @block.gpsimd
    def _(pool):
        nc.gpsimd.memset(xt[:, NT, :], 0.0).then_inc(pad_ok, 1)

        def store_strip(s, prompt, sample, c, normed, n=None):
            if normed:
                pool.wait_ge(strip_ok, (s + 1).v)
            else:
                pool.wait_ge(bank_free, (n + NQ).v)
            src = rows[:, s.mod(2)]
            pool.dma_start(prompt[NM:, c].rearrange("(i p) d -> p i d", p=P), src[:, 0:NT, :]).then_inc(stored, 16)
            pool.wait_ge(stored, s.times(ST_STRIP, 16))
            pool.dma_start(sample[:, c], src[0:NS, NT, :]).then_inc(stored, 16)
            pool.dma_start(prompt[0:NM, c], src[NS:NS + NM, NT, :]).then_inc(stored, 16)
            pool.wait_ge(stored, s.times(ST_STRIP, ST_STRIP))

        def store_logf():
            pool.wait_ge(s_read, 1)
            pool.dma_start(negc, ncum[:]).then_inc(lf_st, 16)
            pool.wait_ge(lf_r, 1)
            pool.dma_start(plf[NM:, :].rearrange("(i p) h -> p i h", p=P), lfr[:, 0:NT, :]).then_inc(lf_st, 16)
            pool.dma_start(slf, lfr[0:NS, NT, :]).then_inc(lf_st, 16)
            pool.dma_start(plf[0:NM, :], lfr[NS:NS + NM, NT, :]).then_inc(lf_st, 16)
            pool.wait_ge(lf_st, 64)

        for s in range(4):
            store_strip(At(s), pq, sq, slice(256 * s, 256 * s + 256), True)
            if s == 0:
                store_logf()
        for kind, (p_rows, s_rows) in ((1, (pk, sk)), (2, (pv, sv)), (3, (prv, srv))):
            with pool.Fori(0, 2) as i:
                for s in range(2):
                    store_strip(At(4 * kind + s, 2, i), p_rows, s_rows, bass.ds(i * 512 + 256 * s, 256), kind == 1,
                                At(N_STRIP + NQ * (4 * kind + s), 2 * NQ, i))
        def row_of(x, h, m=1, k=0):
            return x[bass.ds(h.times(m, k), 1)].rearrange("a p n -> (a p) n")

        with pool.Fori(0, FH // 2) as i:
            for b in range(2):
                h = At(b, 2, i)
                pool.wait_ge(unit_v, h.times(1, 1))
                pool.dma_start(row_of(rot, h), stage[:, b, :]).then_inc(stored, 16)
                pool.wait_ge(stored, h.times(64, ST_TURN + 16))
                pool.wait_ge(bank_free, h.times(9, N_TURN + 6))
                pool.dma_start(row_of(gates, h, 3, 0), stage[:, 1 - b, 0:TOUT]).then_inc(stored, 16)
                pool.wait_ge(stored, h.times(64, ST_TURN + 32))
                pool.wait_ge(o_read, h.times(9, O0 + 9))
                pool.dma_start(row_of(foxT, h), fst[:]).then_inc(stored, 16)
                pool.wait_ge(stored, h.times(64, ST_TURN + 48))
                pool.wait_ge(bank_free, h.times(9, N_TURN + 9))
                pool.dma_start(row_of(gates, h, 3, 1), stage[:, b, 0:TOUT]).then_inc(stored, 16)
                pool.wait_ge(stored, h.times(64, ST_TURN + 64))
        nc.gpsimd.memset(yraw[:, NT, :], 0.0)
        nc.gpsimd.memset(bns[:, NT, :], 1.0).then_inc(yz_ok, 1)

        def ret_head(r, gb):
            def store_gb(q):
                pool.wait_ge(bank_free, r.times(12, N_GB + 3 * q + 3))
                pool.dma_start(row_of(gates, r, 12, 3 * q + 2), stage[:, q % 2, 0:TOUT]).then_inc(stored, 16)
                pool.wait_ge(stored, r.times(64, ST_GB + 16 * q + 16))

            if gb:
                store_gb(0)
                store_gb(1)
            pool.wait_ge(r_bd, r.times(NCH, NCH))
            pool.dma_start(row_of(pst, r), state[:]).then_inc(r_sto, 16)
            pool.dma_start(row_of(sst, r), s0s[:]).then_inc(r_sto, 16)
            pool.wait_ge(r_sto, r.times(64, 32))
            if gb:
                store_gb(2)
            pool.wait_ge(r_tr, r.times(5, 5))
            for e in range(2):
                pool.dma_start(row_of(retT, r, 2, e), rgT[:, e, :]).then_inc(r_sto, 16)
            pool.wait_ge(r_sto, r.times(64, 64))
            if gb:
                store_gb(3)

        for half in range(2):
            with pool.Fori(0, 2) as i:
                ret_head(At(2 * half, 1, i), half == 0)
        pool.wait_ge(a_lo, A_M)
        nc.gpsimd.memset(hsb[:, NT, :], 0.0).then_inc(hz_ok, 1)
        for s in range(4):
            c = slice(256 * s, 256 * s + 256)
            pool.wait_ge(bank_free, N_WO + NQ * (s + 1))
            pool.dma_start(hrow[0:SEQ, c].rearrange("(i p) d -> p i d", p=P), hsb[:, 0:NT, c]).then_inc(h_st, 16)
            pool.dma_start(hrow[SEQ:, c], hsb[0:NS, NT, c]).then_inc(h_st, 16)
            pool.wait_ge(h_st, 32 * (s + 1))
        pool.wait_ge(v_norm, 2 * NQ)
        nc.gpsimd.memset(yT[:], 0.0).then_inc(y_zero, 1)

    @block.tensor
    def _(pe):
        pe.wait_ge(const_in, 48)
        for i in range(4):
            turn_rows_pe(pe, xn, i, 0, 0)
        pe.wait_ge(w_lo_s, 2)
        for i in range(NQ):
            if i + 4 < NQ:
                turn_rows_pe(pe, xn, i + 4, 0, 0)
            pe.wait_ge(a_lo, 2 * i + 2)
            strip_step(pe, At(i), At(0), i)
        pe.wait_ge(w_lo_s, U_FF + 1)
        for j, (c, w) in enumerate(T3):
            turned_step(pe, At(N_FF + j), U_FF % 4, c, w)

        def strip(u, n):
            pe.wait_ge(w_lo_s, (u + 2).v)
            for i in range(NQ):
                strip_step(pe, n + i, u, i)

        def logf_turns():
            pe.wait_ge(small_in, 80)
            for c in range(NC):
                mm = nc.tensor.transpose(pt[0:FH, 0, c * P:c * P + P], crow[:, c, :], ident[:])
            mm.then_inc(t_done[0], 1)
            pe.wait_ge(lf_ok, 1)
            for i in range(NQ):
                w = P if i < NT else NS + NM
                mm = nc.tensor.transpose(pt[0:w, 1, FH * i:FH * i + FH], lf[:, i * P:i * P + w], ident[0:FH, 0:FH])
            mm.then_inc(t_done[1], 1)

        for s in range(1, 4):
            strip(At(U_STRIP + 2 * s), At(N_STRIP + NQ * s))
            if s == 1:
                logf_turns()
        for kind in range(1, 4):
            with pe.Fori(0, 2) as i:
                for s in range(2):
                    strip(At(U_STRIP + 8 * kind + 2 * s, 4, i), At(N_STRIP + NQ * (4 * kind + s), 2 * NQ, i))
        T_READ0 = (1, 1)
        pe.wait_ge(const_ok, 1)

        def tgroup(h, g):
            j, blocks, bank = GROUPS[g]
            pe.wait_ge(t_read[bank], h.times(PER_BANK[bank], T_READ0[bank] + nth(g)))
            if j < 0:
                for src, c, n in turn_prologue(blocks)[0]:
                    mm = nc.tensor.transpose(pt[:, bank, c:c + n], src, ident[0:n, 0:n])
            else:
                for x, b in enumerate(blocks):
                    c, k = prob_block(j, b)
                    m, o = (NS, P + (x - 1) * NS) if j == NT and x else (P, x * P)
                    mm = nc.tensor.transpose(pt[0:k, bank, o:o + m], prob[0:m, j % 2, c:c + k], ident[0:m, 0:m])
            mm.then_inc(t_done[bank], 1)

        def turned_before(h, g):
            for b in range(2):
                pe.wait_ge(t_read[b], h.times(PER_BANK[b], T_READ0[b] + sum(x[2] == b for x in GROUPS[:g])))

        def scores(h, j):
            pe.wait_ge(s_read, h.times(9, S0 + j))
            if j == 0:
                turned_before(h, 6)
            if j < NT:
                n = NM + P * (j + 1)
                for a in range(0, n, 512):
                    b = min(n, a + 512)
                    d0 = max(a, n - P)
                    mm = nc.tensor.matmul(ps[:, a:b], qT[:, j * P:j * P + P], kT[:, a:b], start=True, stop=(d0 >= b))
                    if d0 < b:
                        mm = nc.tensor.matmul(ps[:, d0:b], identr[:], maskr[:, d0 - n + P:b - n + P], start=False, stop=True)
            else:
                q = qT[:, SEQ:TOUT]
                nc.tensor.matmul(ps[0:NS, 0:512], q, kcT[:], start=True, stop=True)
                nc.tensor.matmul(ps[0:NS, 512:512 + NS], q, kT[:, NKEY:NKEY + NS], start=True, stop=False)
                mm = nc.tensor.matmul(ps[0:NS, 512:512 + NS], ident[:, 0:NS], maskr[:, 0:NS].bitcast(F32), start=False, stop=True)
            mm.then_inc(s_done, 1)

        def turn_probs(h, j):
            pe.wait_ge(p_done, h.times(9, j + 1))
            for g in step_groups(j)[:2]:
                tgroup(h, g)

        def weigh(h, j):
            gs = step_groups(j)
            for g in gs[2:]:
                tgroup(h, g)
            early = [b for g in gs[:2] for b in GROUPS[g][1]]
            turned_before(h, gs[:2][-1] + 1)
            if j == 0:
                pe.wait_ge(ld_v, h.times(64, 64))
            pe.wait_ge(o_read, h.times(9, O0 + j))
            w = NS if j == NT else P
            if j == NT:
                parts = [(b, vcrow[:, b, :], pT[:, b, 0:w]) for b in range(NC)] + [(NC, vsrow[:], pT[0:NS, NC, 0:w])]
            else:
                parts = [(b, vrow[:, b, :], pT[:, b, 0:w]) for b in range(j + 1)] + [(NT, vmrow[:], pT[0:NM, NT, 0:w])]
            for x, (b, v, p) in enumerate(parts):
                if b not in early and parts[x - 1][0] in early:
                    turned_before(h, gs[-1] + 1)
                mm = nc.tensor.matmul(po[:, 0:w], v, p, start=(x == 0), stop=(x == len(parts) - 1))
            mm.then_inc(o_done, 1)

        def piece(h, p):
            x, j = p // 9, p // 3 % 3
            c, w = (T3 if x == 0 else O3)[j]
            u = At(U_TURN + 3 * h.first + x, 3 * h.step, h.i)
            if p % 9 == 0:
                pe.wait_ge(w_lo_s, (u + 1).v)
            turned_piece(pe, At(N_TURN + 9 * h.first + p // 3, 9 * h.step, h.i), ring(u), c, w, p % 3)

        with pe.Fori(0, FH // 2) as i:
            for b in range(2):
                h = At(b, 2, i)
                pe.wait_ge(ld_qk, h.times(96, 96))
                for g in range(6):
                    tgroup(h, g)
                    piece(h, g)
                scores(h, 0)
                for p in range(6, 9):
                    piece(h, p)
                for j in range(1, 9):
                    scores(h, j)
                    piece(h, 7 + 2 * j)
                    turn_probs(h, j - 1)
                    piece(h, 8 + 2 * j)
                    weigh(h, j - 1)
                piece(h, 25)
                turn_probs(h, 8)
                piece(h, 26)
                weigh(h, 8)
        def ret_a(r, c):
            c0, m = CH[c]
            if c:
                pe.wait_ge(r_ad, r.times(NCH, c))
                nc.tensor.matmul(ps[0:m, 0:m], rkT[:, c0:c0 + m], rqT[:, c0:c0 + m], start=True, stop=True)
            nc.tensor.transpose(pt[0:m, 0, 0:P], rkT[:, c0:c0 + m], ident[:]).then_inc(r_a, 1)

        def ret_b(r, c):
            c0, m = CH[c]
            pe.wait_ge(r_ad, r.times(NCH, c + 1))
            if c:
                pe.wait_ge(r_bd, r.times(NCH, c))
            v = rvm[:] if c == 0 else (rvs[:] if c == NCH - 1 else rvrow[:, c - 1, :])
            mm = nc.tensor.matmul(ps[:, 1024:1024 + RV], kd[0:m, c % 2, :], v, start=True, stop=True)
            if c == 0:
                mm.then_inc(r_b, 1)
            else:
                st = s0s if c == NCH - 1 else state
                nc.tensor.matmul(ps[0:m, 512:512 + RV], sTd[0:m, c % 2, 0:m], v, start=True, stop=False)
                nc.tensor.matmul(ps[0:m, 512:512 + RV], qg[:, c % 2, 0:m], st[:], start=False, stop=True).then_inc(r_b, 1)

        def ret_piece(r, fox, p):
            x, (c, w) = p // 9, O3[p // 3 % 3]
            if fox and p in (0, 3, 6):
                pe.wait_ge(a_lo, A_NORM1 + KC * (p // 3 + 1))
            if p % 9 == 0:
                pe.wait_ge(w_lo_s, r.times(4, U_GB + x + 1))
            turned_piece(pe, At(N_GB + 12 * r.first + p // 3, 12 * r.step, r.i), (U_GB + x) % 4, c, w, p % 3)

        def ret_head(r, fox):
            pe.wait_ge(ld_r, r.times(48, 48))
            ret_a(r, 0)
            ret_piece(r, fox, 0)
            for c in range(1, NCH):
                ret_a(r, c)
                ret_piece(r, fox, 2 * c - 1)
                if c == 1:
                    pe.wait_ge(ld_rv, r.times(48, 48))
                ret_b(r, c - 1)
                ret_piece(r, fox, 2 * c)
            pe.wait_ge(ld_s, r.times(48, 48))
            ret_b(r, NCH - 1)
            for p in range(19, 27):
                ret_piece(r, fox, p)
            pe.wait_ge(r_n, r.times(1, 1))
            for q, (e, tiles) in enumerate(RT_GROUPS):
                if q >= 2:
                    pe.wait_ge(r_tr, r.times(5, q - 1))
                for x, (ee, i, w) in enumerate(tiles):
                    mm = nc.tensor.transpose(pt[:, q % 2, P * x:P * x + w], yraw[0:w, i, ee * P:ee * P + P], ident[0:w, 0:w])
                mm.then_inc(r_t, 1)
                ret_piece(r, fox, 27 + q)
            for p in range(32, 36):
                ret_piece(r, fox, p)
            pe.wait_ge(r_tr, r.times(5, 5))

        for half in range(2):
            with pe.Fori(0, 2) as i:
                ret_head(At(2 * half, 1, i), half == 1)

        with pe.Fori(0, 2) as i:
            for q in range(4):
                pe.wait_ge(w_lo_s, At(U_RET + q + 1, 4, i).v)
                for j, (c, w) in enumerate(O3):
                    if q == 0:
                        pe.wait_ge(a_lo, A_FOX + KC * (j + 1))
                    turned_step(pe, At(N_RET + 3 * q + j, 12, i), (U_RET + q) % 4, c, w)
        for s in range(4):
            u, n = At(U_WO + 2 * s), At(N_WO + NQ * s)
            pe.wait_ge(w_lo_s, (u + 2).v)
            for i in range(NQ):
                pe.wait_ge(a_lo, A_RET + KC * (third_of(i) + 1))
                strip_step(pe, n + i, u, i)
                if s == 3 and i >= 4:
                    turn_rows_pe(pe, hn, i - 4, A_M, NQ)

        def ff1(g, q, j):
            c, w = O3[j]
            if j == 0:
                pe.wait_ge(w_lo_s, g.times(8, U_MLP + q + 1))
            turned_step(pe, At(N_MLP + G_N * g.first + 3 * q + j, G_N * g.step, g.i), (U_MLP + q) % 4, c, w)

        def ff2(g, q, m, j, step):
            c, w = O3[j]
            turned_step(pe, At(N_MLP + G_N * g.first + 12 + step, G_N * g.step, g.i), (U_MLP + q) % 4, c, w,
                        hi=uh, lo=ul, kc=4, m0=m * P)

        def group(g, first_unit=True):
            for q in range(0 if first_unit else 1, 4):
                for j in range(3):
                    ff1(g, q, j)
            for q in range(4):
                pe.wait_ge(w_lo_s, g.times(8, U_MLP + 5 + q))
                for m in range(2):
                    for j in range(3):
                        if q == 0 and m == 0:
                            pe.wait_ge(u_lo, g.times(12, 10 + j))
                        ff2(g, q, m, j, 6 * q + 3 * m + j)

        for j in range(3):
            for i in ((5,), (6, 7), (8,))[j]:
                turn_rows_pe(pe, hn, i, A_M, NQ)
            pe.wait_ge(a_lo, A_M + 2 * (third_last(j) + 1))
            ff1(At(0), 0, j)
        group(At(0), False)
        with pe.Fori(0, 6) as i:
            group(At(1, 1, i))

        def turn_y(i):
            w = P if i < NT else NS
            pe.wait_ge(bank_free, N_MLP + 7 * G_N + 12 + 8 * (third_of(i) + 1))
            for g in range(2):
                if i:
                    pe.wait_ge(y_rd, 2 * i + g - 1)
                for c in range(4):
                    mm = nc.tensor.transpose(pt[0:w, g, c * P:c * P + P], yT[:, 4 * g + c, i * P:i * P + w], ident[:])
                mm.then_inc(t_done[g], 1)

        for q in range(4):
            for j in range(3):
                ff1(At(7), q, j)
        for j in range(3):
            pe.wait_ge(u_lo, 7 * 12 + 10 + j)
            for q in range(4):
                pe.wait_ge(w_lo_s, U_END - 3 + q)
                for m in range(2):
                    ff2(At(7), q, m, j, 8 * j + 2 * q + m)
                if q:
                    for i in LAST_TURNS[j][q - 1]:
                        turn_y(i)
        for i in range(5, NQ):
            turn_y(i)

    @block.scalar
    def _(act):
        def square1(i):
            act.wait_ge(x_in[i], 16 if i < NT else 32)
            wait(act, a_ssq, i - 1)
            nc.scalar.activation(xsq[:, i % 2, :], xt[:, i, :], ACT.Square, accum_out=stat[:, 0, i:i + 1]).then_inc(a_ssq, 1)

        def root1(b):
            act.wait_ge(ms_ok, b + 1)
            nc.scalar.activation(stat[:, 2, 3 * b:3 * b + 3], stat[:, 1, 3 * b:3 * b + 3], ACT.Sqrt).then_inc(a_root, 1)

        for i in range(3):
            square1(i)
        root1(0)
        square1(3)
        turn_rows_act(act, 0, (0, 0))
        square1(4)
        turn_rows_act(act, 1, (0, 0))
        square1(5)
        root1(1)
        square1(6)
        turn_rows_act(act, 2, (0, 0))
        split_hi(act, At(0), At(0))
        split_hi(act, At(1), At(0))
        square1(7)
        turn_rows_act(act, 3, (0, 0))
        square1(8)
        turn_rows_act(act, 4, (0, 0))
        root1(2)
        for i in range(5, NQ):
            turn_rows_act(act, i, (0, 0))
        split_hi(act, At(U_FF), At(0))
        split_hi(act, At(U_STRIP + 2), At(0))
        split_hi(act, At(U_STRIP + 3), At(N_FF))

        def log_gates():
            act.wait_ge(lf_raw, 1)
            nc.scalar.activation(lfc[:, 0, :], lfc[:, 1, :], ACT.Exp, scale=-1.0).then_inc(e_done, 1)
            act.wait_ge(e_done, 1)
            nc.scalar.activation(lfc[:, 1, :], lfc[:, 0, :], ACT.Ln, bias=1.0).then_inc(lf_e, 1)

        def logf_rows():
            act.wait_ge(t_done[1], NQ + 1)
            nc.scalar.copy(lfr[:, 0:NT, :], pt[:, 1, 0:NT * FH].rearrange("p (i h) -> p i h", h=FH)).then_inc(t_read[1], 1)
            nc.scalar.copy(lfr[0:NS + NM, NT, :], pt[0:NS + NM, 1, NT * FH:NQ * FH]).then_inc(lf_r, 1)

        def strip(s, root, squares):
            u, n = At(U_STRIP + 2 * s.first, 2 * s.step, s.i), At(N_STRIP + NQ * s.first, NQ * s.step, s.i)
            for j in range(2):
                split_hi(act, u + 2 + j, n)
            if root:
                act.wait_ge(ssq_v, s.v)
                nc.scalar.activation(stat[:, 2, :], stat[:, 1, :], ACT.Sqrt).then_inc(a_root, 1)
            if squares:
                head_squares(s, n)

        def head_squares(s, n):
            for i in range(NQ):
                act.wait_ge(bank_free, (n + i + 1).v)
                for e in range(2):
                    ins = nc.scalar.activation(junk[:, 2 * i + e, :], rows[:, s.mod(2), i, e * P:e * P + P], ACT.Square,
                                               accum_out=stat[:, 0, 2 * i + e:2 * i + e + 1])
            ins.then_inc(ssq2, 1)

        head_squares(At(0), At(0))
        log_gates()
        strip(At(1), True, True)
        logf_rows()
        with act.Fori(0, 3) as i:
            for s in range(2):
                strip(At(2 + s, 2, i), True, True)
        strip(At(8), True, False)
        strip(At(9), False, False)
        with act.Fori(0, 3) as i:
            for s in range(2):
                strip(At(10 + s, 2, i), False, False)

        def exps(h, j):
            act.wait_ge(m_done, h.times(9, j + 1))
            m, n = (P, NM + P * (j + 1)) if j < NT else (NS, NPAST + NS)
            nc.scalar.activation(prob[0:m, j % 2, 0:n], prob[0:m, j % 2, 0:n], ACT.Exp, bias=mx[0:m, j % 2:j % 2 + 1],
                                 accum_out=lsum[0:m, j % 2:j % 2 + 1]).then_inc(e_done, 1)

        def reads(h, gs):
            for g in gs:
                if GROUPS[g][2] == 1:
                    act.wait_ge(t_done[1], h.times(PER_BANK[1], T_ATT[1] + nth(g) + 1))
                    read_group(lambda o, i_: nc.scalar.copy(o, i_), g).then_inc(t_read[1], 1)

        def turn_split(h, x):
            split_hi(act, At(U_TURN + 3 * h.first + x, 3 * h.step, h.i),
                     At(N_TURN + 9 * h.first + 3 * x - 6, 9 * h.step, h.i))

        with act.Fori(0, FH // 2) as i:
            for b in range(2):
                h = At(b, 2, i)
                reads(h, range(6))
                exps(h, 0)
                for j in range(1, 9):
                    reads(h, step_groups(j - 1))
                    exps(h, j)
                    if j in (2, 4, 6):
                        turn_split(h, {2: 2, 4: 3, 6: 4}[j])
                reads(h, step_groups(8))
        def open_gate(x, i=None, step=0):
            act.wait_ge(g_in[x % 2], At(16 * (x // 2 + 1), 8 * step, i).v)
            nc.scalar.activation(stage[:, x % 2, 0:TOUT], stage[:, x % 2, 0:TOUT], ACT.Sigmoid).then_inc(g_ok, 1)

        def ret_head(r, fox):
            def split(x):
                split_hi(act, At(U_GB + 4 * r.first + x, 4, r.i), At(N_GB + 12 * r.first + 3 * x - 6, 12, r.i))

            split(2)
            if fox:
                open_gate(0, r.i, 4)
                open_gate(1, r.i, 4)
            act.wait_ge(ld_s, r.times(48, 48))
            nc.scalar.activation(rgT[:], rgT[:], ACT.Silu).then_inc(r_g, 1)
            split(3)
            if fox:
                open_gate(2, r.i, 4)
            split(4)
            act.wait_ge(r_v, r.times(1, 1))
            nc.scalar.activation(stat[:, 2, 0:NQ], stat[:, 1, 0:NQ], ACT.Sqrt).then_inc(a_root, 1)
            if fox:
                open_gate(3, r.i, 4)
            split(5)

        with act.Fori(0, 2) as i:
            ret_head(At(0, 1, i), False)
        act.wait_ge(f_in, 16 * KC)
        for j in range(3):
            act.wait_ge(mm_done, N_FOX - 2 + j)
            resplit_hi(j, m_rows)
        with act.Fori(0, 2) as i:
            ret_head(At(2, 1, i), True)
        act.wait_ge(ar_in, 16 * 6)
        act.wait_ge(r_tr, 5 * RH)
        for j in range(3):
            act.wait_ge(mm_done, N_RET - 2 + j)
            resplit_hi(j, ret_rows)
        with act.Fori(0, 2) as i:
            for q in range(4):
                open_gate(8 + q, i, 4)
                split_hi(act, At(U_RET + q + 2, 4, i), At(N_RET + 3 * q, 12, i))
        for j in range(3):
            act.wait_ge(mm_done, N_WO - 2 + j)
            act.wait_ge(m_ok, 3 * KC - 2 + j)
            resplit_hi(j, m_rows)
        for s in range(4):
            for j in range(2):
                split_hi(act, At(U_WO + 2 * s + 2 + j), At(N_WO + NQ * s))

        def root3(b):
            act.wait_ge(r_v, RH + 1 + b)
            nc.scalar.activation(stat[:, 2, 3 * b:3 * b + 3], stat[:, 1, 3 * b:3 * b + 3], ACT.Sqrt).then_inc(a_root, 1)

        for i in range(NQ):
            act.wait_ge(bank_free, N_WO + 3 * NQ + i + 1)
            wait(act, a_ssq, NQ + i - 1)
            nc.scalar.activation(hsq[:, i % 2, :], hsb[:, i, :], ACT.Square, accum_out=stat[:, 0, i:i + 1]).then_inc(a_ssq, 1)
            if i in (3, 6):
                root3(i // 3 - 1)
            if i >= 4:
                turn_rows_act(act, i - 4, T_NORM2)
        root3(2)
        for i in range(5, NQ):
            turn_rows_act(act, i, T_NORM2)

        def mlp_group(g, tail):
            for q in range(4):
                split_hi(act, At(U_MLP + q + 2, 8, g), At(N_MLP + 3 * q, G_N, g))
                for j, (c, w) in enumerate(O3):
                    n = At(N_MLP + 3 * q + j, G_N, g)
                    act.wait_ge(mm_done, (n + 1).v)
                    par = (3 * q + j) % 2
                    nc.scalar.activation(relu[:, par, 0:w], pd[:, n.mod(NB), 0:w], ACT.Relu).then_inc(u_relu, 1)
                    act.wait_ge(bank_free, (n + 1).v)
                    nc.scalar.copy(uh[:, q, c:c + w], usq[:, par, 0:w]).then_inc(u_hi, 1)
            if tail:
                for q in range(2):
                    split_hi(act, At(U_END - 2 + q), At(N_MLP + 7 * G_N + 9 + 3 * q))
                return
            for q in range(4):
                split_hi(act, At(U_MLP + 6 + q, 8, g), At(N_MLP + 12 + 6 * q, G_N, g))

        with act.Fori(0, 7) as g:
            mlp_group(g, False)
        mlp_group(7, True)

    @block.vector
    def _(dve):
        ch = [At(0)]
        dve.wait_ge(const_in, 48)
        nc.vector.tensor_copy(identr[:], ident[:])
        nc.vector.tensor_copy(maskr[:], maskf[:]).then_inc(const_ok, 1)
        def norm1_batch(b):
            dve.wait_ge(a_ssq, 3 * b + 3)
            c = slice(3 * b, 3 * b + 3)
            nc.vector.tensor_scalar(stat[:, 1, c], stat[:, 0, c], 1.0 / D, EPS, ALU.mult, ALU.add).then_inc(ms_ok, 1)
            dve.wait_ge(a_root, b + 1)
            root_end(dve, 3, 1.0, ch, 3 * b)

        def norm_row(i, src, dst, gain, t_base):
            if i >= 2:
                for g in range(2):
                    dve.wait_ge(t_done[g], t_base[g] + i - 1)
            nc.vector.scalar_tensor_tensor(dst[:, i % 2, :], src[:, i, :], stat[:, 5, i:i + 1], gain[:],
                                           ALU.mult, ALU.mult).then_inc(v_norm, 1)

        def forget_read(j):
            c, w = T3[j]
            dve.wait_ge(bf_in, 16)
            dve.wait_ge(mm_done, N_FF + j + 1)
            nc.vector.tensor_scalar(lf[:, c:c + w], pd[0:FH, (N_FF + j) % NB, 0:w], bfT[:, 0:1], None, ALU.add).then_inc(bank_free, 1)

        def strip_read(s, n, i):
            dve.wait_ge(mm_done, (n + i + 1).v)
            nc.vector.tensor_copy(rows[:, s.mod(2), i, :], pd[:, (n + i).mod(NB), 0:256]).then_inc(bank_free, 1)

        for i in range(NQ):
            if i % 3 == 0:
                norm1_batch(i // 3)
            norm_row(i, xt, xn, g1, (0, 0))
            if i:
                turn_rows_dve(dve, i - 1, 0)
            if i == 3:
                split_lo(dve, At(0))
                split_lo(dve, At(1))
            if i >= 5:
                strip_read(At(0), At(0), i - 5)
        turn_rows_dve(dve, NQ - 1, 0)
        for i in range(4, NQ):
            strip_read(At(0), At(0), i)
            if i in (6, 7):
                split_lo(dve, At(i - 4))
        forget_read(0)
        split_lo(dve, At(U_STRIP + 3))
        forget_read(1)
        forget_read(2)
        dve.wait_ge(bank_free, N_FF + 3)
        nc.vector.scalar_tensor_tensor(lfc[:, 1, :], lf[:], -1.0, lf[:], ALU.mult, ALU.max).then_inc(lf_raw, 1)

        def logf_rest():
            dve.wait_ge(small_in, 80)
            dve.wait_ge(lf_e, 1)
            link(dve, nc.vector.memset(lfc[:, 0, :], 1.0), ch)
            nc.vector.scalar_tensor_tensor(lf[:], lf[:], 0.0, lfc[:, 1, :], ALU.min, ALU.subtract).then_inc(lf_ok, 1)
            dve.wait_ge(lf_ok, 1)
            one = lfc[:, 0, :]
            dve.wait_ge(t_done[0], NQ + 1)
            nc.vector.tensor_copy(cst[:, NKEY:NKEY + NPAST], pt[0:FH, 0, :]).then_inc(t_read[0], 1)
            dve.wait_ge(t_read[0], 1)
            nc.vector.tensor_tensor_scan(cst[:, 0:NM], one[:, 0:NM], lf[:, TOUT:TALL], 0.0, ALU.mult, ALU.add).then_inc(o_read, 1)
            dve.wait_ge(o_read, 1)
            link(dve, nc.vector.tensor_tensor_scan(cst[:, NM:NKEY], one[:, 0:SEQ], lf[:, 0:SEQ], cst[:, NM - 1:NM], ALU.mult, ALU.add), ch)
            link(dve, nc.vector.tensor_tensor_scan(cst[:, NKEY:NKEY + NPAST], one[:, 0:NPAST], cst[:, NKEY:NKEY + NPAST], 0.0, ALU.mult, ALU.add), ch)
            link(dve, nc.vector.tensor_tensor_scan(cst[:, NKEY + NPAST:], one[:, 0:NS], lf[:, SEQ:TOUT], cst[:, NKEY + NPAST - 1:NKEY + NPAST], ALU.mult, ALU.add), ch)
            nc.vector.tensor_scalar(ncum[:], cst[:], -1.0, None, ALU.mult).then_inc(s_read, 1)

        def strip(s, gain=None, scale=None):
            u, n = At(U_STRIP + 2 * s.first, 2 * s.step, s.i), At(N_STRIP + NQ * s.first, NQ * s.step, s.i)
            for i in range(NQ):
                if i == 0:
                    wait(dve, stored, s.times(ST_STRIP, -ST_STRIP) if s.i is not None or s.first > 1 else 0)
                strip_read(s, n, i)
                if i in (4, 5):
                    split_lo(dve, u + (i - 2))
                if gain is None:
                    continue
                if i == 0:
                    dve.wait_ge(ssq2, s.v)
                    nc.vector.tensor_scalar(stat[:, 1, :], stat[:, 0, :], 1.0 / P, EPS, ALU.mult, ALU.add).then_inc(ssq_v, 1)
                if i == 1:
                    dve.wait_ge(a_root, (s + 3).v)
                    root_end(dve, 18, scale, ch)
                if 1 <= i <= 3:
                    for x in range(3 * i - 3, 3 * i):
                        for e in range(2):
                            r = rows[:, 1 - s.mod(2), x, e * P:e * P + P]
                            ins = nc.vector.scalar_tensor_tensor(r, r, stat[:, 5, 2 * x + e:2 * x + e + 1], gain[:], ALU.mult, ALU.mult)
                if i == 3:
                    ins.then_inc(strip_ok, 1)

        for s in range(1, 5):
            strip(At(s), gq, SCALE)
            if s == 1:
                logf_rest()
        c0 = ch[0]
        with dve.Fori(0, 2) as i:
            ch[0] = At(c0.first, 10, i)
            for s in range(2):
                strip(At(5 + s, 2, i), gk, 1.0)
            assert ch[0].first == c0.first + 10
        ch[0] = At(c0.first + 20)
        strip(At(9))
        with dve.Fori(0, 3) as i:
            for s in range(2):
                strip(At(10 + s, 2, i))

        def maxes(h, j):
            dve.wait_ge(s_done, h.times(9, j + 1))
            m, n = (P, NM + P * (j + 1)) if j < NT else (NS, NPAST + NS)
            if j == 0:
                dve.wait_ge(ld_n, h.times(16, 16))
            z, k0 = prob[0:m, j % 2, 0:n], (NKEY if j == NT else 0)
            nc.vector.tensor_tensor(z, ps[0:m, 0:n], ncr[0:m, k0:k0 + n], ALU.add).then_inc(s_read, 1)
            dve.wait_ge(s_read, h.times(9, S0 + j + 1))
            nc.vector.tensor_reduce(mx[0:m, j % 2:j % 2 + 1], z, AX.X, ALU.max, negate=True).then_inc(m_done, 1)

        def scale_probs(h, j):
            dve.wait_ge(e_done, h.times(9, E0 + j + 1))
            m, n = (P, NM + P * (j + 1)) if j < NT else (NS, NPAST + NS)
            link(dve, nc.vector.reciprocal(linv[0:m, j % 2:j % 2 + 1], lsum[0:m, j % 2:j % 2 + 1]), ch)
            nc.vector.tensor_scalar(prob[0:m, j % 2, 0:n], prob[0:m, j % 2, 0:n], linv[0:m, j % 2:j % 2 + 1], None,
                                    ALU.mult).then_inc(p_done, 1)

        def reads(h, gs):
            for g in gs:
                if GROUPS[g][2] == 0:
                    dve.wait_ge(t_done[0], h.times(PER_BANK[0], T_ATT[0] + nth(g) + 1))
                    read_group(lambda o, i_: nc.vector.tensor_copy(o, i_), g).then_inc(t_read[0], 1)

        def out_read(h, j):
            dve.wait_ge(o_done, h.times(9, j + 1))
            if j == 0:
                dve.wait_ge(stored, h.times(64, ST_TURN))
            w = NS if j == NT else P
            nc.vector.tensor_copy(fst[:, j * P:j * P + w], po[:, 0:w]).then_inc(o_read, 1)

        def turn_split(h, x):
            split_lo(dve, At(U_TURN + 3 * h.first + x, 3 * h.step, h.i))

        def turn_read(h, t):
            x, j = t // 3, t % 3
            c, w = (T3 if x == 0 else O3)[j]
            n = At(N_TURN + 9 * h.first + t, 9 * h.step, h.i)
            slot = (h.first + x) % 2
            if j == 0:
                dve.wait_ge(stored, h.times(64, ST_TURN + (-32, 0, 16)[x]))
            dve.wait_ge(mm_done, (n + 1).v)
            z = pd[:, n.mod(NB), 0:w]
            if x:
                nc.vector.tensor_copy(stage[:, slot, c:c + w], z).then_inc(bank_free, 1)
                return
            tmp = rtmp[:, n.mod(2)]
            nc.vector.tensor_tensor(tmp[:, 0, 0:w], z, cosT[:, c:c + w], ALU.mult)
            nc.vector.tensor_tensor(tmp[0:64, 1, 0:w], z[64:P], sinT[64:P, c:c + w], ALU.mult)
            nc.vector.tensor_tensor(tmp[64:P, 1, 0:w], z[0:64], sinT[0:64, c:c + w], ALU.mult).then_inc(bank_free, 1)
            dve.wait_ge(bank_free, (n + 1).v)
            ins = nc.vector.tensor_tensor(stage[:, slot, c:c + w], tmp[:, 0, 0:w], tmp[:, 1, 0:w], ALU.add)
            if j == 2:
                ins.then_inc(unit_v, 1)

        c0 = ch[0]
        with dve.Fori(0, FH // 2) as i:
            for b in range(2):
                h = At(b, 2, i)
                ch[0] = At(c0.first + 9 * b, 18, i)
                reads(h, range(3))
                turn_read(h, 0)
                reads(h, range(3, 6))
                maxes(h, 0)
                turn_read(h, 1)
                for j in range(1, 9):
                    scale_probs(h, j - 1)
                    maxes(h, j)
                    if j in (2, 5, 8):
                        turn_read(h, {2: 3, 5: 5, 8: 7}[j])
                    reads(h, step_groups(j - 1))
                    if j in (1, 3, 6):
                        turn_read(h, {1: 2, 3: 4, 6: 6}[j])
                    out_read(h, j - 1)
                    if j in (2, 4, 6):
                        turn_split(h, {2: 2, 4: 3, 6: 4}[j])
                scale_probs(h, 8)
                reads(h, step_groups(8))
                turn_read(h, 8)
                out_read(h, 8)
        ch[0] = At(c0.first + 9 * FH)
        def ret_ad(r, c):
            c0_, m = CH[c]
            dve.wait_ge(r_a, r.times(NCH, c + 1))
            if c >= 2:
                dve.wait_ge(r_b, r.times(NCH, c - 1))
            kcol = D_COL + (C_KM if c == 0 else (C_KS if c == NCH - 1 else C_KP))
            if c:
                nc.vector.tensor_tensor(sTd[0:m, c % 2, 0:m], ps[0:m, 0:m], dec[0:m, 0:m], ALU.mult)
                nc.vector.tensor_tensor(qg[:, c % 2, 0:m], rqT[:, c0_:c0_ + m], dec[:, D_GQ:D_GQ + m], ALU.mult)
            nc.vector.tensor_scalar(kd[0:m, c % 2, :], pt[0:m, 0, 0:P], dec[0:m, kcol:kcol + 1], None, ALU.mult).then_inc(r_ad, 1)

        def ret_bd(r, c):
            c0_, m = CH[c]
            dve.wait_ge(r_b, r.times(NCH, c + 1))
            U = ps[:, 1024:1024 + RV]
            if c == 0:
                nc.vector.tensor_copy(state[:], U).then_inc(r_bd, 1)
                return
            i = c - 1
            nc.vector.tensor_copy(yraw[0:m, i, :], ps[0:m, 512:512 + RV])
            link(dve, nc.vector.bn_stats(bns[0:m, i, 0:6], ps[0:m, 512:512 + RV]), ch)
            st, gcol = (s0s, C_GS) if c == NCH - 1 else (state, C_GP)
            nc.vector.scalar_tensor_tensor(st[:], st[:], dec[:, D_COL + gcol:D_COL + gcol + 1], U, ALU.mult, ALU.add)
            nc.vector.bn_aggr(bns[0:m, i, 6:8], bns[0:m, i, 0:6]).then_inc(r_bd, 1)
            dve.wait_ge(r_bd, r.times(NCH, c + 1))

        def gated(n, gate_count, slot, m, c, w, first):
            dve.wait_ge(g_ok, gate_count)
            dve.wait_ge(mm_done, (n + 1).v)
            z, gt = pd[:, n.mod(NB), 0:w], stage[:, slot, c:c + w]
            if first:
                nc.vector.tensor_tensor(m, z, gt, ALU.mult).then_inc(bank_free, 1)
                return
            nc.vector.tensor_tensor(mtmp[:, n.mod(2), 0:w], z, gt, ALU.mult).then_inc(bank_free, 1)
            dve.wait_ge(bank_free, (n + 1).v)
            nc.vector.tensor_tensor(m, m, mtmp[:, n.mod(2), 0:w], ALU.add).then_inc(m_ok, 1)

        def ret_head(r, fox):
            def read(t):
                q, (c, w) = t // 3, O3[t % 3]
                n = At(N_GB + 12 * r.first + t, 12, r.i)
                if fox:
                    m = mT[:, bass.ds(r.times(4, q - 8), 1), c:c + w].rearrange("p a n -> p (a n)")
                    gated(n, r.times(4, q - 7), q % 2, m, c, w, True)
                    return
                if t % 3 == 0:
                    dve.wait_ge(stored, r.times(64, ST_GB + 16 * (q - 1)))
                dve.wait_ge(mm_done, (n + 1).v)
                nc.vector.tensor_copy(stage[:, q % 2, c:c + w], pd[:, n.mod(NB), 0:w]).then_inc(bank_free, 1)

            def split(x):
                split_lo(dve, At(U_GB + 4 * r.first + x, 4, r.i))

            dve.wait_ge(ld_r, r.times(48, 48))
            ret_ad(r, 0)
            split(2)
            for c in range(1, NCH):
                ret_ad(r, c)
                if c == 1 and r.first == 2:
                    resplit_lo(dve, 2, m_rows, A_NORM1)
                if c in (3, 6, 9):
                    read({3: 1, 6: 3, 9: 5}[c])
                ret_bd(r, c - 1)
                if c in (1, 4, 7):
                    read({1: 0, 4: 2, 7: 4}[c])
                if c == 5:
                    split(3)
            dve.wait_ge(ld_s, r.times(48, 48))
            dve.wait_ge(yz_ok, 1)
            ret_bd(r, NCH - 1)
            read(6)
            nc.vector.tensor_scalar(stat[:, 1, 0:NQ], bns[:, :, 7], 1.0, EPS, ALU.mult, ALU.add).then_inc(r_v, 1)
            split(4)
            dve.wait_ge(a_root, r.times(1, 12))
            root_end(dve, NQ, 1.0, ch)
            read(7)
            for i in range(NQ):
                m = P if i < NT else NS
                ins = nc.vector.tensor_scalar(yraw[0:m, i, :], yraw[0:m, i, :], bns[0:m, i, 6:7], stat[0:m, 5, i:i + 1],
                                              ALU.subtract, ALU.mult)
            ins.then_inc(r_n, 1)
            read(8)
            dve.wait_ge(r_g, r.times(1, 1))
            dve.wait_ge(ld_g, 16)
            for q, (e, tiles) in enumerate(RT_GROUPS):
                dve.wait_ge(r_t, r.times(5, q + 1))
                gain = lambda ee: gnT[:, bass.ds(r.times(2, ee), 1)]
                if e is not None:
                    t0 = tiles[0][1] * P
                    ins = nc.vector.scalar_tensor_tensor(rgT[:, e, t0:t0 + 512], pt[:, q % 2, :], gain(e),
                                                         rgT[:, e, t0:t0 + 512], ALU.mult, ALU.mult)
                else:
                    for ee in range(2):
                        ins = nc.vector.scalar_tensor_tensor(rgT[:, ee, SEQ:TOUT], pt[:, q % 2, P * ee:P * ee + NS],
                                                             gain(ee), rgT[:, ee, SEQ:TOUT], ALU.mult, ALU.mult)
                ins.then_inc(r_tr, 1)
                if q == 2:
                    read(9)
            split(5)
            if r.first == 1:
                resplit_lo(dve, 0, m_rows, A_NORM1)
            if r.first == 3:
                resplit_lo(dve, 0, ret_rows, A_FOX)
            read(10)
            if r.first == 1:
                resplit_lo(dve, 1, m_rows, A_NORM1)
            if r.first == 3:
                resplit_lo(dve, 1, ret_rows, A_FOX)
            read(11)
            dve.wait_ge(r_sto, r.times(64, 32))
        for r in range(RH):
            ret_head(At(r), r >= 2)

        resplit_lo(dve, 2, ret_rows, A_FOX)
        dve.wait_ge(r_sto, 64 * RH)
        for q in range(KC):
            split_lo(dve, At(U_RET + q + 2))
            for j, (c, w) in enumerate(O3):
                gated(At(N_RET + 3 * q + j), 9 + q, q % 2, mT[:, q, c:c + w], c, w, False)
                if q == KC - 1 and j < 2:
                    resplit_lo(dve, j, m_rows, A_RET)

        def norm2_batch(b):
            dve.wait_ge(a_ssq, NQ + 3 * b + 3)
            c = slice(3 * b, 3 * b + 3)
            nc.vector.tensor_scalar(stat[:, 1, c], stat[:, 0, c], 1.0 / D, EPS, ALU.mult, ALU.add).then_inc(r_v, 1)
            dve.wait_ge(a_root, 12 + RH + b)
            root_end(dve, 3, 1.0, ch, 3 * b)

        def norm2_row(i):
            norm_row(i, hsb, hn, g2, T_NORM2)

        def norm2_split(i):
            turn_rows_dve(dve, i, A_M)

        for s in range(4):
            dve.wait_ge(x2_in[s % 2], 32 * (s // 2 + 1))
            if s == 3:
                dve.wait_ge(g2_in, 16)
            for i in range(NQ):
                n = At(N_WO + NQ * s + i)
                if s == 0 and i == 0:
                    dve.wait_ge(bank_free, N_WO)
                if s == 0 and i == 2:
                    resplit_lo(dve, 2, m_rows, A_RET)
                if s == 0 and i == NT:
                    dve.wait_ge(hz_ok, 1)
                dve.wait_ge(mm_done, (n + 1).v)
                m = P if i < NT else NS
                nc.vector.tensor_tensor(hsb[0:m, i, 256 * s:256 * s + 256], pd[0:m, n.mod(NB), 0:256],
                                        xrow[0:m, s % 2, i, :], ALU.add).then_inc(bank_free, 1)
                if i in ((1, 2) if s == 3 else (4, 5)):
                    split_lo(dve, At(U_WO + 2 * s + (2 if i in (1, 4) else 3)))
                if s == 3 and i >= 3:
                    if i in (3, 6):
                        norm2_batch(i // 3 - 1)
                    norm2_row(i - 3)
                    if i >= 4:
                        norm2_split(i - 4)
        norm2_batch(2)
        for i in range(6, NQ):
            norm2_row(i)
            norm2_split(i - 1)
        norm2_split(NQ - 1)

        def mlp_group(g, tail):
            for q in range(4):
                split_lo(dve, At(U_MLP + q + 2, 8, g))
                for j, (c, w) in enumerate(O3):
                    n = At(N_MLP + 3 * q + j, G_N, g)
                    par = (3 * q + j) % 2
                    dve.wait_ge(u_relu, At(3 * q + j + 1, 12, g).v)
                    nc.vector.scalar_tensor_tensor(usq[:, par, 0:w], pd[:, n.mod(NB), 0:w], 0.0, relu[:, par, 0:w],
                                                   ALU.max, ALU.mult).then_inc(bank_free, 1)
                    dve.wait_ge(u_hi, At(3 * q + j + 1, 12, g).v)
                    nc.vector.tensor_tensor(ul[:, q, c:c + w], usq[:, par, 0:w], uh[:, q, c:c + w], ALU.subtract).then_inc(u_lo, 1)
            def accumulate(q, m, j, step):
                c, w = O3[j]
                n = At(N_MLP + 12 + step, G_N, g) if not tail else At(N_MLP + 7 * G_N + 12 + step)
                dve.wait_ge(mm_done, (n + 1).v)
                dve.wait_ge(bank_free, n.v)
                y = yT[:, 2 * q + m, c:c + w]
                nc.vector.tensor_tensor(y, y, pd[:, n.mod(NB), 0:w], ALU.add).then_inc(bank_free, 1)

            if tail:
                for q in range(2):
                    split_lo(dve, At(U_END - 2 + q))
                for j in range(3):
                    for q in range(4):
                        for m in range(2):
                            accumulate(q, m, j, 8 * j + 2 * q + m)
                        if q:
                            for i in LAST_TURNS[j][q - 1]:
                                y_out(i)
                return
            dve.wait_ge(y_zero, 1)
            for q in range(4):
                split_lo(dve, At(U_MLP + 6 + q, 8, g))
                for m in range(2):
                    for j in range(3):
                        accumulate(q, m, j, 6 * q + 3 * m + j)

        def y_out(i):
            w = P if i < NT else NS
            dve.wait_ge(hb_in[i % 2], 16 * (i // 2 + 1))
            if i >= 2:
                dve.wait_ge(y_st[i % 2], 16 * (i // 2))
            for g in range(2):
                dve.wait_ge(t_done[g], T_FIN[g] + i + 1)
                nc.vector.tensor_tensor(yout[0:w, i % 2, 512 * g:512 * g + 512], pt[0:w, g, :],
                                        hback[0:w, i % 2, 512 * g:512 * g + 512], ALU.add).then_inc(y_rd, 1)

        with dve.Fori(0, 7) as g:
            mlp_group(g, False)
        mlp_group(7, True)
        for i in range(5, NQ):
            y_out(i)

    ctx.close()


_INS = ["x_prompt", "x_sample", "state_ret", "cache_fox_k", "cache_fox_v", "cache_fox_logf", "meta_tokens",
        "norm1_g", "w_in", "b_forget", "q_norm_g", "k_norm_g", "ret_gn_g", "w_ret_out", "w_fox_out", "w_o",
        "norm2_g", "w_ff1", "w_ff2"]
_OUTS = [(1, 1024, 1024), (1, 32, 1024), (1, 1, 4, 128, 256), (1, 1, 1040, 8, 128), (1, 1, 1040, 8, 128),
         (1, 1, 1040, 8), (1, 1, 4, 128, 256), (1, 1, 32, 8, 128), (1, 1, 32, 8, 128), (1, 1, 32, 8)]


def shape_constants():
    import numpy as np

    f = np.float32
    ident = np.eye(P, dtype=f)
    mask = np.where(np.arange(P)[None, :] > np.arange(P)[:, None], f(NEG), f(0.0)).astype(f)
    pos = np.concatenate([np.arange(SEQ), NPAST + np.arange(NS), np.arange(NM) - NM]).astype(f)
    half = P // 2
    inv = (f(10000.0) ** (-np.arange(half, dtype=f) / f(half))).astype(f)
    ang = (pos[:, None] * inv[None, :]).astype(f)
    cos, sin = np.cos(ang).astype(f).T, np.sin(ang).astype(f).T
    cosT = np.concatenate([cos, cos], 0)
    sinT = np.concatenate([sin, -sin], 0)
    decay = np.zeros((RH, P, 264), f)
    n = np.arange(P, dtype=np.float64)
    for h in range(RH):
        lg = float(np.log(1.0 - 2.0 ** (-5.0 - h)))
        diff = n[None, :] - n[:, None]
        decay[h, :, 0:P] = np.where(diff >= 0, np.exp(lg * np.maximum(diff, 0)), 0) * SCALE
        decay[h, :, P:2 * P] = np.exp(lg * (n + 1))[None, :]
        decay[h, :, 2 * P + 0] = np.exp(lg * (P - 1 - n)) * SCALE
        decay[h, :, 2 * P + 1] = np.exp(lg * (NM - 1 - np.minimum(n, NM - 1))) * SCALE
        decay[h, :, 2 * P + 2] = np.exp(lg * (NS - 1 - np.minimum(n, NS - 1))) * SCALE
        decay[h, :, 2 * P + 3] = np.exp(lg * P)
        decay[h, :, 2 * P + 4] = np.exp(lg * NS)
    return {"ident": ident, "mask": mask, "cos": np.ascontiguousarray(cosT), "sin": np.ascontiguousarray(sinT),
            "decay": decay}


def kernel(**inputs):
    import numpy as np
    import concourse.bacc as _bacc
    from concourse.bass_utils import run_bass_kernel_spmd as _run

    nc = _bacc.Bacc("TRN2", target_bir_lowering=False, num_devices=1)
    arrays, args = {}, []
    named = [(n, inputs[n]) for n in _INS] + [(f"c_{n}", a) for n, a in shape_constants().items()]
    for name, a in named:
        a = np.ascontiguousarray(a)
        arrays[f"in_{name}"] = a
        args.append(nc.dram_tensor(f"in_{name}", a.shape, mybir.dt.from_np(a.dtype), kind="ExternalInput").ap())
    for i, shape in enumerate(_OUTS):
        args.append(nc.dram_tensor(f"out_{i}", shape, F32, kind="ExternalOutput").ap())
    hybrid_step(nc, *args)
    r = _run(nc, [arrays], core_ids=[0])
    return tuple(r.results[0][f"out_{i}"] for i in range(len(_OUTS)))
```
